# Optimizing a Trainium2 kernel written in Bass

```python
import jax, jax.numpy as jnp
from jax import lax
import numpy as np

'''Hybrid decoder trunk: DEPTH post-norm (DeepNorm) layers. Each layer has ONE combined input
projection whose columns are partitioned among three parallel head groups (stick-breaking
attention, multi-scale retention, DSA indexer-sparse attention). All groups read the same
residual stream, their outputs are concatenated over head groups and passed through ONE output
projection. The channel mixer is a grouped top-2 mixture of experts whose router is shared by
all layers.
Inputs:  x (BATCH, SEQ, D_MODEL) float32 plus parameters (see setup_inputs).
Output:  (BATCH, SEQ, D_MODEL).'''

D_MODEL = 2048
BATCH = 1
SEQ = 256
DEPTH = 2

HEAD_DIM = 128
SB_HEADS = 6
RET_HEADS = 4
DSA_HEADS = 6
D_SB = SB_HEADS * HEAD_DIM
D_RET = RET_HEADS * HEAD_DIM
D_DSA = DSA_HEADS * HEAD_DIM
D_MIX = D_SB + D_RET + D_DSA
KV_RANK = 256
IDX_HEADS = 8
IDX_DIM = 64
IDX_SCALE = IDX_DIM ** -0.5 * IDX_HEADS ** -0.5
TOPK_MAX = 256
Q_BLOCK = 128
RET_CHUNK = 128
N_EXPERTS = 16
N_GROUPS = 4
EXPERTS_PER_GROUP = N_EXPERTS // N_GROUPS
TOP_K_EXPERTS = 2
D_FF_EXPERT = 512
LN_EPS = 1e-5
RMS_EPS = 1e-6
GN_EPS = 1e-6
DEEPNORM_ALPHA = (2 * DEPTH) ** 0.25
DEEPNORM_BETA = (8 * DEPTH) ** -0.25
SPLITS = (D_SB, D_SB, D_SB,
          D_RET, D_RET, D_RET, D_RET,
          D_DSA, KV_RANK, IDX_HEADS * IDX_DIM, IDX_DIM, IDX_HEADS)
D_IN = sum(SPLITS)

kernel_name = 'hybrid_sb_ret_dsa_grouped_moe_deepnorm'

def layer_norm(x, g, b):
    xf = x.astype(jnp.float32)
    mu = jnp.mean(xf, axis=-1, keepdims=True)
    var = jnp.mean(jnp.square(xf - mu), axis=-1, keepdims=True)
    return ((xf - mu) * lax.rsqrt(var + LN_EPS) * g + b).astype(x.dtype)

def rms_norm(x, g):
    xf = x.astype(jnp.float32)
    y = xf * lax.rsqrt(jnp.mean(jnp.square(xf), axis=-1, keepdims=True) + RMS_EPS) * g
    return y.astype(x.dtype)

def split_columns(p):
    outs, o = [], 0
    for n in SPLITS:
        outs.append(p[..., o:o + n])
        o += n
    return outs

def to_blocks(x):
    b, s = x.shape[:2]
    return jnp.moveaxis(x.reshape((b, s // Q_BLOCK, Q_BLOCK) + x.shape[2:]), 1, 0)

def from_blocks(y):
    y = jnp.moveaxis(y, 0, 1)
    return y.reshape((y.shape[0], y.shape[1] * y.shape[2]) + y.shape[3:])

def stick_breaking_attention(q, k, v):
    b, s, h, d = q.shape
    scale = d ** -0.5
    kf = k.astype(jnp.float32)
    vf = v.astype(jnp.float32)
    key_pos = jnp.arange(s)

    def block(args):
        qblk, i = args
        t = i * Q_BLOCK + jnp.arange(Q_BLOCK)
        strict = key_pos[None, :] < t[:, None]
        z = jnp.einsum('bqhd,bkhd->bhqk', qblk.astype(jnp.float32), kf) * scale
        log_rem = jnp.where(strict, jax.nn.log_sigmoid(-z), 0.0)
        after = lax.cumsum(log_rem, axis=3, reverse=True) - log_rem
        a = jnp.where(strict, jnp.exp(jax.nn.log_sigmoid(z) + after), 0.0)
        return jnp.einsum('bhqk,bkhd->bqhd', a, vf)

    nb = s // Q_BLOCK
    out = lax.map(block, (to_blocks(q), jnp.arange(nb)))
    return from_blocks(out).reshape(b, s, h * d).astype(q.dtype)

def rotary(x, pos):
    half = x.shape[-1] // 2
    theta = 10000.0 ** (-jnp.linspace(0.0, 1.0, half, dtype=jnp.float32))
    ang = pos[:, None] * theta[None, :]
    cos = jnp.cos(ang)[None, :, None, :]
    sin = jnp.sin(ang)[None, :, None, :]
    x1, x2 = x[..., :half], x[..., half:]
    return jnp.concatenate([x1 * cos - x2 * sin, x1 * sin + x2 * cos], axis=-1)

def retention(q, k, v, g, gn_g):
    b, s, h, d = q.shape
    pos = jnp.arange(s, dtype=jnp.float32)
    qf = rotary(q.astype(jnp.float32), pos)
    kf = rotary(k.astype(jnp.float32), pos) * d ** -0.5
    vf = v.astype(jnp.float32)
    log_gamma = jnp.log1p(-(2.0 ** (-5.0 - jnp.arange(h, dtype=jnp.float32))))
    c = RET_CHUNK
    nc = s // c
    idx = jnp.arange(c, dtype=jnp.float32)
    diff = idx[:, None] - idx[None, :]
    intra = jnp.where(diff >= 0, jnp.exp(jnp.maximum(diff, 0.0)[None] * log_gamma[:, None, None]), 0.0)
    q_decay = jnp.exp((idx[None, :] + 1.0) * log_gamma[:, None])
    k_decay = jnp.exp((c - 1.0 - idx[None, :]) * log_gamma[:, None])
    chunk_decay = jnp.exp(c * log_gamma)

    def chunks(x):
        return x.reshape(b, nc, c, h, d).transpose(1, 0, 3, 2, 4)

    def step(state, inp):
        qc, kc, vc = inp
        scores = jnp.einsum('bhid,bhjd->bhij', qc, kc) * intra[None]
        o = (jnp.einsum('bhij,bhje->bhie', scores, vc)
             + jnp.einsum('bhid,bhde->bhie', qc * q_decay[None, :, :, None], state))
        state = (chunk_decay[None, :, None, None] * state
                 + jnp.einsum('bhjd,bhje->bhde', kc * k_decay[None, :, :, None], vc))
        return state, o

    state0 = jnp.zeros((b, h, d, d), jnp.float32)
    _, outs = lax.scan(step, state0, (chunks(qf), chunks(kf), chunks(vf)))
    o = outs.transpose(1, 0, 3, 2, 4).reshape(b, s, h, d)
    mu = jnp.mean(o, axis=-1, keepdims=True)
    var = jnp.mean(jnp.square(o - mu), axis=-1, keepdims=True)
    o = ((o - mu) * lax.rsqrt(var + GN_EPS)).reshape(b, s, h * d) * gn_g
    return (jax.nn.silu(g.astype(jnp.float32)) * o).astype(q.dtype)

def dsa_attention(q, c_kv, q_idx, k_idx, w_idx, kv_norm_g, w_kv_up):
    b, s, h, d = q.shape
    topk = min(TOPK_MAX, s // 4)
    kv = jnp.einsum('bsr,rn->bsn', rms_norm(c_kv, kv_norm_g), w_kv_up).reshape(b, s, h, 2, d)
    k = kv[..., 0, :]
    v = kv[..., 1, :]
    k_idx_f = k_idx.astype(jnp.float32)
    key_pos = jnp.arange(s)
    gather = jax.vmap(lambda xx, ii: xx[ii])

    def block(args):
        qb, qib, wb, i = args
        t = i * Q_BLOCK + jnp.arange(Q_BLOCK)
        causal = key_pos[None, :] <= t[:, None]
        rel = jax.nn.relu(jnp.einsum('bqhd,bkd->bqhk', qib.astype(jnp.float32), k_idx_f))
        score = jnp.einsum('bqhk,bqh->bqk', rel, wb.astype(jnp.float32)) * IDX_SCALE
        score = jnp.where(causal[None], score, -jnp.inf)
        _, sel = lax.top_k(score, topk)
        valid = sel <= t[None, :, None]
        k_sel = gather(k, sel).astype(jnp.float32)
        v_sel = gather(v, sel).astype(jnp.float32)
        logits = jnp.einsum('bqhd,bqkhd->bhqk', qb.astype(jnp.float32), k_sel) * d ** -0.5
        logits = jnp.where(valid[:, None], logits, -jnp.inf)
        p = jax.nn.softmax(logits, axis=-1)
        return jnp.einsum('bhqk,bqkhd->bqhd', p, v_sel)

    nb = s // Q_BLOCK
    out = lax.map(block, (to_blocks(q), to_blocks(q_idx), to_blocks(w_idx), jnp.arange(nb)))
    return from_blocks(out).reshape(b, s, h * d).astype(q.dtype)

def grouped_moe(x, w_router, w_gate, w_up, w_down):
    logits = jnp.einsum('bsd,de->bse', x.astype(jnp.float32), w_router.astype(jnp.float32))
    probs = jax.nn.softmax(logits, axis=-1)
    grouped = probs.reshape(probs.shape[:2] + (N_GROUPS, EXPERTS_PER_GROUP))
    group_score = jnp.sum(lax.top_k(grouped, TOP_K_EXPERTS)[0], axis=-1)
    g_sel = jnp.argmax(group_score, axis=-1)
    in_group = jnp.take_along_axis(grouped, g_sel[..., None, None], axis=2)[..., 0, :]
    top_w, top_i = lax.top_k(in_group, TOP_K_EXPERTS)
    top_w = top_w / jnp.sum(top_w, axis=-1, keepdims=True)
    expert_ids = g_sel[..., None] * EXPERTS_PER_GROUP + top_i
    gates = jnp.sum(jax.nn.one_hot(expert_ids, N_EXPERTS, dtype=jnp.float32) * top_w[..., None], axis=-2)
    hg = jnp.einsum('bsd,edf->bsef', x, w_gate)
    hu = jnp.einsum('bsd,edf->bsef', x, w_up)
    act = jax.nn.silu(hg) * hu * gates[..., None].astype(x.dtype)
    return jnp.einsum('bsef,efd->bsd', act, w_down)

def setup_inputs(seed: int = 0) -> dict:
    key = jax.random.key(seed)
    ks = jax.random.split(key, 16)
    f32 = jnp.float32
    nrm = lambda k, shp, sc: jax.random.normal(k, shp, f32) * sc
    return {
        'x': nrm(ks[0], (BATCH, SEQ, D_MODEL), 1.0),
        'w_in': nrm(ks[1], (DEPTH, D_MODEL, D_IN), D_MODEL ** -0.5),
        'w_kv_up': nrm(ks[2], (DEPTH, KV_RANK, DSA_HEADS * 2 * HEAD_DIM), KV_RANK ** -0.5),
        'kv_norm_g': 1.0 + nrm(ks[3], (DEPTH, KV_RANK), 0.02),
        'ret_gn_g': 1.0 + nrm(ks[4], (DEPTH, D_RET), 0.02),
        'w_o': nrm(ks[5], (DEPTH, D_MIX, D_MODEL), D_MIX ** -0.5 * DEEPNORM_BETA),
        'ln1_g': 1.0 + nrm(ks[6], (DEPTH, D_MODEL), 0.02),
        'ln1_b': nrm(ks[7], (DEPTH, D_MODEL), 0.02),
        'w_router': nrm(ks[8], (D_MODEL, N_EXPERTS), D_MODEL ** -0.5),
        'w_gate': nrm(ks[9], (DEPTH, N_EXPERTS, D_MODEL, D_FF_EXPERT), D_MODEL ** -0.5),
        'w_up': nrm(ks[10], (DEPTH, N_EXPERTS, D_MODEL, D_FF_EXPERT), D_MODEL ** -0.5),
        'w_down': nrm(ks[11], (DEPTH, N_EXPERTS, D_FF_EXPERT, D_MODEL), D_FF_EXPERT ** -0.5 * DEEPNORM_BETA),
        'ln2_g': 1.0 + nrm(ks[12], (DEPTH, D_MODEL), 0.02),
        'ln2_b': nrm(ks[13], (DEPTH, D_MODEL), 0.02),
    }

def reference(x, w_in, w_kv_up, kv_norm_g, ret_gn_g, w_o, ln1_g, ln1_b, w_router,
              w_gate, w_up, w_down, ln2_g, ln2_b):
    b, s, _ = x.shape
    for l in range(DEPTH):
        proj = jnp.einsum('bsd,dn->bsn', x, w_in[l])
        (sb_q, sb_k, sb_v, r_q, r_k, r_v, r_g,
         d_q, d_ckv, d_qi, d_ki, d_w) = split_columns(proj)
        heads = lambda t, n: t.reshape(b, s, n, HEAD_DIM)
        y_sb = stick_breaking_attention(heads(sb_q, SB_HEADS), heads(sb_k, SB_HEADS), heads(sb_v, SB_HEADS))
        y_ret = retention(heads(r_q, RET_HEADS), heads(r_k, RET_HEADS), heads(r_v, RET_HEADS), r_g, ret_gn_g[l])
        y_dsa = dsa_attention(heads(d_q, DSA_HEADS), d_ckv, d_qi.reshape(b, s, IDX_HEADS, IDX_DIM),
                              d_ki, d_w, kv_norm_g[l], w_kv_up[l])
        mix = jnp.einsum('bsm,md->bsd', jnp.concatenate([y_sb, y_ret, y_dsa], axis=-1), w_o[l])
        x = layer_norm(DEEPNORM_ALPHA * x + mix, ln1_g[l], ln1_b[l])
        ffn = grouped_moe(x, w_router, w_gate[l], w_up[l], w_down[l])
        x = layer_norm(DEEPNORM_ALPHA * x + ffn, ln2_g[l], ln2_b[l])
    return x


_drawn_inputs = setup_inputs


def setup_inputs(seed=0):
    import zlib

    import numpy as np

    out = dict(_drawn_inputs(seed))
    spreads = {}
    factors = {'kv_norm_g': 3.618}
    for name, (base, spread) in spreads.items():
        noise = np.random.default_rng([zlib.crc32(name.encode()), seed]).standard_normal(out[name].shape)
        drawn = base * np.exp(spread * noise) if base else spread * noise
        out[name] = __import__('jax').numpy.asarray(drawn.astype(out[name].dtype))
    for name, factor in factors.items():
        out[name] = (out[name] * factor).astype(out[name].dtype)
    return out
```

```python
from contextlib import ExitStack

import concourse.bass as bass
from concourse import mybir

F32 = mybir.dt.float32
ALU = mybir.AluOpType
ACT = mybir.ActivationFunctionType
AX_X = mybir.AxisListType.X

P = 128
D_MODEL, SEQ, DEPTH = 2048, 256, 2
TILES = SEQ // P
HEAD_DIM = 128
SB_HEADS, RET_HEADS, DSA_HEADS = 6, 4, 6
KV_RANK, IDX_HEADS, IDX_DIM = 256, 8, 64
TOPK = min(256, SEQ // 4)
N_EXPERTS, N_GROUPS, D_FF = 16, 4, 512
PER_GROUP = N_EXPERTS // N_GROUPS
LN_EPS, RMS_EPS, GN_EPS = 1e-5, 1e-6, 1e-6
ALPHA = (2 * DEPTH) ** 0.25
SCALE = HEAD_DIM ** -0.5
IDX_SCALE = IDX_DIM ** -0.5 * IDX_HEADS ** -0.5
NEG = -1.0e30
TAKEN = -3.0e38

C_SBQ = 0
C_SBK = C_SBQ + SB_HEADS * HEAD_DIM
C_SBV = C_SBK + SB_HEADS * HEAD_DIM
C_RQ = C_SBV + SB_HEADS * HEAD_DIM
C_RK = C_RQ + RET_HEADS * HEAD_DIM
C_RV = C_RK + RET_HEADS * HEAD_DIM
C_RG = C_RV + RET_HEADS * HEAD_DIM
C_DQ = C_RG + RET_HEADS * HEAD_DIM
C_CKV = C_DQ + DSA_HEADS * HEAD_DIM
C_QI = C_CKV + KV_RANK
C_KI = C_QI + IDX_HEADS * IDX_DIM
C_W = C_KI + IDX_DIM
D_IN = C_W + IDX_HEADS

KT = D_MODEL // P
NW = 512
KU = 4
CHUNK_UNITS = KT // KU
RING = 8
CHUNKS = [10, 11, 9, 8, 0, 1, 2, 5, 6, 4, 7, 3]
WO_CHUNKS = D_MODEL // NW
IN_UNITS = len(CHUNKS) * CHUNK_UNITS
WO_UNITS = WO_CHUNKS * CHUNK_UNITS
EXPERT_UNITS = 3 * CHUNK_UNITS
EXPERTS_IN_BODY = 2
LAYER_UNITS = IN_UNITS + WO_UNITS + N_EXPERTS * EXPERT_UNITS
LAYER_TURNS = LAYER_UNITS // RING

TRI = 3 * P

T_ID = 0
T_SUM = T_ID + P
T_NONE = T_SUM + P
T_STRICT = T_NONE + P
T_NSTRICT = T_STRICT + P
T_CAUSAL = T_NSTRICT + P
T_DECAY = T_CAUSAL + P
T_COS = T_DECAY + RET_HEADS * TRI
T_SIN = T_COS + TILES * HEAD_DIM
T_RANK = T_SIN + TILES * HEAD_DIM
T_COLS = T_RANK + N_EXPERTS


def width(n):
    return min(NW, D_IN - n * NW)


def plan():
    idx = [[("qiT", 0), ("qiT", 1)], [("ckvT", 0), ("kiT", 0)]]
    idx += [[("idx", h), ("idx", h + 1)] for h in range(0, IDX_HEADS, 2)]
    idx[-1].append(("topk", 0))
    dsa = []
    for i in range(DSA_HEADS + 1):
        a, b = [], []
        if i < DSA_HEADS:
            a += [("kv", i), ("dqT", i)]
            b += [("log", i)]
        if i >= 1:
            a += [("pT", i - 1)]
            b += [("out", i - 1)]
        dsa += [a, b[::-1]]
    sb = []
    for i in range(SB_HEADS + 2):
        a = []
        if i < SB_HEADS:
            a.append(("sbT", i))
        if 1 <= i <= SB_HEADS:
            a.append(("z", i - 1))
        if i >= 2:
            a.append(("arg", i - 2))
        sb.append(a)
    ret = []
    for i in range(RET_HEADS + 1):
        a = []
        if i < RET_HEADS:
            a.append(("rT", i))
        if i >= 1:
            a += [("rs", i - 1)]
        ret.append(a)
    streams = [
        [(2, [("ckvn", 0)])] + [(2, s) for s in idx] + [(4, s) for s in dsa],
        [(7, s) for s in sb] + [(10, [("sbo", 4), ("sbo", 5)])],
        [(10, [("rot", 0)])] + [(10, s) for s in ret] + [(11, [("ro", h), ("ro", h + 1)]) for h in (0, 2)]
        + [(11, [("gn", 0)])],
    ]
    steps = []
    for u in range(IN_UNITS):
        steps.append(("proj", u))
        have = u // CHUNK_UNITS
        for s in streams:
            if s and s[0][0] <= have:
                steps += s.pop(0)[1]
    for s in streams:
        for need, more in s:
            steps += more
    steps += [("sbo", h) for h in range(4)] + [("ryT", 0), ("ryT", 1)]
    return steps


STEPS = plan()
DRAIN = {"qiT": "act", "ckvT": "dve", "kiT": "act", "idx": "act", "kv": "act", "dqT": "dve", "log": "dve",
         "pT": "act", "out": "dve", "sbT": "act", "z": "dve", "arg": "act", "sbo": "dve", "rT": "dve",
         "rs": "dve", "ro": "dve", "ryT": "dve"}
FILLS = [s for s in STEPS if s[0] in DRAIN]
FILL_AT = {s: n for n, s in enumerate(FILLS)}
BANKS = 4


def reads(kind, h):
    return {"idx": [("qiT", h // 4), ("kiT", 0)], "kv": [("ckvT", 0)], "log": [("kv", h), ("dqT", h)],
            "out": [("pT", h)], "z": [("sbT", h)], "arg": [("sbT", h)], "rs": [("rT", h)],
            "sbo": [("arg", h)], "ro": [("rs", h)]}.get(kind, [])


DRAINS = {e: sum(DRAIN[s[0]] == e for s in FILLS) for e in ("act", "dve")}
DRAIN_AT = {s: sum(DRAIN[r[0]] == DRAIN[s[0]] for r in FILLS[:n + 1]) for n, s in enumerate(FILLS)}

ACT_LINKS = 16
DVE_LINKS = 156
POOL_LINKS = 7
XT_FILLS = TILES * KT // 4
NORMS = 4
(N_CKV, N_RET, N_LN1, N_LN2) = range(NORMS)


def trunk(nc, x, w_in, w_kv_up, kv_norm_g, ret_gn_g, w_o, ln1_g, ln1_b, w_router,
          w_gate, w_up, w_down, ln2_g, ln2_b, tables, out):
    with ExitStack() as ctx:
        def sb(name, *shape):
            return ctx.enter_context(nc.sbuf_tensor(name, [P, *shape], F32))

        def sem(name):
            return ctx.enter_context(nc.semaphore(name))

        ring = sb("ring", RING, KU, NW)
        xs = sb("xs", TILES, D_MODEL)
        xT = sb("xT", KT, SEQ)
        proj = sb("proj", TILES * D_IN)
        kvup = sb("kvup", KV_RANK // P, DSA_HEADS * 2 * HEAD_DIM)
        yT = sb("yT", KT, SEQ)
        tab = sb("tab", T_COLS)
        wr = sb("wr", KT, N_EXPERTS)
        gn_col = sb("gn_col", RET_HEADS)
        kvg_col = sb("kvg_col", KV_RANK // P)
        dkv = sb("dkv", 2, 4 * P)
        dp = sb("dp", 2, TRI)
        sba = sb("sba", SB_HEADS, TRI)
        ra = sb("ra", RET_HEADS, TRI)
        sel = sb("sel", TRI)
        st = sb("st", TILES, 4, 6)
        mv = sb("mv", TILES * RET_HEADS, 2)
        var = sb("var", TILES * RET_HEADS)
        rstd = sb("rstd", TILES * RET_HEADS)
        nt = sb("nt", TILES * RET_HEADS)
        top8 = sb("top8", 8)
        nmax = sb("nmax", 2, TILES)
        psums = sb("psums", 2, TILES)
        gates = sb("gates", TILES, N_EXPERTS)

        pr = proj[:, :].rearrange("p (t n) -> p t n", t=TILES)
        ro = pr[:, :, C_RQ:C_RQ + RET_HEADS * P]
        score = yT[:, 0:2, :].rearrange("p k s -> p (k s)")[:, 0:TRI]
        work = yT[:, 2:4, :].rearrange("p k s -> p (k s)")[:, 0:TRI]
        rel = [yT[:, k:k + 2, :].rearrange("p k s -> p (k s)")[:, 0:TRI] for k in (4, 14)]
        rot = [yT[:, k:k + 2, :].rearrange("p k s -> p (k s)") for k in (6, 8)]
        sig_g = yT[:, 6:10, :].rearrange("p (t k) s -> p t (k s)", t=TILES)
        ln_g, ln_b = proj[:, 0:D_MODEL], proj[:, D_MODEL:2 * D_MODEL]
        sg = [proj[:, (4 + t) * D_MODEL // 2:(4 + t) * D_MODEL // 2 + D_FF] for t in range(TILES)]
        hT = [proj[:, (6 + t) * D_MODEL // 2:(6 + t) * D_MODEL // 2 + D_FF] for t in range(TILES)]
        rt = proj[:, 4 * D_MODEL:4 * D_MODEL + 8 * TILES * N_EXPERTS].rearrange(
            "p (i t e) -> p i t e", i=8, t=TILES)

        pp = [ctx.enter_context(nc.psum_tensor(f"pp{i}", [P, NW], F32)) for i in range(4)]
        pb = [ctx.enter_context(nc.psum_tensor(f"pb{i}", [P, NW], F32)) for i in range(BANKS)]

        consts_in = sem("consts_in")
        x_in = sem("x_in")
        layer_in = sem("layer_in")
        lnp_in = sem("lnp_in")
        unit_in = [sem(f"unit_in{i}") for i in range(RING)]
        slots_free = sem("slots_free")
        xt_filled = sem("xt_filled")
        xt_copied = sem("xt_copied")
        chunk_out = sem("chunk_out")
        filled = sem("filled")
        act_drained = sem("act_drained")
        dve_drained = sem("dve_drained")
        ckvn_ready = sem("ckvn_ready")
        rel_ready = sem("rel_ready")
        rel_used = sem("rel_used")
        ln_ready = sem("ln_ready")
        sp_ready = sem("sp_ready")
        max_ready = sem("max_ready")
        exp_ready = sem("exp_ready")
        p_ready = sem("p_ready")
        rot_ready = sem("rot_ready")
        gexp_ready = sem("gexp_ready")
        gn_ready = sem("gn_ready")
        var_ready = sem("var_ready")
        root_ready = sem("root_ready")
        mix_added = sem("mix_added")
        x_ready = sem("x_ready")
        route_filled = sem("route_filled")
        rexp_ready = sem("rexp_ready")
        rmax_ready = sem("rmax_ready")
        gexp2 = sem("gate_exp")
        h_ready = sem("h_ready")
        hT_filled = sem("hT_filled")
        hT_ready = sem("hT_ready")
        down_filled = sem("down_filled")
        down_added = sem("down_added")
        out_done = sem("out_done")
        act_link = sem("act_link")
        dve_link = sem("dve_link")
        moe_link = sem("moe_link")
        waited = sem("waited")
        pool_link = sem("pool_link")

        ident = tab[:, T_ID:T_ID + P]

        def freed(l, unit):
            return l * LAYER_UNITS + (RING + unit + 1)

        def wait_drained(eng, l, *steps):
            for which, semaphore in (("act", act_drained), ("dve", dve_drained)):
                at = [DRAIN_AT[s] for s in steps if DRAIN[s[0]] == which]
                if at:
                    eng.wait_ge(semaphore, l * DRAINS[which] + max(at))

        def wait_filled(eng, l, step):
            eng.wait_ge(filled, l * len(FILLS) + FILL_AT[step] + 1)

        def bank(step):
            return pb[FILL_AT[step] % BANKS]

        def wait_apart(eng, semaphore, value):
            eng.wait_ge(semaphore, value)
            eng.sem_inc(waited, 1)

        def col(c, t, n=P):
            return pr[:, t, c:c + n]

        def kvn(r):
            return cols(C_CKV + r * P)

        def cols(c):
            return pr[:, :, c:c + P]

        block = ctx.enter_context(nc.Block())

        @block.sync
        def _(sp):
            with sp.Fori(0, DEPTH) as l:
                g = 0

                def unit(src, dst, base, g):
                    if g % RING == 0:
                        wait_apart(sp, slots_free, base + g + 1)
                    else:
                        sp.wait_ge(slots_free, base + g + 1)
                    sp.dma_start(dst, src).then_inc(unit_in[g % RING], 16)

                for n in CHUNKS:
                    for q in range(CHUNK_UNITS):
                        src = w_in[bass.ds(l, 1), q * KU * P:(q + 1) * KU * P, n * NW:n * NW + width(n)]
                        unit(src.rearrange("a (k p) n -> p (a k) n", p=P), ring[:, g % RING, :, 0:width(n)],
                             l * LAYER_UNITS, g)
                        g += 1
                for n in range(WO_CHUNKS):
                    for q in range(CHUNK_UNITS):
                        src = w_o[bass.ds(l, 1), q * KU * P:(q + 1) * KU * P, n * NW:(n + 1) * NW]
                        unit(src.rearrange("a (k p) n -> p (a k) n", p=P), ring[:, g % RING, :, :],
                             l * LAYER_UNITS, g)
                        g += 1
                first = g
                with sp.Fori(0, N_EXPERTS // EXPERTS_IN_BODY) as pair:
                    u = 0
                    for j in range(EXPERTS_IN_BODY):
                        e = pair * EXPERTS_IN_BODY + j
                        base = l * LAYER_UNITS + pair * (EXPERTS_IN_BODY * EXPERT_UNITS) + first
                        for w in (w_gate, w_up):
                            for q in range(CHUNK_UNITS):
                                src = w[bass.ds(l * N_EXPERTS + e, 1), q * KU * P:(q + 1) * KU * P, :]
                                unit(src.rearrange("a (k p) n -> p (a k) n", p=P), ring[:, u % RING, :, :], base, u)
                                u += 1
                        for q in range(CHUNK_UNITS):
                            src = w_down[bass.ds(l * N_EXPERTS + e, 1), q * P:(q + 1) * P, :]
                            unit(src.rearrange("a p n -> p (a n)"),
                                 ring[:, u % RING, :, :].rearrange("p k n -> p (k n)"), base, u)
                            u += 1
            sp.wait_ge(x_ready, 4 * DEPTH + 1)
            sp.dma_start(out.rearrange("a (t p) d -> p (a t) d", p=P), xs[:, :, :]).then_inc(out_done, 16)
            sp.wait_ge(out_done, 16)

        @block.gpsimd
        def _(pool):
            links = [0]
            pool.wait_ge(consts_in, 32)
            with pool.Fori(0, DEPTH) as l:
                def link(ins):
                    links[0] += 1
                    ins.then_inc(pool_link, 1)
                    pool.wait_ge(pool_link, l * POOL_LINKS + links[0])

                pool.wait_ge(chunk_out, l * len(CHUNKS) + 10)
                n = 0
                for c in (C_RQ, C_RK):
                    for t in range(TILES):
                        v = pr[:, t, c:c + RET_HEADS * P].rearrange("p (h d) -> p h d", h=RET_HEADS)
                        a = rot[0].rearrange("p (h d) -> p h d", h=RET_HEADS)
                        b = rot[1].rearrange("p (h d) -> p h d", h=RET_HEADS)
                        half = HEAD_DIM // 2

                        def table(first, n):
                            return tab[:, first:first + n].unsqueeze(1).broadcast_to([P, RET_HEADS, n])

                        pool.tensor_tensor(a, v, table(T_COS + t * P, P), ALU.mult)
                        pool.tensor_tensor(b[:, :, 0:half], v[:, :, half:P], table(T_SIN + t * P, half), ALU.mult)
                        link(pool.tensor_tensor(b[:, :, half:P], v[:, :, 0:half],
                                                table(T_SIN + t * P + half, half), ALU.mult))
                        last = pool.tensor_tensor(v, a, b, ALU.add)
                        n += 1
                        if n < 2 * TILES:
                            link(last)
                        else:
                            last.then_inc(rot_ready, 1)
            assert links[0] == POOL_LINKS, links

        @block.scalar
        def _(act):
            act.dma_start(tab[:, :], tables).then_inc(consts_in, 16)
            act.dma_start(wr[:, :, :], w_router.rearrange("(k p) e -> p k e", p=P)).then_inc(consts_in, 16)
            act.dma_start(xs[:, :, :], x.rearrange("a (t p) d -> p (a t) d", p=P)).then_inc(x_in, 16)
            act.sem_inc(hT_ready, 1)
            links = [0]
            with act.Fori(0, DEPTH) as l:
                def link(ins):
                    links[0] += 1
                    ins.then_inc(act_link, 1)
                    act.wait_ge(act_link, l * ACT_LINKS + links[0])

                def root(which, n):
                    act.wait_ge(var_ready, l * NORMS + which + 1)
                    link(act.activation(rstd[:, 0:n], var[:, 0:n], ACT.Ln))
                    act.activation(rstd[:, 0:n], rstd[:, 0:n], ACT.Exp, scale=-0.5).then_inc(root_ready, 1)

                def copy_xT(i):
                    for f in range(XT_FILLS):
                        t, k = f // (KT // 4), f % (KT // 4) * 4
                        act.wait_ge(xt_filled, l * (2 * XT_FILLS) + (i * XT_FILLS + f + 1))
                        act.activation(xT[:, k:k + 4, t * P:(t + 1) * P],
                                       pb[f % BANKS][:, :].rearrange("p (k s) -> p k s", k=4),
                                       ACT.Copy).then_inc(xt_copied, 1)

                act.wait_ge(xt_filled, l * (2 * XT_FILLS) + 1)
                act.dma_start(kvup[:, :, :],
                              w_kv_up[bass.ds(l, 1)].rearrange("a (r p) n -> p (a r) n", p=P)).then_inc(layer_in, 16)
                act.dma_start(kvg_col[:, :],
                              kv_norm_g[bass.ds(l, 1)].rearrange("a p r -> (a p) r")).then_inc(layer_in, 16)
                act.dma_start(gn_col[:, :],
                              ret_gn_g[bass.ds(l, 1)].rearrange("a p h -> (a p) h")).then_inc(layer_in, 16)
                copy_xT(0)

                for kind, h in STEPS:
                    step = (kind, h)
                    if kind == "proj" and h % CHUNK_UNITS == CHUNK_UNITS - 1:
                        c = h // CHUNK_UNITS
                        n = CHUNKS[c]
                        act.wait_ge(slots_free, freed(l, h))
                        act.activation(pr[:, 0, n * NW:n * NW + width(n)], pp[2 * (c % 2)][:, 0:width(n)], ACT.Copy)
                        act.activation(pr[:, 1, n * NW:n * NW + width(n)], pp[2 * (c % 2) + 1][:, 0:width(n)],
                                       ACT.Copy).then_inc(chunk_out, 1)
                    elif kind == "ckvn":
                        root(N_CKV, TILES)
                    elif kind == "qiT":
                        wait_filled(act, l, step)
                        for j in range(2):
                            last = act.activation(cols(C_QI + (2 * h + j) * P),
                                                  bank(step)[:, j * SEQ:(j + 1) * SEQ].rearrange("p (t s) -> p t s", t=2),
                                                  ACT.Copy)
                        last.then_inc(act_drained, 1)
                    elif kind == "kiT":
                        wait_filled(act, l, step)
                        act.activation(dkv[:, 1, 0:SEQ], bank(step)[:, 0:SEQ], ACT.Copy).then_inc(act_drained, 1)
                    elif kind == "idx":
                        wait_filled(act, l, step)
                        if h >= 2:
                            act.wait_ge(rel_used, l * IDX_HEADS + h - 1)
                        act.activation(rel[h % 2], bank(step)[:, 0:TRI], ACT.Relu).then_inc(act_drained, 1)
                    elif kind == "kv":
                        wait_filled(act, l, step)
                        act.activation(dkv[:, h % 2, :], bank(step)[:, :], ACT.Copy).then_inc(act_drained, 1)
                    elif kind == "log":
                        act.wait_ge(max_ready, l * DSA_HEADS + h + 1)
                        for t, (a, b) in enumerate(((0, P), (P, TRI))):
                            last = act.activation(dp[:, h % 2, a:b], dp[:, h % 2, a:b], ACT.Exp,
                                                  bias=nmax[:, h % 2, t:t + 1], accum_out=psums[:, h % 2, t:t + 1])
                            last.then_inc(exp_ready, 1)
                    elif kind == "pT":
                        wait_filled(act, l, step)
                        act.activation(dp[:, h % 2, :], bank(step)[:, 0:TRI], ACT.Copy).then_inc(act_drained, 1)
                    elif kind == "sbT":
                        wait_filled(act, l, step)
                        b = bank(step)[:, :].rearrange("p (j t s) -> p j t s", j=2, t=2)
                        act.activation(cols(C_SBQ + h * P), b[:, 0], ACT.Copy, scale=SCALE)
                        act.activation(cols(C_SBK + h * P), b[:, 1], ACT.Copy).then_inc(act_drained, 1)
                    elif kind == "z":
                        wait_filled(act, l, step)
                        link(act.activation(sba[:, h, :], bank(step)[:, 0:TRI], ACT.Abs))
                        link(act.activation(sba[:, h, :], sba[:, h, :], ACT.Exp, scale=-1.0))
                        act.activation(sba[:, h, :], sba[:, h, :], ACT.Ln, bias=1.0).then_inc(ln_ready, 1)
                    elif kind == "arg":
                        wait_filled(act, l, step)
                        act.activation(sba[:, h, :], bank(step)[:, 0:TRI], ACT.Exp).then_inc(act_drained, 1)
                    elif kind == "gn":
                        act.wait_ge(chunk_out, l * len(CHUNKS) + 11)
                        act.wait_ge(rot_ready, l + 1)
                        act.activation(sig_g, pr[:, :, C_RG:C_RG + RET_HEADS * P], ACT.Exp,
                                       scale=-1.0).then_inc(gexp_ready, 1)
                        root(N_RET, TILES * RET_HEADS)

                act.wait_ge(dve_drained, (l + 1) * DRAINS["dve"])
                act.wait_ge(filled, (l + 1) * len(FILLS))
                act.dma_start(ln_g, ln1_g[bass.ds(l, 1)].broadcast_to([P, D_MODEL])).then_inc(lnp_in, 16)
                act.dma_start(ln_b, ln1_b[bass.ds(l, 1)].broadcast_to([P, D_MODEL])).then_inc(lnp_in, 16)
                root(N_LN1, TILES)
                copy_xT(1)
                act.dma_start(ln_g, ln2_g[bass.ds(l, 1)].broadcast_to([P, D_MODEL])).then_inc(lnp_in, 16)
                act.dma_start(ln_b, ln2_b[bass.ds(l, 1)].broadcast_to([P, D_MODEL])).then_inc(lnp_in, 16)
                act.wait_ge(rmax_ready, l + 1)
                act.activation(rt[:, 1], rt[:, 0], ACT.Exp).then_inc(rexp_ready, 1)

                with act.Fori(0, N_EXPERTS // EXPERTS_IN_BODY) as pair:
                    for j in range(EXPERTS_IN_BODY):
                        n = l * N_EXPERTS + pair * EXPERTS_IN_BODY + j
                        act.wait_ge(slots_free, l * LAYER_UNITS + pair * (EXPERTS_IN_BODY * EXPERT_UNITS)
                                    + (RING + IN_UNITS + WO_UNITS + j * EXPERT_UNITS + 2 * CHUNK_UNITS))
                        for t in range(TILES):
                            act.wait_ge(hT_filled, n * TILES + 1)
                            act.activation(sg[t], pp[t][:, :], ACT.Exp, scale=-1.0).then_inc(gexp2, 1)
                        for t in range(TILES):
                            act.wait_ge(hT_filled, n * TILES + t + 2)
                            act.activation(hT[t], pb[0][:, :], ACT.Copy).then_inc(hT_ready, 1)
                root(N_LN2, TILES)
            assert links[0] == ACT_LINKS, links

        @block.tensor
        def _(pe):
            pe.sem_inc(slots_free, RING)
            pe.sem_inc(hT_filled, 1)
            pe.wait_ge(consts_in, 32)
            pe.wait_ge(x_in, 16)
            mm = pe.matmul
            with pe.Fori(0, DEPTH) as l:
                def transpose_x(i):
                    for f in range(XT_FILLS):
                        t, k = f // (KT // 4), f % (KT // 4) * 4
                        if f >= BANKS:
                            pe.wait_ge(xt_copied, l * (2 * XT_FILLS) + (i * XT_FILLS + f - BANKS + 1))
                        for j in range(4):
                            last = pe.transpose(pb[f % BANKS][:, j * P:(j + 1) * P],
                                                xs[:, t, (k + j) * P:(k + j + 1) * P], ident)
                        last.then_inc(xt_filled, 1)

                def rows(src, w, banks, first_unit, n_units):
                    for q in range(n_units):
                        slot = (first_unit + q) % RING
                        pe.wait_ge(unit_in[slot], l * (16 * LAYER_TURNS) + 16 * ((first_unit + q) // RING + 1))
                        for t in range(TILES):
                            for kk in range(KU):
                                k = q * KU + kk
                                last = mm(banks[t][:, 0:w], src[:, k, t * P:(t + 1) * P], ring[:, slot, kk, 0:w],
                                          start=(k == 0), stop=(k == KT - 1))
                        last.then_inc(slots_free, 1)

                pe.wait_ge(x_ready, l * 4 + 1)
                transpose_x(0)
                pe.wait_ge(xt_copied, l * (2 * XT_FILLS) + XT_FILLS)

                for kind, h in STEPS:
                    step = (kind, h)
                    if kind in DRAIN:
                        f = FILL_AT[step]
                        wait_drained(pe, l, *FILLS[max(f - BANKS, 0):max(f - BANKS + 1, 0)], *reads(kind, h))
                        b = bank(step)
                    if kind == "proj":
                        c, q = h // CHUNK_UNITS, h % CHUNK_UNITS
                        w = width(CHUNKS[c])
                        if q == 0 and c >= 2:
                            pe.wait_ge(chunk_out, l * len(CHUNKS) + c - 1)
                        slot = h % RING
                        pe.wait_ge(unit_in[slot], l * (16 * LAYER_TURNS) + 16 * (h // RING + 1))
                        for t in range(TILES):
                            for kk in range(KU):
                                k = q * KU + kk
                                last = mm(pp[2 * (c % 2) + t][:, 0:w], xT[:, k, t * P:(t + 1) * P],
                                          ring[:, slot, kk, 0:w], start=(k == 0), stop=(k == KT - 1))
                        last.then_inc(slots_free, 1)
                    elif kind == "qiT":
                        pe.wait_ge(chunk_out, l * len(CHUNKS) + 2)
                        for j in range(4):
                            last = pe.transpose(b[:, j * P:(j + 1) * P], col(C_QI + (2 * h + j // 2) * P, j % 2), ident)
                        last.then_inc(filled, 1)
                    elif kind == "ckvT":
                        pe.wait_ge(ckvn_ready, l + 1)
                        for j in range(4):
                            last = pe.transpose(b[:, j * P:(j + 1) * P], col(C_CKV + (j // 2) * P, j % 2), ident)
                        last.then_inc(filled, 1)
                    elif kind == "kiT":
                        for t in range(TILES):
                            last = pe.transpose(b[:, t * P:(t + 1) * P], dkv[:, 0, t * P:(t + 1) * P], ident)
                        last.then_inc(filled, 1)
                    elif kind == "idx":
                        r = slice(IDX_DIM * (h % 2), IDX_DIM * (h % 2) + IDX_DIM)
                        c = C_QI + (h // 2) * P
                        mm(b[:, 0:P], pr[r, 0, c:c + P], dkv[r, 1, 0:P], start=True, stop=True)
                        mm(b[:, P:TRI], pr[r, 1, c:c + P], dkv[r, 1, 0:SEQ], start=True, stop=True).then_inc(filled, 1)
                    elif kind == "kv":
                        pe.wait_ge(layer_in, l * 48 + 48)
                        c = h * 2 * P
                        for r in range(2):
                            mm(b[:, 0:SEQ], kvup[:, r, c:c + P], kvn(r), start=(r == 0), stop=(r == 1))
                        for t in range(TILES):
                            for r in range(2):
                                last = mm(b[:, (2 + t) * P:(3 + t) * P], kvn(r)[:, t, :], kvup[:, r, c + P:c + 2 * P],
                                          start=(r == 0), stop=(r == 1))
                        last.then_inc(filled, 1)
                    elif kind == "dqT":
                        pe.wait_ge(chunk_out, l * len(CHUNKS) + 4)
                        for t in range(TILES):
                            last = pe.transpose(b[:, t * P:(t + 1) * P], col(C_DQ + h * P, t), ident)
                        last.then_inc(filled, 1)
                    elif kind == "log":
                        q = cols(C_DQ + h * P)
                        mm(b[:, 0:P], q[:, 0, :], dkv[:, h % 2, 0:P], start=True, stop=True)
                        mm(b[:, P:TRI], q[:, 1, :], dkv[:, h % 2, 0:SEQ], start=True, stop=True).then_inc(filled, 1)
                    elif kind == "pT":
                        pe.wait_ge(p_ready, l * DSA_HEADS + h + 1)
                        for j in range(3):
                            last = pe.transpose(b[:, j * P:(j + 1) * P], dp[:, h % 2, j * P:(j + 1) * P], ident)
                        last.then_inc(filled, 1)
                    elif kind == "out":
                        mm(b[:, 0:P], dkv[:, h % 2, 2 * P:3 * P], dp[:, h % 2, 0:P], start=True, stop=True)
                        mm(b[:, P:SEQ], dkv[:, h % 2, 2 * P:3 * P], dp[:, h % 2, P:SEQ], start=True, stop=False)
                        mm(b[:, P:SEQ], dkv[:, h % 2, 3 * P:4 * P], dp[:, h % 2, SEQ:TRI],
                           start=False, stop=True).then_inc(filled, 1)
                    elif kind in ("sbT", "rT"):
                        if kind == "sbT":
                            pe.wait_ge(chunk_out, l * len(CHUNKS) + 7)
                            cq, ck = C_SBQ + h * P, C_SBK + h * P
                        else:
                            pe.wait_ge(rot_ready, l + 1)
                            cq, ck = C_RQ + h * P, C_RK + h * P
                        for j in range(4):
                            last = pe.transpose(b[:, j * P:(j + 1) * P], col((cq, ck)[j // 2], j % 2), ident)
                        last.then_inc(filled, 1)
                    elif kind in ("z", "arg", "rs"):
                        cq, ck = (C_RQ + h * P, C_RK + h * P) if kind == "rs" else (C_SBQ + h * P, C_SBK + h * P)
                        if kind == "arg":
                            pe.wait_ge(sp_ready, l * SB_HEADS + h + 1)
                        for at, j, i in ((0, 0, 0), (P, 0, 1), (SEQ, 1, 1)):
                            o = b[:, at:at + P]
                            last = mm(o, cols(ck)[:, j, :], cols(cq)[:, i, :], start=True, stop=(kind != "arg"))
                            if kind == "arg":
                                mm(o, tab[:, T_SUM:T_SUM + P], sba[:, h, at:at + P], start=False, stop=False)
                                if i == j:
                                    last = mm(o, ident, tab[:, T_NSTRICT:T_NSTRICT + P], start=False, stop=True)
                                else:
                                    last = mm(o, tab[:, T_NONE:T_NONE + P], sba[:, h, SEQ:TRI], start=False, stop=True)
                        last.then_inc(filled, 1)
                    elif kind == "sbo":
                        pe.wait_ge(chunk_out, l * len(CHUNKS) + (12 if h < 4 else 10))
                        mm(b[:, 0:P], col(C_SBV + h * P, 0), sba[:, h, 0:P], start=True, stop=True)
                        mm(b[:, P:SEQ], col(C_SBV + h * P, 0), sba[:, h, P:SEQ], start=True, stop=False)
                        mm(b[:, P:SEQ], col(C_SBV + h * P, 1), sba[:, h, SEQ:TRI], start=False,
                           stop=True).then_inc(filled, 1)
                    elif kind == "ro":
                        pe.wait_ge(chunk_out, l * len(CHUNKS) + 11)
                        a = ra[:, h, :]
                        mm(b[:, 0:P], a[:, 0:P], col(C_RV + h * P, 0), start=True, stop=True)
                        mm(b[:, P:SEQ], a[:, P:SEQ], col(C_RV + h * P, 0), start=True, stop=False)
                        mm(b[:, P:SEQ], a[:, SEQ:TRI], col(C_RV + h * P, 1), start=False,
                           stop=True).then_inc(filled, 1)
                    elif kind == "ryT":
                        pe.wait_ge(gn_ready, l + 1)
                        for j in range(4):
                            last = pe.transpose(b[:, j * P:(j + 1) * P],
                                                ro[:, j % 2, (2 * h + j // 2) * P:(2 * h + j // 2 + 1) * P], ident)
                        last.then_inc(filled, 1)

                pe.wait_ge(dve_drained, (l + 1) * DRAINS["dve"])
                for n in range(WO_CHUNKS):
                    if n >= 2:
                        pe.wait_ge(mix_added, l * WO_CHUNKS + n - 1)
                    rows(yT, NW, [pp[2 * (n % 2)], pp[2 * (n % 2) + 1]], IN_UNITS + n * CHUNK_UNITS, CHUNK_UNITS)
                pe.wait_ge(x_ready, l * 4 + 3)
                transpose_x(1)
                pe.wait_ge(xt_copied, (l + 1) * (2 * XT_FILLS))
                for t in range(TILES):
                    for k in range(KT):
                        last = mm(pb[1][:, t * N_EXPERTS:(t + 1) * N_EXPERTS], xT[:, k, t * P:(t + 1) * P], wr[:, k, :],
                                  start=(k == 0), stop=(k == KT - 1))
                last.then_inc(route_filled, 1)

                wait_apart(pe, rmax_ready, l + 1)
                with pe.Fori(0, N_EXPERTS // EXPERTS_IN_BODY) as pair:
                    for j in range(EXPERTS_IN_BODY):
                        n = l * N_EXPERTS + pair * EXPERTS_IN_BODY + j
                        turns = l * (16 * LAYER_TURNS) + pair * (16 * EXPERTS_IN_BODY * EXPERT_UNITS // RING)
                        turn0 = (IN_UNITS + WO_UNITS) // RING
                        pe.wait_ge(h_ready, n * TILES + 1)
                        for w in range(2):
                            for q in range(CHUNK_UNITS):
                                u = j * EXPERT_UNITS + w * CHUNK_UNITS + q
                                pe.wait_ge(unit_in[u % RING], turns + 16 * (turn0 + u // RING + 1))
                                for t in range(TILES):
                                    for kk in range(KU):
                                        k = q * KU + kk
                                        last = mm(pp[2 * w + t][:, :], xT[:, k, t * P:(t + 1) * P],
                                                  ring[:, u % RING, kk, :], start=(k == 0), stop=(k == KT - 1))
                                last.then_inc(slots_free, 1)
                        for t in range(TILES):
                            pe.wait_ge(h_ready, n * TILES + t + 2)
                            pe.wait_ge(hT_ready, n * TILES + t + 1)
                            for k in range(4):
                                last = pe.transpose(pb[0][:, k * P:(k + 1) * P], sg[t][:, k * P:(k + 1) * P], ident)
                            last.then_inc(hT_filled, 1)
                            pe.wait_ge(hT_ready, n * TILES + t + 2)
                            for c in range(4):
                                d = t * 4 + c
                                pe.wait_ge(down_added, n * 8 + (d + 1))
                                for k in range(4):
                                    u = j * EXPERT_UNITS + 2 * CHUNK_UNITS + k
                                    pe.wait_ge(unit_in[u % RING], turns + 16 * (turn0 + u // RING + 1))
                                    wd = ring[:, u % RING, :, :].rearrange("p k n -> p (k n)")
                                    last = mm(pb[1 + d % 2][:, :], hT[t][:, k * P:(k + 1) * P],
                                              wd[:, c * NW:(c + 1) * NW], start=(k == 0), stop=(k == 3))
                                    if d == 7:
                                        last.then_inc(slots_free, 1)
                                if d < 7:
                                    last.then_inc(down_filled, 1)

        @block.vector
        def _(dve):
            links = [0]
            dve.wait_ge(consts_in, 32)
            dve.wait_ge(x_in, 16)
            dve.sem_inc(down_added, 2)
            dve.sem_inc(h_ready, 1)
            dve.sem_inc(x_ready, 1)
            with dve.Fori(0, DEPTH) as l:
                def link(ins, alone=False):
                    links[0] += 1
                    ins.then_inc(dve_link, 1)
                    if alone:
                        wait_apart(dve, dve_link, l * DVE_LINKS + links[0])
                    else:
                        dve.wait_ge(dve_link, l * DVE_LINKS + links[0])

                def root(which, n, variance, eps):
                    dve.tensor_scalar(var[:, 0:n], variance, eps, None, ALU.add).then_inc(var_ready, 1)
                    dve.wait_ge(root_ready, l * NORMS + which + 1)
                    link(dve.tensor_tensor(nt[:, 0:n], rstd[:, 0:n], rstd[:, 0:n], ALU.mult))
                    link(dve.tensor_tensor(nt[:, 0:n], nt[:, 0:n], var[:, 0:n], ALU.mult))
                    link(dve.tensor_scalar(nt[:, 0:n], nt[:, 0:n], -0.5, 1.5, ALU.mult, ALU.add))
                    link(dve.tensor_tensor(rstd[:, 0:n], rstd[:, 0:n], nt[:, 0:n], ALU.mult))

                def layer_norm(which, i):
                    for t in range(TILES):
                        link(dve.bn_aggr(mv[:, t, :], st[:, t, :, :].rearrange("p a b -> p (a b)")), alone=True)
                    root(which, TILES, mv[:, 0:TILES, 1], LN_EPS)
                    dve.wait_ge(lnp_in, l * 64 + 32 * (i + 1))
                    for t in range(TILES):
                        link(dve.tensor_scalar(xs[:, t, :], xs[:, t, :], mv[:, t, 0:1], rstd[:, t:t + 1],
                                               ALU.subtract, ALU.mult))
                        link(dve.tensor_tensor(xs[:, t, :], xs[:, t, :], ln_g, ALU.mult))
                        dve.tensor_tensor(xs[:, t, :], xs[:, t, :], ln_b, ALU.add).then_inc(x_ready, 1)

                for kind, h in STEPS:
                    step = (kind, h)
                    if kind == "ckvn":
                        dve.wait_ge(chunk_out, l * len(CHUNKS) + 2)
                        for t in range(TILES):
                            for j in range(2):
                                link(dve.tensor_copy(dkv[:, 0, t * P + j * IDX_DIM:t * P + (j + 1) * IDX_DIM],
                                                     col(C_KI, t, IDX_DIM)))
                        for t in range(TILES):
                            link(dve.bn_stats(st[:, t, 0, :], col(C_CKV, t, KV_RANK)), alone=True)
                            link(dve.bn_aggr(mv[:, t, :], st[:, t, 0, :]))
                        link(dve.tensor_tensor(nt[:, 0:TILES], mv[:, 0:TILES, 0], mv[:, 0:TILES, 0], ALU.mult))
                        link(dve.tensor_tensor(nt[:, 0:TILES], nt[:, 0:TILES], mv[:, 0:TILES, 1], ALU.add))
                        root(N_CKV, TILES, nt[:, 0:TILES], RMS_EPS)
                        dve.tensor_scalar(col(C_CKV, 0, KV_RANK), col(C_CKV, 0, KV_RANK), rstd[:, 0:1], None, ALU.mult)
                        dve.tensor_scalar(col(C_CKV, 1, KV_RANK), col(C_CKV, 1, KV_RANK), rstd[:, 1:2], None,
                                          ALU.mult).then_inc(ckvn_ready, 1)
                    elif kind == "ckvT":
                        wait_filled(dve, l, step)
                        dve.wait_ge(layer_in, l * 48 + 48)
                        for r in range(2):
                            last = dve.tensor_scalar(kvn(r), bank(step)[:, r * SEQ:(r + 1) * SEQ].rearrange(
                                "p (t s) -> p t s", t=2), kvg_col[:, r:r + 1], None, ALU.mult)
                        last.then_inc(dve_drained, 1)
                    elif kind == "idx":
                        wait_drained(dve, l, step)
                        for t, (a, b) in enumerate(((0, P), (P, TRI))):
                            w = col(C_W + h, t, 1)
                            if h == 0:
                                last = dve.tensor_scalar(score[:, a:b], rel[h % 2][:, a:b], w, None, ALU.mult)
                            else:
                                last = dve.scalar_tensor_tensor(score[:, a:b], rel[h % 2][:, a:b], w, score[:, a:b],
                                                                ALU.mult, ALU.add)
                        last.then_inc(rel_used, 1)
                        dve.wait_ge(rel_used, l * IDX_HEADS + h + 1)
                    elif kind == "topk":
                        link(dve.tensor_scalar(work, score, IDX_SCALE, None, ALU.mult))
                        diag = work.rearrange("p (b j) -> p b j", b=3)[:, 0:3:2, :]
                        link(dve.tensor_tensor(diag, diag,
                                               tab[:, T_CAUSAL:T_CAUSAL + P].unsqueeze(1).broadcast_to([P, 2, P]),
                                               ALU.add), alone=True)
                        for a, b in ((0, P), (P, TRI)):
                            for _ in range(TOPK // 8):
                                link(dve.max(top8[:, :], work[:, a:b]), alone=True)
                                link(dve.match_replace(work[:, a:b], top8[:, :], work[:, a:b], TAKEN), alone=True)
                        link(dve.tensor_scalar(sel[:, :], work, 0.5 * TAKEN, NEG, ALU.is_gt, ALU.mult))
                        diag = sel[:, :].rearrange("p (b j) -> p b j", b=3)[:, 0:3:2, :]
                        link(dve.tensor_tensor(diag, diag,
                                               tab[:, T_CAUSAL:T_CAUSAL + P].unsqueeze(1).broadcast_to([P, 2, P]),
                                               ALU.min))
                    elif kind == "dqT":
                        wait_filled(dve, l, step)
                        dve.tensor_copy(cols(C_DQ + h * P), bank(step)[:, 0:SEQ].rearrange(
                            "p (t s) -> p t s", t=2)).then_inc(dve_drained, 1)
                    elif kind == "log":
                        wait_filled(dve, l, step)
                        dve.scalar_tensor_tensor(dp[:, h % 2, :], bank(step)[:, 0:TRI], SCALE, sel[:, :],
                                                 ALU.mult, ALU.add).then_inc(dve_drained, 1)
                        wait_drained(dve, l, step)
                        for t, (a, b) in enumerate(((0, P), (P, TRI))):
                            link(dve.tensor_reduce(nmax[:, h % 2, t:t + 1], dp[:, h % 2, a:b], AX_X, ALU.max))
                        dve.tensor_scalar(nmax[:, h % 2, :], nmax[:, h % 2, :], -1.0, None,
                                          ALU.mult).then_inc(max_ready, 1)
                        dve.wait_ge(exp_ready, l * (2 * DSA_HEADS) + 2 * (h + 1))
                        link(dve.reciprocal(psums[:, h % 2, :], psums[:, h % 2, :]))
                        dve.tensor_scalar(dp[:, h % 2, 0:P], dp[:, h % 2, 0:P], psums[:, h % 2, 0:1], None, ALU.mult)
                        dve.tensor_scalar(dp[:, h % 2, P:TRI], dp[:, h % 2, P:TRI], psums[:, h % 2, 1:2], None,
                                          ALU.mult).then_inc(p_ready, 1)
                    elif kind in ("out", "sbo"):
                        wait_filled(dve, l, step)
                        m = h if kind == "sbo" else SB_HEADS + RET_HEADS + h
                        dve.tensor_copy(yT[:, m, :], bank(step)[:, 0:SEQ]).then_inc(dve_drained, 1)
                    elif kind == "z":
                        dve.wait_ge(ln_ready, l * SB_HEADS + h + 1)
                        dve.scalar_tensor_tensor(sba[:, h, :], bank(step)[:, 0:TRI], 0.0, sba[:, h, :],
                                                 ALU.max, ALU.add).then_inc(dve_drained, 1)
                        wait_drained(dve, l, step)
                        diag = sba[:, h, :].rearrange("p (b j) -> p b j", b=3)[:, 0:3:2, :]
                        dve.tensor_tensor(diag, diag,
                                          tab[:, T_STRICT:T_STRICT + P].unsqueeze(1).broadcast_to([P, 2, P]),
                                          ALU.mult).then_inc(sp_ready, 1)
                    elif kind == "rT":
                        wait_filled(dve, l, step)
                        b = bank(step)[:, :].rearrange("p (j t s) -> p j t s", j=2, t=2)
                        dve.tensor_copy(cols(C_RQ + h * P), b[:, 0])
                        dve.tensor_copy(cols(C_RK + h * P), b[:, 1]).then_inc(dve_drained, 1)
                    elif kind == "rs":
                        wait_filled(dve, l, step)
                        dve.tensor_tensor(ra[:, h, :], bank(step)[:, 0:TRI],
                                          tab[:, T_DECAY + h * TRI:T_DECAY + (h + 1) * TRI],
                                          ALU.mult).then_inc(dve_drained, 1)
                    elif kind == "ro":
                        wait_filled(dve, l, step)
                        dve.tensor_copy(ro[:, :, h * P:(h + 1) * P],
                                        bank(step)[:, 0:SEQ].rearrange("p (t d) -> p t d", t=2)).then_inc(dve_drained, 1)
                    elif kind == "gn":
                        wait_drained(dve, l, ("ro", RET_HEADS - 1))
                        for t in range(TILES):
                            for i in range(RET_HEADS):
                                last = dve.bn_stats(st[:, t, i, :], ro[:, t, i * P:(i + 1) * P])
                        link(last, alone=True)
                        for i in range(TILES * RET_HEADS):
                            last = dve.bn_aggr(mv[:, i, :], st[:, i // RET_HEADS, i % RET_HEADS, :])
                        link(last)
                        dve.wait_ge(gexp_ready, l + 1)
                        g = sig_g
                        link(dve.tensor_scalar(g, g, 1.0, None, ALU.add))
                        link(dve.reciprocal(g, g))
                        link(dve.tensor_tensor(g, g, pr[:, :, C_RG:C_RG + RET_HEADS * P], ALU.mult))
                        root(N_RET, TILES * RET_HEADS, mv[:, :, 1], GN_EPS)
                        for i in range(TILES * RET_HEADS):
                            t, k = i // RET_HEADS, i % RET_HEADS
                            v = ro[:, t, k * P:(k + 1) * P]
                            last = dve.tensor_scalar(v, v, mv[:, i, 0:1], rstd[:, i:i + 1], ALU.subtract, ALU.mult)
                        link(last)
                        dve.tensor_tensor(ro, ro, g, ALU.mult).then_inc(gn_ready, 1)
                    elif kind == "ryT":
                        wait_filled(dve, l, step)
                        for j in range(2):
                            last = dve.tensor_scalar(yT[:, SB_HEADS + 2 * h + j, :], bank(step)[:, j * SEQ:(j + 1) * SEQ],
                                                     gn_col[:, 2 * h + j:2 * h + j + 1], None, ALU.mult)
                        last.then_inc(dve_drained, 1)

                for n in range(WO_CHUNKS):
                    dve.wait_ge(slots_free, freed(l, IN_UNITS + (n + 1) * CHUNK_UNITS - 1))
                    for t in range(TILES):
                        v = xs[:, t, n * NW:(n + 1) * NW]
                        last = dve.scalar_tensor_tensor(v, v, ALPHA, pp[2 * (n % 2) + t][:, :], ALU.mult, ALU.add)
                    last.then_inc(mix_added, 1)
                    dve.wait_ge(mix_added, l * WO_CHUNKS + n + 1)
                    for t in range(TILES):
                        link(dve.bn_stats(st[:, t, n, :], xs[:, t, n * NW:(n + 1) * NW]), alone=True)
                layer_norm(N_LN1, 0)

                dve.wait_ge(route_filled, l + 1)
                lg, pe_, c1, c2, c3, gr, m1, m2 = (rt[:, i] for i in range(8))
                link(dve.tensor_copy(lg, pb[1][:, 0:TILES * N_EXPERTS].rearrange("p (t e) -> p t e", t=TILES)))
                link(dve.tensor_reduce(nt[:, 0:TILES], lg, AX_X, ALU.max))
                dve.tensor_tensor(lg, lg, nt[:, 0:TILES].unsqueeze(2).broadcast_to([P, TILES, N_EXPERTS]),
                                  ALU.subtract).then_inc(rmax_ready, 1)
                dve.wait_ge(rexp_ready, l + 1)
                link(dve.tensor_reduce(nt[:, 0:TILES], pe_, AX_X, ALU.add))
                link(dve.reciprocal(nt[:, 0:TILES], nt[:, 0:TILES]))
                link(dve.tensor_tensor(pe_, pe_, nt[:, 0:TILES].unsqueeze(2).broadcast_to([P, TILES, N_EXPERTS]),
                                       ALU.mult))
                pg = pe_.rearrange("p t (g e) -> p t g e", g=N_GROUPS)

                def part(v, i):
                    return v[:, :, i * N_GROUPS:(i + 1) * N_GROUPS]

                link(dve.tensor_tensor(part(c1, 0), pg[:, :, :, 0], pg[:, :, :, 1], ALU.max))
                link(dve.tensor_tensor(part(c1, 1), pg[:, :, :, 0], pg[:, :, :, 1], ALU.min))
                link(dve.tensor_tensor(part(c1, 2), pg[:, :, :, 2], pg[:, :, :, 3], ALU.max))
                link(dve.tensor_tensor(part(c1, 3), pg[:, :, :, 2], pg[:, :, :, 3], ALU.min))
                link(dve.tensor_tensor(part(c2, 0), part(c1, 0), part(c1, 2), ALU.max))
                link(dve.tensor_tensor(part(c2, 1), part(c1, 0), part(c1, 2), ALU.min))
                link(dve.tensor_tensor(part(c2, 2), part(c1, 1), part(c1, 3), ALU.max))
                link(dve.tensor_tensor(part(c2, 1), part(c2, 1), part(c2, 2), ALU.max))
                link(dve.tensor_tensor(part(c2, 0), part(c2, 0), part(c2, 1), ALU.add))
                gs = part(c2, 0)
                rank = tab[:, T_RANK:T_RANK + N_EXPERTS].unsqueeze(1).broadcast_to([P, TILES, N_EXPERTS])
                grank = tab[:, T_RANK:T_RANK + N_GROUPS].unsqueeze(1).broadcast_to([P, TILES, N_GROUPS])

                def best(value, order, mask, n, tmp):
                    def over(v):
                        return v.unsqueeze(2).broadcast_to([P, TILES, n])
                    link(dve.tensor_reduce(nt[:, 0:2], value, AX_X, ALU.max))
                    link(dve.tensor_tensor(mask, value, over(nt[:, 0:2]), ALU.is_equal))
                    link(dve.tensor_tensor(mask, mask, order, ALU.mult))
                    link(dve.tensor_reduce(nt[:, 2:4], mask, AX_X, ALU.max))
                    link(dve.tensor_tensor(mask, mask, over(nt[:, 2:4]), ALU.is_equal))

                best(gs, grank, part(c3, 0), N_GROUPS, c1)
                link(dve.tensor_copy(gr.rearrange("p t (g e) -> p t g e", g=N_GROUPS),
                                     part(c3, 0).unsqueeze(3).broadcast_to([P, TILES, N_GROUPS, PER_GROUP])))
                link(dve.tensor_tensor(c1, pe_, gr, ALU.mult))
                link(dve.tensor_scalar(c2, gr, 1.0, None, ALU.subtract))
                link(dve.tensor_tensor(c1, c1, c2, ALU.add))
                best(c1, rank, m1, N_EXPERTS, c3)
                link(dve.tensor_copy(nt[:, 4:6], nt[:, 0:2]))
                link(dve.tensor_scalar(c2, m1, -4.0, None, ALU.mult))
                link(dve.tensor_tensor(c1, c1, c2, ALU.add))
                best(c1, rank, m2, N_EXPERTS, c3)
                link(dve.tensor_tensor(nt[:, 2:4], nt[:, 0:2], nt[:, 4:6], ALU.add))
                link(dve.reciprocal(nt[:, 2:4], nt[:, 2:4]))
                link(dve.tensor_tensor(m1, m1, m2, ALU.add))
                link(dve.tensor_tensor(m1, m1, pe_, ALU.mult))
                link(dve.tensor_tensor(gates[:, :, :], m1, nt[:, 2:4].unsqueeze(2).broadcast_to([P, TILES, N_EXPERTS]),
                                       ALU.mult))
                dve.wait_ge(xt_filled, (l + 1) * (2 * XT_FILLS))
                link(dve.tensor_scalar(xs[:, :, :], xs[:, :, :], ALPHA, None, ALU.mult), alone=True)

                with dve.Fori(0, N_EXPERTS // EXPERTS_IN_BODY) as pair:
                    for j in range(EXPERTS_IN_BODY):
                        e = pair * EXPERTS_IN_BODY + j
                        n = l * N_EXPERTS + e
                        for t in range(TILES):
                            dve.wait_ge(gexp2, n * TILES + t + 1)
                            own = (n * TILES + t) * 3
                            dve.tensor_scalar(sg[t], sg[t], 1.0, None, ALU.add).then_inc(moe_link, 1)
                            dve.wait_ge(moe_link, own + 1)
                            dve.reciprocal(sg[t], sg[t]).then_inc(moe_link, 1)
                            dve.wait_ge(moe_link, own + 2)
                            dve.tensor_tensor(sg[t], sg[t], pp[t][:, :], ALU.mult).then_inc(moe_link, 1)
                            dve.wait_ge(moe_link, own + 3)
                            dve.scalar_tensor_tensor(sg[t], pp[2 + t][:, :], gates[:, t, bass.ds(e, 1)], sg[t],
                                                     ALU.mult, ALU.mult).then_inc(h_ready, 1)
                        for t in range(TILES):
                            for c in range(4):
                                d = t * 4 + c
                                if d < 7:
                                    dve.wait_ge(down_filled, n * 7 + d + 1)
                                else:
                                    dve.wait_ge(slots_free, l * LAYER_UNITS + pair * (EXPERTS_IN_BODY * EXPERT_UNITS)
                                                + (RING + IN_UNITS + WO_UNITS + (j + 1) * EXPERT_UNITS))
                                if d == 0:
                                    dve.wait_ge(down_added, n * 8 + 2)
                                v = xs[:, t, c * NW:(c + 1) * NW]
                                dve.tensor_tensor(v, v, pb[1 + d % 2][:, :], ALU.add).then_inc(down_added, 1)
                dve.wait_ge(down_added, (l + 1) * (N_EXPERTS * 8) + 2)
                for t in range(TILES):
                    for n in range(WO_CHUNKS):
                        link(dve.bn_stats(st[:, t, n, :], xs[:, t, n * NW:(n + 1) * NW]), alone=True)
                layer_norm(N_LN2, 1)
            assert links[0] == DVE_LINKS, links


def constants():
    import numpy as np
    f = np.float32
    tab = np.zeros((P, T_COLS), f)
    p, i = np.arange(P)[:, None], np.arange(P)[None, :]
    tab[:, T_ID:T_ID + P] = p == i
    tab[:, T_SUM:T_SUM + P] = np.where(p >= i, f(-1), f(0))
    tab[:, T_NONE:T_NONE + P] = -1
    tab[:, T_STRICT:T_STRICT + P] = p < i
    tab[:, T_NSTRICT:T_NSTRICT + P] = np.where(p >= i, f(NEG), f(0))
    tab[:, T_CAUSAL:T_CAUSAL + P] = np.where(i > p, f(NEG), f(0))
    for h in range(RET_HEADS):
        log_gamma = np.log1p(-(2.0 ** (-5.0 - h)))
        for at, key, query in ((0, p, np.arange(SEQ)[None, :]), (SEQ, p + P, i + P)):
            d = query - key
            v = np.where(d >= 0, np.exp(np.maximum(d, 0) * log_gamma) * SCALE, 0.0)
            first = T_DECAY + h * TRI + at
            tab[:, first:first + v.shape[1]] = v
    theta = f(10000.0) ** (-np.linspace(0.0, 1.0, HEAD_DIM // 2, dtype=f))
    for t in range(TILES):
        ang = (np.arange(P, dtype=f) + f(t * P))[:, None] * theta[None, :]
        tab[:, T_COS + t * P:T_COS + (t + 1) * P] = np.concatenate([np.cos(ang)] * 2, 1)
        tab[:, T_SIN + t * P:T_SIN + (t + 1) * P] = np.concatenate([-np.sin(ang), np.sin(ang)], 1)
    tab[:, T_RANK:T_RANK + N_EXPERTS] = np.arange(N_EXPERTS, 0, -1)
    return tab


INPUTS = ["x", "w_in", "w_kv_up", "kv_norm_g", "ret_gn_g", "w_o", "ln1_g", "ln1_b", "w_router",
          "w_gate", "w_up", "w_down", "ln2_g", "ln2_b"]


def kernel(**inputs):
    import numpy as np
    import concourse.bacc as bacc
    from concourse.bass_utils import run_bass_kernel_spmd

    nc = bacc.Bacc("TRN2", target_bir_lowering=False, num_devices=1)
    arrays, args = {}, {}
    for name in INPUTS + ["tables"]:
        a = constants() if name == "tables" else np.ascontiguousarray(inputs[name])
        if name in ("w_gate", "w_up", "w_down"):
            a = a.reshape((DEPTH * N_EXPERTS,) + a.shape[2:])
        if name in ("kv_norm_g", "ret_gn_g"):
            a = np.ascontiguousarray(a.reshape(DEPTH, -1, P).transpose(0, 2, 1))
        arrays[f"in_{name}"] = a
        args[name] = nc.dram_tensor(f"in_{name}", a.shape, F32, kind="ExternalInput").ap()
    args["out"] = nc.dram_tensor("result", (1, SEQ, D_MODEL), F32, kind="ExternalOutput").ap()
    trunk(nc, **args)
    r = run_bass_kernel_spmd(nc, [arrays], core_ids=[0])
    return r.results[0]["result"]
```

```python
from contextlib import ExitStack

import concourse.bass as bass
from concourse import mybir

F32 = mybir.dt.float32
I32 = mybir.dt.int32
U32 = mybir.dt.uint32
ALU = mybir.AluOpType
ACT = mybir.ActivationFunctionType
AX_X = mybir.AxisListType.X

P = 128
D_MODEL, SEQ, DEPTH = 2048, 256, 2
TILES = SEQ // P
HEAD_DIM = 128
SB_HEADS, RET_HEADS, DSA_HEADS = 6, 4, 6
KV_RANK, IDX_HEADS, IDX_DIM = 256, 8, 64
TOPK = min(256, SEQ // 4)
N_EXPERTS, N_GROUPS, D_FF = 16, 4, 512
PER_GROUP = N_EXPERTS // N_GROUPS
LN_EPS, RMS_EPS, GN_EPS = 1e-5, 1e-6, 1e-6
ALPHA = (2 * DEPTH) ** 0.25
SCALE = HEAD_DIM ** -0.5
IDX_SCALE = IDX_DIM ** -0.5 * IDX_HEADS ** -0.5
NEG = -1.0e30
TAKEN = -3.0e38

C_SBQ = 0
C_SBK = C_SBQ + SB_HEADS * HEAD_DIM
C_SBV = C_SBK + SB_HEADS * HEAD_DIM
C_RQ = C_SBV + SB_HEADS * HEAD_DIM
C_RK = C_RQ + RET_HEADS * HEAD_DIM
C_RV = C_RK + RET_HEADS * HEAD_DIM
C_RG = C_RV + RET_HEADS * HEAD_DIM
C_DQ = C_RG + RET_HEADS * HEAD_DIM
C_CKV = C_DQ + DSA_HEADS * HEAD_DIM
C_QI = C_CKV + KV_RANK
C_KI = C_QI + IDX_HEADS * IDX_DIM
C_W = C_KI + IDX_DIM
D_IN = C_W + IDX_HEADS

KT = D_MODEL // P
NW = 512
KU = 4
CHUNK_UNITS = KT // KU
RING = 8
CHUNKS = [10, 11, 9, 8, 0, 1, 2, 5, 6, 4, 7, 3]
WO_CHUNKS = D_MODEL // NW
IN_UNITS = len(CHUNKS) * CHUNK_UNITS
WO_UNITS = WO_CHUNKS * CHUNK_UNITS
EXPERT_UNITS = 3 * CHUNK_UNITS
MOE = IN_UNITS + WO_UNITS
SLOTS = P
ROWS = 2 * SEQ
COUNTS = 4 * N_EXPERTS + 2

OVER_W, OVER_X, OVER_PE, OVER_ACT, OVER_DVE, OVER_LINK = 16 * EXPERT_UNITS, 32, 10, 6, 5, 3


PAIRS = N_EXPERTS // 2 - 1
PAIR_UNITS = 2 * EXPERT_UNITS
LAYER_UNITS = IN_UNITS + WO_UNITS + N_EXPERTS * EXPERT_UNITS
LAYER_TURNS = LAYER_UNITS // RING
FRONT_0 = MOE
FRONT_ODD = FRONT_0 + 2 * CHUNK_UNITS
BACK_EVEN = FRONT_ODD + 2 * CHUNK_UNITS
FRONT_EVEN = BACK_EVEN + CHUNK_UNITS
BACK_ODD = FRONT_EVEN + 2 * CHUNK_UNITS
LAST = PAIRS * PAIR_UNITS
BACK_LAST = BACK_EVEN + LAST + CHUNK_UNITS

TRI = 3 * P
MOST_OVERS = DEPTH * (ROWS // (SLOTS + 1))

T_ID = 0
T_SUM = T_ID + P
T_NONE = T_SUM + P
T_STRICT = T_NONE + P
T_NSTRICT = T_STRICT + P
T_CAUSAL = T_NSTRICT + P
T_DECAY = T_CAUSAL + P
T_COS = T_DECAY + RET_HEADS * TRI
T_SIN = T_COS + TILES * HEAD_DIM
T_RANK = T_SIN + TILES * HEAD_DIM
T_COLS = T_RANK + N_EXPERTS


def width(n):
    return min(NW, D_IN - n * NW)


def plan():
    idx = [[("qiT", 0), ("qiT", 1)], [("ckvT", 0), ("kiT", 0)]]
    idx += [[("idx", h), ("idx", h + 1)] for h in range(0, IDX_HEADS, 2)]
    idx[-1].append(("topk", 0))
    dsa = []
    for i in range(DSA_HEADS + 1):
        a, b = [], []
        if i < DSA_HEADS:
            a += [("kv", i), ("dqT", i)]
            b += [("log", i)]
        if i >= 1:
            a += [("pT", i - 1)]
            b += [("out", i - 1)]
        dsa += [a, b[::-1]]
    sb = []
    for i in range(SB_HEADS + 2):
        a = []
        if i < SB_HEADS:
            a.append(("sbT", i))
        if 1 <= i <= SB_HEADS:
            a.append(("z", i - 1))
        if i >= 2:
            a.append(("arg", i - 2))
        sb.append(a)
    ret = []
    for i in range(RET_HEADS + 1):
        a = []
        if i < RET_HEADS:
            a.append(("rT", i))
        if i >= 1:
            a += [("rs", i - 1)]
        ret.append(a)
    streams = [
        [(2, [("ckvn", 0)])] + [(2, s) for s in idx] + [(4, s) for s in dsa],
        [(7, s) for s in sb] + [(10, [("sbo", 4), ("sbo", 5)])],
        [(10, [("rot", 0)])] + [(10, s) for s in ret] + [(11, [("ro", h), ("ro", h + 1)]) for h in (0, 2)]
        + [(11, [("gn", 0)])],
    ]
    steps = []
    for u in range(IN_UNITS):
        steps.append(("proj", u))
        have = u // CHUNK_UNITS
        for s in streams:
            if s and s[0][0] <= have:
                steps += s.pop(0)[1]
    for s in streams:
        for need, more in s:
            steps += more
    steps += [("sbo", h) for h in range(4)] + [("ryT", 0), ("ryT", 1)]
    return steps


STEPS = plan()
DRAIN = {"qiT": "act", "ckvT": "dve", "kiT": "act", "idx": "act", "kv": "act", "dqT": "dve", "log": "dve",
         "pT": "act", "out": "dve", "sbT": "act", "z": "dve", "arg": "act", "sbo": "dve", "rT": "dve",
         "rs": "dve", "ro": "dve", "ryT": "dve"}
FILLS = [s for s in STEPS if s[0] in DRAIN]
FILL_AT = {s: n for n, s in enumerate(FILLS)}
BANKS = 4


def reads(kind, h):
    return {"idx": [("qiT", h // 4), ("kiT", 0)], "kv": [("ckvT", 0)], "log": [("kv", h), ("dqT", h)],
            "out": [("pT", h)], "z": [("sbT", h)], "arg": [("sbT", h)], "rs": [("rT", h)],
            "sbo": [("arg", h)], "ro": [("rs", h)]}.get(kind, [])


DRAINS = {e: sum(DRAIN[s[0]] == e for s in FILLS) for e in ("act", "dve")}
DRAIN_AT = {s: sum(DRAIN[r[0]] == DRAIN[s[0]] for r in FILLS[:n + 1]) for n, s in enumerate(FILLS)}

ACT_LINKS = 16
DVE_LINKS = 184
POOL_LINKS = 7
XT_FILLS = TILES * KT // 4
NORMS = 4
(N_CKV, N_RET, N_LN1, N_LN2) = range(NORMS)


def trunk(nc, x, w_in, w_kv_up, kv_norm_g, ret_gn_g, w_o, ln1_g, ln1_b, w_router,
          w_gate, w_up, w_down, ln2_g, ln2_b, tables, out):
    with ExitStack() as ctx:
        def sb(name, *shape):
            return ctx.enter_context(nc.sbuf_tensor(name, [P, *shape], F32))

        def sem(name):
            return ctx.enter_context(nc.semaphore(name))

        ring = sb("ring", RING, KU, NW)
        xs = sb("xs", TILES, D_MODEL)
        xT = sb("xT", KT, SEQ)
        proj = sb("proj", TILES * D_IN)
        kvup = sb("kvup", KV_RANK // P, DSA_HEADS * 2 * HEAD_DIM)
        yT = sb("yT", KT, SEQ)
        tab = sb("tab", T_COLS)
        wr = sb("wr", KT, N_EXPERTS)
        gn_col = sb("gn_col", RET_HEADS)
        kvg_col = sb("kvg_col", KV_RANK // P)
        dkv = sb("dkv", 2, 4 * P)
        dp = sb("dp", 2, TRI)
        sba = sb("sba", SB_HEADS, TRI)
        ra = sb("ra", RET_HEADS, TRI)
        sel = sb("sel", TRI)
        st = sb("st", TILES, 4, 6)
        mv = sb("mv", TILES * RET_HEADS, 2)
        var = sb("var", TILES * RET_HEADS)
        rstd = sb("rstd", TILES * RET_HEADS)
        nt = sb("nt", TILES * RET_HEADS)
        top8 = sb("top8", 8)
        nmax = sb("nmax", 2, TILES)
        psums = sb("psums", 2, TILES)
        wts = sb("wts", 2, TILES)
        place = ctx.enter_context(nc.sbuf_tensor("place", [P, 2 * TILES], U32))
        overs = sb("overs", 1)
        counts = ctx.enter_context(nc.sbuf_tensor("counts", [P, COUNTS], I32))

        pr = proj[:, :].rearrange("p (t n) -> p t n", t=TILES)
        ro = pr[:, :, C_RQ:C_RQ + RET_HEADS * P]
        score = yT[:, 0:2, :].rearrange("p k s -> p (k s)")[:, 0:TRI]
        work = yT[:, 2:4, :].rearrange("p k s -> p (k s)")[:, 0:TRI]
        rel = [yT[:, k:k + 2, :].rearrange("p k s -> p (k s)")[:, 0:TRI] for k in (4, 14)]
        rot = [yT[:, k:k + 2, :].rearrange("p k s -> p (k s)") for k in (6, 8)]
        sig_g = yT[:, 6:10, :].rearrange("p (t k) s -> p t (k s)", t=TILES)
        ln_g, ln_b = proj[:, 0:D_MODEL], proj[:, D_MODEL:2 * D_MODEL]
        xg = [proj[:, (2 + i) * D_MODEL:(3 + i) * D_MODEL] for i in range(2)]
        sg = [proj[:, 4 * D_MODEL + i * D_FF:4 * D_MODEL + (i + 1) * D_FF] for i in range(2)]
        hT = [proj[:, 4 * D_MODEL + (2 + i) * D_FF:4 * D_MODEL + (3 + i) * D_FF] for i in range(2)]
        rt = proj[:, 5 * D_MODEL:5 * D_MODEL + 8 * TILES * N_EXPERTS].rearrange(
            "p (i t e) -> p i t e", i=8, t=TILES)
        yb = [yT[:, i * KT // 2:(i + 1) * KT // 2, :].rearrange("p k s -> p (k s)") for i in range(2)]

        pp = [ctx.enter_context(nc.psum_tensor(f"pp{i}", [P, NW], F32)) for i in range(4)]
        pb = [ctx.enter_context(nc.psum_tensor(f"pb{i}", [P, NW], F32)) for i in range(BANKS)]

        consts_in = sem("consts_in")
        x_in = sem("x_in")
        layer_in = sem("layer_in")
        lnp_in = sem("lnp_in")
        unit_in = [sem(f"unit_in{i}") for i in range(RING)]
        slots_free = sem("slots_free")
        xt_filled = sem("xt_filled")
        xt_copied = sem("xt_copied")
        chunk_out = sem("chunk_out")
        filled = sem("filled")
        act_drained = sem("act_drained")
        dve_drained = sem("dve_drained")
        ckvn_ready = sem("ckvn_ready")
        rel_ready = sem("rel_ready")
        rel_used = sem("rel_used")
        ln_ready = sem("ln_ready")
        sp_ready = sem("sp_ready")
        max_ready = sem("max_ready")
        exp_ready = sem("exp_ready")
        p_ready = sem("p_ready")
        rot_ready = sem("rot_ready")
        gexp_ready = sem("gexp_ready")
        gn_ready = sem("gn_ready")
        var_ready = sem("var_ready")
        root_ready = sem("root_ready")
        mix_added = sem("mix_added")
        x_ready = sem("x_ready")
        route_filled = sem("route_filled")
        rexp_ready = sem("rexp_ready")
        rmax_ready = sem("rmax_ready")
        chosen = sem("chosen")
        counted = sem("counted")
        routed = sem("routed")
        sorted_out = sem("sorted_out")
        xg_in = [sem(f"xg_in{i}") for i in range(2)]
        xw_filled = sem("xw_filled")
        xw_copied = sem("xw_copied")
        gate_exp = sem("gate_exp")
        h_ready = sem("h_ready")
        hT_filled = sem("hT_filled")
        hT_ready = sem("hT_ready")
        y_copied = sem("y_copied")
        y_out = sem("y_out")
        back_in = [sem(f"back_in{i}") for i in range(2 * TILES)]
        over_w = sem("over_w")
        over_x = sem("over_x")
        over_pe = sem("over_pe")
        over_act = sem("over_act")
        over_dve = sem("over_dve")
        over_link = sem("over_link")
        out_done = sem("out_done")
        act_link = sem("act_link")
        dve_link = sem("dve_link")
        moe_link = sem("moe_link")
        waited = sem("waited")
        pool_link = sem("pool_link")

        ident = tab[:, T_ID:T_ID + P]

        def freed(l, unit):
            return l * LAYER_UNITS + (RING + unit + 1)

        def wait_drained(eng, l, *steps):
            for which, semaphore in (("act", act_drained), ("dve", dve_drained)):
                at = [DRAIN_AT[s] for s in steps if DRAIN[s[0]] == which]
                if at:
                    eng.wait_ge(semaphore, l * DRAINS[which] + max(at))

        def wait_filled(eng, l, step):
            eng.wait_ge(filled, l * len(FILLS) + FILL_AT[step] + 1)

        def bank(step):
            return pb[FILL_AT[step] % BANKS]

        def wait_apart(eng, semaphore, value):
            eng.wait_ge(semaphore, value)
            eng.sem_inc(waited, 1)

        def col(c, t, n=P):
            return pr[:, t, c:c + n]

        def kvn(r):
            return cols(C_CKV + r * P)

        def cols(c):
            return pr[:, :, c:c + P]

        x_sorted = nc.dram_tensor("x_sorted", (ROWS + SLOTS, D_MODEL), F32, kind="Internal").ap()
        y_sorted = nc.dram_tensor("y_sorted", (ROWS + SLOTS, D_MODEL), F32, kind="Internal").ap()

        def window(eng, e, table):
            return eng.value_load(counts[0:1, bass.ds(e + table * N_EXPERTS, 1)], min_val=0, max_val=ROWS)

        def tokens(eng, e):
            return eng.value_load(counts[0:1, bass.ds(e + N_EXPERTS, 1)], min_val=0, max_val=SEQ)

        def overs_before(eng, e):
            return eng.value_load(counts[0:1, bass.ds(e + 3 * N_EXPERTS, 1)], min_val=0, max_val=MOST_OVERS)

        def most_tokens(eng):
            return eng.value_load(counts[0:1, COUNTS - 2:COUNTS - 1], min_val=0, max_val=SEQ)

        block = ctx.enter_context(nc.Block())

        @block.sync
        def _(sp):
            sp.sem_inc(over_x, 16)
            with sp.Fori(0, DEPTH) as l:
                g = 0

                def unit(src, dst, base, g):
                    if g % RING == 0:
                        wait_apart(sp, slots_free, base + g + 1)
                    else:
                        sp.wait_ge(slots_free, base + g + 1)
                    sp.dma_start(dst, src).then_inc(unit_in[g % RING], 16)

                for n in CHUNKS:
                    for q in range(CHUNK_UNITS):
                        src = w_in[bass.ds(l, 1), q * KU * P:(q + 1) * KU * P, n * NW:n * NW + width(n)]
                        unit(src.rearrange("a (k p) n -> p (a k) n", p=P), ring[:, g % RING, :, 0:width(n)],
                             l * LAYER_UNITS, g)
                        g += 1
                for n in range(WO_CHUNKS):
                    for q in range(CHUNK_UNITS):
                        src = w_o[bass.ds(l, 1), q * KU * P:(q + 1) * KU * P, n * NW:(n + 1) * NW]
                        unit(src.rearrange("a (k p) n -> p (a k) n", p=P), ring[:, g % RING, :, :],
                             l * LAYER_UNITS, g)
                        g += 1

                def front(e, u, pair):
                    for i, w in enumerate((w_gate, w_up)):
                        for q in range(CHUNK_UNITS):
                            src = w[bass.ds(l * N_EXPERTS + e, 1), q * KU * P:(q + 1) * KU * P, :]
                            unit(src.rearrange("a (k p) n -> p (a k) n", p=P), ring[:, u % RING, :, :],
                                 l * LAYER_UNITS + pair * PAIR_UNITS, u)
                            u += 1

                def back(e, u, pair):
                    for c in range(WO_CHUNKS):
                        src = w_down[bass.ds(l * N_EXPERTS + e, 1), :, c * NW:(c + 1) * NW]
                        unit(src.rearrange("a (k p) n -> p (a k) n", p=P), ring[:, u % RING, :, :],
                             l * LAYER_UNITS + pair * PAIR_UNITS, u)
                        u += 1

                front(0, FRONT_0, 0)
                with sp.Fori(0, PAIRS) as pair:
                    front(pair * 2 + 1, FRONT_ODD, pair)
                    back(pair * 2, BACK_EVEN, pair)
                    front(pair * 2 + 2, FRONT_EVEN, pair)
                    back(pair * 2 + 1, BACK_ODD, pair)
                front(N_EXPERTS - 1, FRONT_ODD + LAST, 0)
                back(N_EXPERTS - 2, BACK_EVEN + LAST, 0)
                back(N_EXPERTS - 1, BACK_LAST, 0)

                wait_apart(sp, routed, l + 1)
                most = most_tokens(sp)
                with sp.If(most > SLOTS):
                    wait_apart(sp, slots_free, (l + 1) * LAYER_UNITS + RING)
                    wait_apart(sp, y_out, (l + 1) * (16 * N_EXPERTS) + 32)
                    with sp.Fori(0, N_EXPERTS) as e:
                        n = tokens(sp, e)
                        with sp.If(n > SLOTS):
                            m = overs_before(sp, e)
                            first = window(sp, e, 2)
                            sp.dma_start(xg[0], x_sorted[bass.ds(first, SLOTS), :]).then_inc(over_x, 16)
                            for i, w in enumerate((w_gate, w_up)):
                                for q in range(CHUNK_UNITS):
                                    src = w[bass.ds(l * N_EXPERTS + e, 1), q * KU * P:(q + 1) * KU * P, :]
                                    sp.dma_start(ring[:, i * CHUNK_UNITS + q, :, :],
                                                 src.rearrange("a (k p) n -> p (a k) n", p=P)).then_inc(over_w, 16)
                            wait_apart(sp, over_pe, m * OVER_PE + 5)
                            for q in range(CHUNK_UNITS):
                                src = w_down[bass.ds(l * N_EXPERTS + e, 1), q * P:(q + 1) * P, :]
                                sp.dma_start(ring[:, q, :, :].rearrange("p k n -> p (k n)"),
                                             src.rearrange("a p n -> p (a n)")).then_inc(over_w, 16)
                            wait_apart(sp, over_dve, (m + 1) * OVER_DVE)
                            sp.dma_start(y_sorted[bass.ds(first, SLOTS), :], yb[0]).then_inc(over_x, 16)
                            wait_apart(sp, over_w, (m + 1) * OVER_W)
                            wait_apart(sp, over_x, (m + 1) * OVER_X + 16)
            sp.wait_ge(x_ready, 4 * DEPTH + 1)
            sp.dma_start(out.rearrange("a (t p) d -> p (a t) d", p=P), xs[:, :, :]).then_inc(out_done, 16)
            sp.wait_ge(out_done, 16)

        @block.gpsimd
        def _(pool):
            links = [0]
            pool.wait_ge(consts_in, 32)
            for table in (x_sorted, y_sorted):
                pool.dma_start(table[ROWS:ROWS + SLOTS, :], x[0, 0:SLOTS, :]).then_inc(y_out, 16)
            pool.wait_ge(y_out, 32)
            with pool.Fori(0, DEPTH) as l:
                def link(ins):
                    links[0] += 1
                    ins.then_inc(pool_link, 1)
                    pool.wait_ge(pool_link, l * POOL_LINKS + links[0])

                pool.wait_ge(chunk_out, l * len(CHUNKS) + 10)
                n = 0
                for c in (C_RQ, C_RK):
                    for t in range(TILES):
                        v = pr[:, t, c:c + RET_HEADS * P].rearrange("p (h d) -> p h d", h=RET_HEADS)
                        a = rot[0].rearrange("p (h d) -> p h d", h=RET_HEADS)
                        b = rot[1].rearrange("p (h d) -> p h d", h=RET_HEADS)
                        half = HEAD_DIM // 2

                        def table(first, n):
                            return tab[:, first:first + n].unsqueeze(1).broadcast_to([P, RET_HEADS, n])

                        pool.tensor_tensor(a, v, table(T_COS + t * P, P), ALU.mult)
                        pool.tensor_tensor(b[:, :, 0:half], v[:, :, half:P], table(T_SIN + t * P, half), ALU.mult)
                        link(pool.tensor_tensor(b[:, :, half:P], v[:, :, 0:half],
                                                table(T_SIN + t * P + half, half), ALU.mult))
                        last = pool.tensor_tensor(v, a, b, ALU.add)
                        n += 1
                        if n < 2 * TILES:
                            link(last)
                        else:
                            last.then_inc(rot_ready, 1)

                wait_apart(pool, routed, l + 1)
                for t in range(TILES):
                    for c in range(2):
                        pool.indirect_dma_start(
                            x_sorted, bass.IndirectOffsetOnAxis(ap=place[:, c * TILES + t:c * TILES + t + 1], axis=0),
                            xs[:, t, :], None).then_inc(sorted_out, 16)
                wait_apart(pool, sorted_out, (l + 1) * 64)

                def load(e, par, first_one=False):
                    first = window(pool, e, 0)
                    if not first_one:
                        wait_apart(pool, xw_filled, (l * N_EXPERTS + e) * 4)
                    pool.dma_start(xg[par], x_sorted[bass.ds(first, SLOTS), :]).then_inc(xg_in[par], 16)

                def store(e, par):
                    first = window(pool, e, 0)
                    n = l * N_EXPERTS + e
                    wait_apart(pool, y_copied, n * 4 + 6)
                    wait_apart(pool, y_out, n * 16 + 32)
                    pool.dma_start(y_sorted[bass.ds(first, SLOTS), :], yb[par]).then_inc(y_out, 16)

                load(0, 0, first_one=True)
                for e in (1, 2):
                    load(e, e % 2)
                with pool.Fori(0, PAIRS - 1) as pair:
                    for par in range(2):
                        load(pair * 2 + (3 + par), 1 - par)
                        store(pair * 2 + par, par)
                load(N_EXPERTS - 1, 1)
                for e in range(N_EXPERTS - 4, N_EXPERTS):
                    store(e, e % 2)
                wait_apart(pool, y_out, (l + 1) * (16 * N_EXPERTS) + 32)

                overs = pool.value_load(counts[0:1, COUNTS - 1:COUNTS], min_val=0, max_val=MOST_OVERS)
                wait_apart(pool, over_x, overs * OVER_X + 16)

                wait_apart(pool, xw_filled, (l + 1) * (4 * N_EXPERTS) + 4)
                for t in range(TILES):
                    for c in range(2):
                        pool.indirect_dma_start(
                            (xg, yb)[t][c], None, y_sorted,
                            bass.IndirectOffsetOnAxis(ap=place[:, c * TILES + t:c * TILES + t + 1], axis=0)).then_inc(
                                back_in[2 * t + c], 16)
            assert links[0] == POOL_LINKS, links

        @block.scalar
        def _(act):
            act.dma_start(tab[:, :], tables).then_inc(consts_in, 16)
            act.dma_start(wr[:, :, :], w_router.rearrange("(k p) e -> p k e", p=P)).then_inc(consts_in, 16)
            act.dma_start(xs[:, :, :], x.rearrange("a (t p) d -> p (a t) d", p=P)).then_inc(x_in, 16)
            act.sem_inc(hT_ready, 1)
            act.sem_inc(xw_copied, 1)
            links = [0]
            with act.Fori(0, DEPTH) as l:
                def link(ins):
                    links[0] += 1
                    ins.then_inc(act_link, 1)
                    act.wait_ge(act_link, l * ACT_LINKS + links[0])

                def root(which, n):
                    act.wait_ge(var_ready, l * NORMS + which + 1)
                    link(act.activation(rstd[:, 0:n], var[:, 0:n], ACT.Ln))
                    act.activation(rstd[:, 0:n], rstd[:, 0:n], ACT.Exp, scale=-0.5).then_inc(root_ready, 1)

                def copy_xT(i):
                    for f in range(XT_FILLS):
                        t, k = f // (KT // 4), f % (KT // 4) * 4
                        act.wait_ge(xt_filled, l * (2 * XT_FILLS) + (i * XT_FILLS + f + 1))
                        act.activation(xT[:, k:k + 4, t * P:(t + 1) * P],
                                       pb[f % BANKS][:, :].rearrange("p (k s) -> p k s", k=4),
                                       ACT.Copy).then_inc(xt_copied, 1)

                act.wait_ge(xt_filled, l * (2 * XT_FILLS) + 1)
                act.dma_start(kvup[:, :, :],
                              w_kv_up[bass.ds(l, 1)].rearrange("a (r p) n -> p (a r) n", p=P)).then_inc(layer_in, 16)
                act.dma_start(kvg_col[:, :],
                              kv_norm_g[bass.ds(l, 1)].rearrange("a p r -> (a p) r")).then_inc(layer_in, 16)
                act.dma_start(gn_col[:, :],
                              ret_gn_g[bass.ds(l, 1)].rearrange("a p h -> (a p) h")).then_inc(layer_in, 16)
                copy_xT(0)

                for kind, h in STEPS:
                    step = (kind, h)
                    if kind == "proj" and h % CHUNK_UNITS == CHUNK_UNITS - 1:
                        c = h // CHUNK_UNITS
                        n = CHUNKS[c]
                        act.wait_ge(slots_free, freed(l, h))
                        act.activation(pr[:, 0, n * NW:n * NW + width(n)], pp[2 * (c % 2)][:, 0:width(n)], ACT.Copy)
                        act.activation(pr[:, 1, n * NW:n * NW + width(n)], pp[2 * (c % 2) + 1][:, 0:width(n)],
                                       ACT.Copy).then_inc(chunk_out, 1)
                    elif kind == "ckvn":
                        root(N_CKV, TILES)
                    elif kind == "qiT":
                        wait_filled(act, l, step)
                        for j in range(2):
                            last = act.activation(cols(C_QI + (2 * h + j) * P),
                                                  bank(step)[:, j * SEQ:(j + 1) * SEQ].rearrange("p (t s) -> p t s", t=2),
                                                  ACT.Copy)
                        last.then_inc(act_drained, 1)
                    elif kind == "kiT":
                        wait_filled(act, l, step)
                        act.activation(dkv[:, 1, 0:SEQ], bank(step)[:, 0:SEQ], ACT.Copy).then_inc(act_drained, 1)
                    elif kind == "idx":
                        wait_filled(act, l, step)
                        if h >= 2:
                            act.wait_ge(rel_used, l * IDX_HEADS + h - 1)
                        act.activation(rel[h % 2], bank(step)[:, 0:TRI], ACT.Relu).then_inc(act_drained, 1)
                    elif kind == "kv":
                        wait_filled(act, l, step)
                        act.activation(dkv[:, h % 2, :], bank(step)[:, :], ACT.Copy).then_inc(act_drained, 1)
                    elif kind == "log":
                        act.wait_ge(max_ready, l * DSA_HEADS + h + 1)
                        for t, (a, b) in enumerate(((0, P), (P, TRI))):
                            last = act.activation(dp[:, h % 2, a:b], dp[:, h % 2, a:b], ACT.Exp,
                                                  bias=nmax[:, h % 2, t:t + 1], accum_out=psums[:, h % 2, t:t + 1])
                            last.then_inc(exp_ready, 1)
                    elif kind == "pT":
                        wait_filled(act, l, step)
                        act.activation(dp[:, h % 2, :], bank(step)[:, 0:TRI], ACT.Copy).then_inc(act_drained, 1)
                    elif kind == "sbT":
                        wait_filled(act, l, step)
                        b = bank(step)[:, :].rearrange("p (j t s) -> p j t s", j=2, t=2)
                        act.activation(cols(C_SBQ + h * P), b[:, 0], ACT.Copy, scale=SCALE)
                        act.activation(cols(C_SBK + h * P), b[:, 1], ACT.Copy).then_inc(act_drained, 1)
                    elif kind == "z":
                        wait_filled(act, l, step)
                        link(act.activation(sba[:, h, :], bank(step)[:, 0:TRI], ACT.Abs))
                        link(act.activation(sba[:, h, :], sba[:, h, :], ACT.Exp, scale=-1.0))
                        act.activation(sba[:, h, :], sba[:, h, :], ACT.Ln, bias=1.0).then_inc(ln_ready, 1)
                    elif kind == "arg":
                        wait_filled(act, l, step)
                        act.activation(sba[:, h, :], bank(step)[:, 0:TRI], ACT.Exp).then_inc(act_drained, 1)
                    elif kind == "gn":
                        act.wait_ge(chunk_out, l * len(CHUNKS) + 11)
                        act.wait_ge(rot_ready, l + 1)
                        act.activation(sig_g, pr[:, :, C_RG:C_RG + RET_HEADS * P], ACT.Exp,
                                       scale=-1.0).then_inc(gexp_ready, 1)
                        root(N_RET, TILES * RET_HEADS)

                act.wait_ge(dve_drained, (l + 1) * DRAINS["dve"])
                act.wait_ge(filled, (l + 1) * len(FILLS))
                act.dma_start(ln_g, ln1_g[bass.ds(l, 1)].broadcast_to([P, D_MODEL])).then_inc(lnp_in, 16)
                act.dma_start(ln_b, ln1_b[bass.ds(l, 1)].broadcast_to([P, D_MODEL])).then_inc(lnp_in, 16)
                root(N_LN1, TILES)
                copy_xT(1)
                act.dma_start(ln_g, ln2_g[bass.ds(l, 1)].broadcast_to([P, D_MODEL])).then_inc(lnp_in, 16)
                act.dma_start(ln_b, ln2_b[bass.ds(l, 1)].broadcast_to([P, D_MODEL])).then_inc(lnp_in, 16)
                act.wait_ge(rmax_ready, l + 1)
                act.activation(rt[:, 1], rt[:, 0], ACT.Exp).then_inc(rexp_ready, 1)


                def copy_window(e, par):
                    for f in range(4):
                        act.wait_ge(xw_filled, (l * N_EXPERTS + e) * 4 + (f + 5))
                        act.activation(xT[:, 4 * f:4 * f + 4, par * P:(par + 1) * P],
                                       pb[3][:, :].rearrange("p (k s) -> p k s", k=4), ACT.Copy).then_inc(xw_copied, 1)

                def front(e, par, u, pair, more=True):
                    if more:
                        copy_window(e + 1, 1 - par)
                    n = l * N_EXPERTS + e
                    act.wait_ge(slots_free, l * LAYER_UNITS + pair * PAIR_UNITS + (RING + u + CHUNK_UNITS))
                    act.wait_ge(hT_filled, n + 1)
                    act.activation(sg[par], pp[2 * par][:, :], ACT.Exp, scale=-1.0).then_inc(gate_exp, 1)

                def back(e, par):
                    act.wait_ge(hT_filled, l * N_EXPERTS + e + 3)
                    act.activation(hT[par], pb[0][:, :], ACT.Copy).then_inc(hT_ready, 1)

                copy_window(0, 0)
                front(0, 0, FRONT_0, 0)
                with act.Fori(0, PAIRS) as pair:
                    back(pair * 2, 0)
                    front(pair * 2 + 1, 1, FRONT_ODD, pair)
                    back(pair * 2 + 1, 1)
                    front(pair * 2 + 2, 0, FRONT_EVEN, pair)
                back(N_EXPERTS - 2, 0)
                front(N_EXPERTS - 1, 1, FRONT_ODD + LAST, 0, more=False)
                back(N_EXPERTS - 1, 1)

                wait_apart(act, routed, l + 1)
                most = most_tokens(act)
                with act.If(most > SLOTS):
                    with act.Fori(0, N_EXPERTS) as e:
                        n = tokens(act, e)
                        with act.If(n > SLOTS):
                            m = overs_before(act, e)
                            for f in range(4):
                                act.wait_ge(over_pe, m * OVER_PE + (f + 1))
                                act.activation(xT[:, 4 * f:4 * f + 4, 0:P],
                                               pb[3][:, :].rearrange("p (k s) -> p k s", k=4),
                                               ACT.Copy).then_inc(over_act, 1)
                            act.wait_ge(over_pe, m * OVER_PE + 5)
                            act.activation(sg[0], pp[0][:, :], ACT.Exp, scale=-1.0).then_inc(over_act, 1)
                            act.wait_ge(over_pe, m * OVER_PE + 6)
                            act.activation(hT[0], pb[0][:, :], ACT.Copy).then_inc(over_act, 1)
                root(N_LN2, TILES)
            assert links[0] == ACT_LINKS, links

        @block.tensor
        def _(pe):
            pe.sem_inc(slots_free, RING)
            pe.sem_inc(hT_filled, 2)
            pe.sem_inc(xw_filled, 4)
            pe.wait_ge(consts_in, 32)
            pe.wait_ge(x_in, 16)
            mm = pe.matmul
            with pe.Fori(0, DEPTH) as l:
                def transpose_x(i):
                    for f in range(XT_FILLS):
                        t, k = f // (KT // 4), f % (KT // 4) * 4
                        if f >= BANKS:
                            pe.wait_ge(xt_copied, l * (2 * XT_FILLS) + (i * XT_FILLS + f - BANKS + 1))
                        for j in range(4):
                            last = pe.transpose(pb[f % BANKS][:, j * P:(j + 1) * P],
                                                xs[:, t, (k + j) * P:(k + j + 1) * P], ident)
                        last.then_inc(xt_filled, 1)

                def rows(src, w, banks, first_unit, n_units):
                    for q in range(n_units):
                        slot = (first_unit + q) % RING
                        pe.wait_ge(unit_in[slot], l * (16 * LAYER_TURNS) + 16 * ((first_unit + q) // RING + 1))
                        for t in range(TILES):
                            for kk in range(KU):
                                k = q * KU + kk
                                last = mm(banks[t][:, 0:w], src[:, k, t * P:(t + 1) * P], ring[:, slot, kk, 0:w],
                                          start=(k == 0), stop=(k == KT - 1))
                        last.then_inc(slots_free, 1)

                pe.wait_ge(x_ready, l * 4 + 1)
                transpose_x(0)
                pe.wait_ge(xt_copied, l * (2 * XT_FILLS) + XT_FILLS)

                for kind, h in STEPS:
                    step = (kind, h)
                    if kind in DRAIN:
                        f = FILL_AT[step]
                        wait_drained(pe, l, *FILLS[max(f - BANKS, 0):max(f - BANKS + 1, 0)], *reads(kind, h))
                        b = bank(step)
                    if kind == "proj":
                        c, q = h // CHUNK_UNITS, h % CHUNK_UNITS
                        w = width(CHUNKS[c])
                        if q == 0 and c >= 2:
                            pe.wait_ge(chunk_out, l * len(CHUNKS) + c - 1)
                        slot = h % RING
                        pe.wait_ge(unit_in[slot], l * (16 * LAYER_TURNS) + 16 * (h // RING + 1))
                        for t in range(TILES):
                            for kk in range(KU):
                                k = q * KU + kk
                                last = mm(pp[2 * (c % 2) + t][:, 0:w], xT[:, k, t * P:(t + 1) * P],
                                          ring[:, slot, kk, 0:w], start=(k == 0), stop=(k == KT - 1))
                        last.then_inc(slots_free, 1)
                    elif kind == "qiT":
                        pe.wait_ge(chunk_out, l * len(CHUNKS) + 2)
                        for j in range(4):
                            last = pe.transpose(b[:, j * P:(j + 1) * P], col(C_QI + (2 * h + j // 2) * P, j % 2), ident)
                        last.then_inc(filled, 1)
                    elif kind == "ckvT":
                        pe.wait_ge(ckvn_ready, l + 1)
                        for j in range(4):
                            last = pe.transpose(b[:, j * P:(j + 1) * P], col(C_CKV + (j // 2) * P, j % 2), ident)
                        last.then_inc(filled, 1)
                    elif kind == "kiT":
                        for t in range(TILES):
                            last = pe.transpose(b[:, t * P:(t + 1) * P], dkv[:, 0, t * P:(t + 1) * P], ident)
                        last.then_inc(filled, 1)
                    elif kind == "idx":
                        r = slice(IDX_DIM * (h % 2), IDX_DIM * (h % 2) + IDX_DIM)
                        c = C_QI + (h // 2) * P
                        mm(b[:, 0:P], pr[r, 0, c:c + P], dkv[r, 1, 0:P], start=True, stop=True)
                        mm(b[:, P:TRI], pr[r, 1, c:c + P], dkv[r, 1, 0:SEQ], start=True, stop=True).then_inc(filled, 1)
                    elif kind == "kv":
                        pe.wait_ge(layer_in, l * 48 + 48)
                        c = h * 2 * P
                        for r in range(2):
                            mm(b[:, 0:SEQ], kvup[:, r, c:c + P], kvn(r), start=(r == 0), stop=(r == 1))
                        for t in range(TILES):
                            for r in range(2):
                                last = mm(b[:, (2 + t) * P:(3 + t) * P], kvn(r)[:, t, :], kvup[:, r, c + P:c + 2 * P],
                                          start=(r == 0), stop=(r == 1))
                        last.then_inc(filled, 1)
                    elif kind == "dqT":
                        pe.wait_ge(chunk_out, l * len(CHUNKS) + 4)
                        for t in range(TILES):
                            last = pe.transpose(b[:, t * P:(t + 1) * P], col(C_DQ + h * P, t), ident)
                        last.then_inc(filled, 1)
                    elif kind == "log":
                        q = cols(C_DQ + h * P)
                        mm(b[:, 0:P], q[:, 0, :], dkv[:, h % 2, 0:P], start=True, stop=True)
                        mm(b[:, P:TRI], q[:, 1, :], dkv[:, h % 2, 0:SEQ], start=True, stop=True).then_inc(filled, 1)
                    elif kind == "pT":
                        pe.wait_ge(p_ready, l * DSA_HEADS + h + 1)
                        for j in range(3):
                            last = pe.transpose(b[:, j * P:(j + 1) * P], dp[:, h % 2, j * P:(j + 1) * P], ident)
                        last.then_inc(filled, 1)
                    elif kind == "out":
                        mm(b[:, 0:P], dkv[:, h % 2, 2 * P:3 * P], dp[:, h % 2, 0:P], start=True, stop=True)
                        mm(b[:, P:SEQ], dkv[:, h % 2, 2 * P:3 * P], dp[:, h % 2, P:SEQ], start=True, stop=False)
                        mm(b[:, P:SEQ], dkv[:, h % 2, 3 * P:4 * P], dp[:, h % 2, SEQ:TRI],
                           start=False, stop=True).then_inc(filled, 1)
                    elif kind in ("sbT", "rT"):
                        if kind == "sbT":
                            pe.wait_ge(chunk_out, l * len(CHUNKS) + 7)
                            cq, ck = C_SBQ + h * P, C_SBK + h * P
                        else:
                            pe.wait_ge(rot_ready, l + 1)
                            cq, ck = C_RQ + h * P, C_RK + h * P
                        for j in range(4):
                            last = pe.transpose(b[:, j * P:(j + 1) * P], col((cq, ck)[j // 2], j % 2), ident)
                        last.then_inc(filled, 1)
                    elif kind in ("z", "arg", "rs"):
                        cq, ck = (C_RQ + h * P, C_RK + h * P) if kind == "rs" else (C_SBQ + h * P, C_SBK + h * P)
                        if kind == "arg":
                            pe.wait_ge(sp_ready, l * SB_HEADS + h + 1)
                        for at, j, i in ((0, 0, 0), (P, 0, 1), (SEQ, 1, 1)):
                            o = b[:, at:at + P]
                            last = mm(o, cols(ck)[:, j, :], cols(cq)[:, i, :], start=True, stop=(kind != "arg"))
                            if kind == "arg":
                                mm(o, tab[:, T_SUM:T_SUM + P], sba[:, h, at:at + P], start=False, stop=False)
                                if i == j:
                                    last = mm(o, ident, tab[:, T_NSTRICT:T_NSTRICT + P], start=False, stop=True)
                                else:
                                    last = mm(o, tab[:, T_NONE:T_NONE + P], sba[:, h, SEQ:TRI], start=False, stop=True)
                        last.then_inc(filled, 1)
                    elif kind == "sbo":
                        pe.wait_ge(chunk_out, l * len(CHUNKS) + (12 if h < 4 else 10))
                        mm(b[:, 0:P], col(C_SBV + h * P, 0), sba[:, h, 0:P], start=True, stop=True)
                        mm(b[:, P:SEQ], col(C_SBV + h * P, 0), sba[:, h, P:SEQ], start=True, stop=False)
                        mm(b[:, P:SEQ], col(C_SBV + h * P, 1), sba[:, h, SEQ:TRI], start=False,
                           stop=True).then_inc(filled, 1)
                    elif kind == "ro":
                        pe.wait_ge(chunk_out, l * len(CHUNKS) + 11)
                        a = ra[:, h, :]
                        mm(b[:, 0:P], a[:, 0:P], col(C_RV + h * P, 0), start=True, stop=True)
                        mm(b[:, P:SEQ], a[:, P:SEQ], col(C_RV + h * P, 0), start=True, stop=False)
                        mm(b[:, P:SEQ], a[:, SEQ:TRI], col(C_RV + h * P, 1), start=False,
                           stop=True).then_inc(filled, 1)
                    elif kind == "ryT":
                        pe.wait_ge(gn_ready, l + 1)
                        for j in range(4):
                            last = pe.transpose(b[:, j * P:(j + 1) * P],
                                                ro[:, j % 2, (2 * h + j // 2) * P:(2 * h + j // 2 + 1) * P], ident)
                        last.then_inc(filled, 1)

                pe.wait_ge(dve_drained, (l + 1) * DRAINS["dve"])
                for n in range(WO_CHUNKS):
                    if n >= 2:
                        pe.wait_ge(mix_added, l * WO_CHUNKS + n - 1)
                    rows(yT, NW, [pp[2 * (n % 2)], pp[2 * (n % 2) + 1]], IN_UNITS + n * CHUNK_UNITS, CHUNK_UNITS)
                pe.wait_ge(x_ready, l * 4 + 3)
                transpose_x(1)
                pe.wait_ge(xt_copied, (l + 1) * (2 * XT_FILLS))
                for t in range(TILES):
                    for k in range(KT):
                        last = mm(pb[1][:, t * N_EXPERTS:(t + 1) * N_EXPERTS], xT[:, k, t * P:(t + 1) * P], wr[:, k, :],
                                  start=(k == 0), stop=(k == KT - 1))
                last.then_inc(route_filled, 1)

                pe.wait_ge(chosen, l + 1)
                b = pb[2]
                mm(b[:, 0:N_EXPERTS], tab[:, T_STRICT:T_STRICT + P], rt[:, 2, 0, :], start=True, stop=True)
                mm(b[:, N_EXPERTS:2 * N_EXPERTS], tab[:, T_STRICT:T_STRICT + P], rt[:, 2, 1, :], start=True, stop=True)
                mm(b[:, 2 * N_EXPERTS:3 * N_EXPERTS], tab[:, T_NONE:T_NONE + P], rt[:, 2, 0, :], start=True, stop=True)
                for t in range(TILES):
                    last = mm(b[:, 3 * N_EXPERTS:4 * N_EXPERTS], tab[:, T_NONE:T_NONE + P], rt[:, 2, t, :],
                              start=(t == 0), stop=(t == TILES - 1))
                last.then_inc(counted, 1)

                def window_part(e, par, f):
                    n = l * N_EXPERTS + e
                    if f == 0:
                        pe.wait_ge(xg_in[par], landed(e, par))
                    pe.wait_ge(xw_copied, n * 4 + (f + 1))
                    for j in range(4):
                        k = 4 * f + j
                        last = pe.transpose(pb[3][:, j * P:(j + 1) * P], xg[par][:, k * P:(k + 1) * P], ident)
                    last.then_inc(xw_filled, 1)

                def landed(e, par):
                    return l * (16 * N_EXPERTS // 2) + (e - par) * 8 + 16

                def wait_unit(u, pair):
                    pe.wait_ge(unit_in[u % RING], l * (16 * LAYER_TURNS) + pair * (16 * PAIR_UNITS // RING)
                               + 16 * (u // RING + 1))

                def front(e, par, u, pair, more=True):
                    n = l * N_EXPERTS + e
                    pe.wait_ge(xw_copied, n * 4 + 5)
                    pe.wait_ge(h_ready, n + 1)
                    for w in range(2):
                        for q in range(CHUNK_UNITS):
                            wait_unit(u, pair)
                            for kk in range(KU):
                                k = q * KU + kk
                                last = mm(pp[2 * par + w][:, :], xT[:, k, par * P:(par + 1) * P],
                                          ring[:, u % RING, kk, :], start=(k == 0), stop=(k == KT - 1))
                            last.then_inc(slots_free, 1)
                            u += 1
                            if w == 0 and more:
                                window_part(e + 1, 1 - par, q)

                def turn(e, par):
                    n = l * N_EXPERTS + e
                    pe.wait_ge(h_ready, n + 3)
                    pe.wait_ge(hT_ready, n + 1)
                    for k in range(4):
                        last = pe.transpose(pb[0][:, k * P:(k + 1) * P], sg[par][:, k * P:(k + 1) * P], ident)
                    last.then_inc(hT_filled, 1)

                def back(e, par, u, pair):
                    n = l * N_EXPERTS + e
                    pe.wait_ge(hT_ready, n + 2)
                    for c in range(WO_CHUNKS):
                        pe.wait_ge(y_copied, n * 4 + (c + 1))
                        wait_unit(u + c, pair)
                        for k in range(KU):
                            last = mm(pb[1 + c % 2][:, :], hT[par][:, k * P:(k + 1) * P],
                                      ring[:, (u + c) % RING, k, :], start=(k == 0), stop=(k == KU - 1))
                        last.then_inc(slots_free, 1)

                for f in range(4):
                    window_part(0, 0, f)
                front(0, 0, FRONT_0, 0)
                with pe.Fori(0, PAIRS) as pair:
                    turn(pair * 2, 0)
                    front(pair * 2 + 1, 1, FRONT_ODD, pair)
                    back(pair * 2, 0, BACK_EVEN, pair)
                    turn(pair * 2 + 1, 1)
                    front(pair * 2 + 2, 0, FRONT_EVEN, pair)
                    back(pair * 2 + 1, 1, BACK_ODD, pair)
                turn(N_EXPERTS - 2, 0)
                front(N_EXPERTS - 1, 1, FRONT_ODD + LAST, 0, more=False)
                back(N_EXPERTS - 2, 0, BACK_EVEN + LAST, 0)
                turn(N_EXPERTS - 1, 1)
                back(N_EXPERTS - 1, 1, BACK_LAST, 0)

                wait_apart(pe, routed, l + 1)
                most = most_tokens(pe)
                with pe.If(most > SLOTS):
                    with pe.Fori(0, N_EXPERTS) as e:
                        many = tokens(pe, e)
                        with pe.If(many > SLOTS):
                            m = overs_before(pe, e)
                            pe.wait_ge(over_x, m * OVER_X + 32)
                            for f in range(4):
                                if f:
                                    pe.wait_ge(over_act, m * OVER_ACT + f)
                                for j in range(4):
                                    k = 4 * f + j
                                    last = pe.transpose(pb[3][:, j * P:(j + 1) * P], xg[0][:, k * P:(k + 1) * P], ident)
                                last.then_inc(over_pe, 1)
                            pe.wait_ge(over_act, m * OVER_ACT + 4)
                            pe.wait_ge(over_w, m * OVER_W + 16 * 2 * CHUNK_UNITS)
                            for w in range(2):
                                for k in range(KT):
                                    last = mm(pp[w][:, :], xT[:, k, 0:P], ring[:, w * CHUNK_UNITS + k // KU, k % KU, :],
                                              start=(k == 0), stop=(k == KT - 1))
                            last.then_inc(over_pe, 1)
                            pe.wait_ge(over_dve, m * OVER_DVE + 1)
                            for k in range(4):
                                last = pe.transpose(pb[0][:, k * P:(k + 1) * P], sg[0][:, k * P:(k + 1) * P], ident)
                            last.then_inc(over_pe, 1)
                            pe.wait_ge(over_act, (m + 1) * OVER_ACT)
                            pe.wait_ge(over_w, (m + 1) * OVER_W)
                            for c in range(4):
                                if c >= 2:
                                    pe.wait_ge(over_dve, m * OVER_DVE + c)
                                for k in range(4):
                                    wd = ring[:, k, :, :].rearrange("p k n -> p (k n)")
                                    last = mm(pb[1 + c % 2][:, :], hT[0][:, k * P:(k + 1) * P],
                                              wd[:, c * NW:(c + 1) * NW], start=(k == 0), stop=(k == 3))
                                last.then_inc(over_pe, 1)

        @block.vector
        def _(dve):
            links = [0]
            dve.wait_ge(consts_in, 32)
            dve.wait_ge(x_in, 16)
            dve.sem_inc(h_ready, 2)
            dve.memset(overs[:, :], 0.0)
            dve.sem_inc(y_copied, 2)
            dve.sem_inc(x_ready, 1)
            with dve.Fori(0, DEPTH) as l:
                def link(ins, alone=False):
                    links[0] += 1
                    ins.then_inc(dve_link, 1)
                    if alone:
                        wait_apart(dve, dve_link, l * DVE_LINKS + links[0])
                    else:
                        dve.wait_ge(dve_link, l * DVE_LINKS + links[0])

                def root(which, n, variance, eps):
                    dve.tensor_scalar(var[:, 0:n], variance, eps, None, ALU.add).then_inc(var_ready, 1)
                    dve.wait_ge(root_ready, l * NORMS + which + 1)
                    link(dve.tensor_tensor(nt[:, 0:n], rstd[:, 0:n], rstd[:, 0:n], ALU.mult))
                    link(dve.tensor_tensor(nt[:, 0:n], nt[:, 0:n], var[:, 0:n], ALU.mult))
                    link(dve.tensor_scalar(nt[:, 0:n], nt[:, 0:n], -0.5, 1.5, ALU.mult, ALU.add))
                    link(dve.tensor_tensor(rstd[:, 0:n], rstd[:, 0:n], nt[:, 0:n], ALU.mult))

                def layer_norm(which, i):
                    for t in range(TILES):
                        link(dve.bn_aggr(mv[:, t, :], st[:, t, :, :].rearrange("p a b -> p (a b)")), alone=True)
                    root(which, TILES, mv[:, 0:TILES, 1], LN_EPS)
                    dve.wait_ge(lnp_in, l * 64 + 32 * (i + 1))
                    for t in range(TILES):
                        link(dve.tensor_scalar(xs[:, t, :], xs[:, t, :], mv[:, t, 0:1], rstd[:, t:t + 1],
                                               ALU.subtract, ALU.mult))
                        link(dve.tensor_tensor(xs[:, t, :], xs[:, t, :], ln_g, ALU.mult))
                        dve.tensor_tensor(xs[:, t, :], xs[:, t, :], ln_b, ALU.add).then_inc(x_ready, 1)

                for kind, h in STEPS:
                    step = (kind, h)
                    if kind == "ckvn":
                        dve.wait_ge(chunk_out, l * len(CHUNKS) + 2)
                        for t in range(TILES):
                            for j in range(2):
                                link(dve.tensor_copy(dkv[:, 0, t * P + j * IDX_DIM:t * P + (j + 1) * IDX_DIM],
                                                     col(C_KI, t, IDX_DIM)))
                        for t in range(TILES):
                            link(dve.bn_stats(st[:, t, 0, :], col(C_CKV, t, KV_RANK)), alone=True)
                            link(dve.bn_aggr(mv[:, t, :], st[:, t, 0, :]))
                        link(dve.tensor_tensor(nt[:, 0:TILES], mv[:, 0:TILES, 0], mv[:, 0:TILES, 0], ALU.mult))
                        link(dve.tensor_tensor(nt[:, 0:TILES], nt[:, 0:TILES], mv[:, 0:TILES, 1], ALU.add))
                        root(N_CKV, TILES, nt[:, 0:TILES], RMS_EPS)
                        dve.tensor_scalar(col(C_CKV, 0, KV_RANK), col(C_CKV, 0, KV_RANK), rstd[:, 0:1], None, ALU.mult)
                        dve.tensor_scalar(col(C_CKV, 1, KV_RANK), col(C_CKV, 1, KV_RANK), rstd[:, 1:2], None,
                                          ALU.mult).then_inc(ckvn_ready, 1)
                    elif kind == "ckvT":
                        wait_filled(dve, l, step)
                        dve.wait_ge(layer_in, l * 48 + 48)
                        for r in range(2):
                            last = dve.tensor_scalar(kvn(r), bank(step)[:, r * SEQ:(r + 1) * SEQ].rearrange(
                                "p (t s) -> p t s", t=2), kvg_col[:, r:r + 1], None, ALU.mult)
                        last.then_inc(dve_drained, 1)
                    elif kind == "idx":
                        wait_drained(dve, l, step)
                        for t, (a, b) in enumerate(((0, P), (P, TRI))):
                            w = col(C_W + h, t, 1)
                            if h == 0:
                                last = dve.tensor_scalar(score[:, a:b], rel[h % 2][:, a:b], w, None, ALU.mult)
                            else:
                                last = dve.scalar_tensor_tensor(score[:, a:b], rel[h % 2][:, a:b], w, score[:, a:b],
                                                                ALU.mult, ALU.add)
                        last.then_inc(rel_used, 1)
                        dve.wait_ge(rel_used, l * IDX_HEADS + h + 1)
                    elif kind == "topk":
                        link(dve.tensor_scalar(work, score, IDX_SCALE, None, ALU.mult))
                        diag = work.rearrange("p (b j) -> p b j", b=3)[:, 0:3:2, :]
                        link(dve.tensor_tensor(diag, diag,
                                               tab[:, T_CAUSAL:T_CAUSAL + P].unsqueeze(1).broadcast_to([P, 2, P]),
                                               ALU.add), alone=True)
                        for a, b in ((0, P), (P, TRI)):
                            for _ in range(TOPK // 8):
                                link(dve.max(top8[:, :], work[:, a:b]), alone=True)
                                link(dve.match_replace(work[:, a:b], top8[:, :], work[:, a:b], TAKEN), alone=True)
                        link(dve.tensor_scalar(sel[:, :], work, 0.5 * TAKEN, NEG, ALU.is_gt, ALU.mult))
                        diag = sel[:, :].rearrange("p (b j) -> p b j", b=3)[:, 0:3:2, :]
                        link(dve.tensor_tensor(diag, diag,
                                               tab[:, T_CAUSAL:T_CAUSAL + P].unsqueeze(1).broadcast_to([P, 2, P]),
                                               ALU.min))
                    elif kind == "dqT":
                        wait_filled(dve, l, step)
                        dve.tensor_copy(cols(C_DQ + h * P), bank(step)[:, 0:SEQ].rearrange(
                            "p (t s) -> p t s", t=2)).then_inc(dve_drained, 1)
                    elif kind == "log":
                        wait_filled(dve, l, step)
                        dve.scalar_tensor_tensor(dp[:, h % 2, :], bank(step)[:, 0:TRI], SCALE, sel[:, :],
                                                 ALU.mult, ALU.add).then_inc(dve_drained, 1)
                        wait_drained(dve, l, step)
                        for t, (a, b) in enumerate(((0, P), (P, TRI))):
                            link(dve.tensor_reduce(nmax[:, h % 2, t:t + 1], dp[:, h % 2, a:b], AX_X, ALU.max))
                        dve.tensor_scalar(nmax[:, h % 2, :], nmax[:, h % 2, :], -1.0, None,
                                          ALU.mult).then_inc(max_ready, 1)
                        dve.wait_ge(exp_ready, l * (2 * DSA_HEADS) + 2 * (h + 1))
                        link(dve.reciprocal(psums[:, h % 2, :], psums[:, h % 2, :]))
                        dve.tensor_scalar(dp[:, h % 2, 0:P], dp[:, h % 2, 0:P], psums[:, h % 2, 0:1], None, ALU.mult)
                        dve.tensor_scalar(dp[:, h % 2, P:TRI], dp[:, h % 2, P:TRI], psums[:, h % 2, 1:2], None,
                                          ALU.mult).then_inc(p_ready, 1)
                    elif kind in ("out", "sbo"):
                        wait_filled(dve, l, step)
                        m = h if kind == "sbo" else SB_HEADS + RET_HEADS + h
                        dve.tensor_copy(yT[:, m, :], bank(step)[:, 0:SEQ]).then_inc(dve_drained, 1)
                    elif kind == "z":
                        dve.wait_ge(ln_ready, l * SB_HEADS + h + 1)
                        dve.scalar_tensor_tensor(sba[:, h, :], bank(step)[:, 0:TRI], 0.0, sba[:, h, :],
                                                 ALU.max, ALU.add).then_inc(dve_drained, 1)
                        wait_drained(dve, l, step)
                        diag = sba[:, h, :].rearrange("p (b j) -> p b j", b=3)[:, 0:3:2, :]
                        dve.tensor_tensor(diag, diag,
                                          tab[:, T_STRICT:T_STRICT + P].unsqueeze(1).broadcast_to([P, 2, P]),
                                          ALU.mult).then_inc(sp_ready, 1)
                    elif kind == "rT":
                        wait_filled(dve, l, step)
                        b = bank(step)[:, :].rearrange("p (j t s) -> p j t s", j=2, t=2)
                        dve.tensor_copy(cols(C_RQ + h * P), b[:, 0])
                        dve.tensor_copy(cols(C_RK + h * P), b[:, 1]).then_inc(dve_drained, 1)
                    elif kind == "rs":
                        wait_filled(dve, l, step)
                        dve.tensor_tensor(ra[:, h, :], bank(step)[:, 0:TRI],
                                          tab[:, T_DECAY + h * TRI:T_DECAY + (h + 1) * TRI],
                                          ALU.mult).then_inc(dve_drained, 1)
                    elif kind == "ro":
                        wait_filled(dve, l, step)
                        dve.tensor_copy(ro[:, :, h * P:(h + 1) * P],
                                        bank(step)[:, 0:SEQ].rearrange("p (t d) -> p t d", t=2)).then_inc(dve_drained, 1)
                    elif kind == "gn":
                        wait_drained(dve, l, ("ro", RET_HEADS - 1))
                        for t in range(TILES):
                            for i in range(RET_HEADS):
                                last = dve.bn_stats(st[:, t, i, :], ro[:, t, i * P:(i + 1) * P])
                        link(last, alone=True)
                        for i in range(TILES * RET_HEADS):
                            last = dve.bn_aggr(mv[:, i, :], st[:, i // RET_HEADS, i % RET_HEADS, :])
                        link(last)
                        dve.wait_ge(gexp_ready, l + 1)
                        g = sig_g
                        link(dve.tensor_scalar(g, g, 1.0, None, ALU.add))
                        link(dve.reciprocal(g, g))
                        link(dve.tensor_tensor(g, g, pr[:, :, C_RG:C_RG + RET_HEADS * P], ALU.mult))
                        root(N_RET, TILES * RET_HEADS, mv[:, :, 1], GN_EPS)
                        for i in range(TILES * RET_HEADS):
                            t, k = i // RET_HEADS, i % RET_HEADS
                            v = ro[:, t, k * P:(k + 1) * P]
                            last = dve.tensor_scalar(v, v, mv[:, i, 0:1], rstd[:, i:i + 1], ALU.subtract, ALU.mult)
                        link(last)
                        dve.tensor_tensor(ro, ro, g, ALU.mult).then_inc(gn_ready, 1)
                    elif kind == "ryT":
                        wait_filled(dve, l, step)
                        for j in range(2):
                            last = dve.tensor_scalar(yT[:, SB_HEADS + 2 * h + j, :], bank(step)[:, j * SEQ:(j + 1) * SEQ],
                                                     gn_col[:, 2 * h + j:2 * h + j + 1], None, ALU.mult)
                        last.then_inc(dve_drained, 1)

                for n in range(WO_CHUNKS):
                    dve.wait_ge(slots_free, freed(l, IN_UNITS + (n + 1) * CHUNK_UNITS - 1))
                    for t in range(TILES):
                        v = xs[:, t, n * NW:(n + 1) * NW]
                        last = dve.scalar_tensor_tensor(v, v, ALPHA, pp[2 * (n % 2) + t][:, :], ALU.mult, ALU.add)
                    last.then_inc(mix_added, 1)
                    dve.wait_ge(mix_added, l * WO_CHUNKS + n + 1)
                    for t in range(TILES):
                        link(dve.bn_stats(st[:, t, n, :], xs[:, t, n * NW:(n + 1) * NW]), alone=True)
                layer_norm(N_LN1, 0)

                dve.wait_ge(route_filled, l + 1)
                lg, pe_, c1, c2, c3, gr, m1, m2 = (rt[:, i] for i in range(8))
                link(dve.tensor_copy(lg, pb[1][:, 0:TILES * N_EXPERTS].rearrange("p (t e) -> p t e", t=TILES)))
                link(dve.tensor_reduce(nt[:, 0:TILES], lg, AX_X, ALU.max))
                dve.tensor_tensor(lg, lg, nt[:, 0:TILES].unsqueeze(2).broadcast_to([P, TILES, N_EXPERTS]),
                                  ALU.subtract).then_inc(rmax_ready, 1)
                dve.wait_ge(rexp_ready, l + 1)
                link(dve.tensor_reduce(nt[:, 0:TILES], pe_, AX_X, ALU.add))
                link(dve.reciprocal(nt[:, 0:TILES], nt[:, 0:TILES]))
                link(dve.tensor_tensor(pe_, pe_, nt[:, 0:TILES].unsqueeze(2).broadcast_to([P, TILES, N_EXPERTS]),
                                       ALU.mult))
                pg = pe_.rearrange("p t (g e) -> p t g e", g=N_GROUPS)

                def part(v, i):
                    return v[:, :, i * N_GROUPS:(i + 1) * N_GROUPS]

                link(dve.tensor_tensor(part(c1, 0), pg[:, :, :, 0], pg[:, :, :, 1], ALU.max))
                link(dve.tensor_tensor(part(c1, 1), pg[:, :, :, 0], pg[:, :, :, 1], ALU.min))
                link(dve.tensor_tensor(part(c1, 2), pg[:, :, :, 2], pg[:, :, :, 3], ALU.max))
                link(dve.tensor_tensor(part(c1, 3), pg[:, :, :, 2], pg[:, :, :, 3], ALU.min))
                link(dve.tensor_tensor(part(c2, 0), part(c1, 0), part(c1, 2), ALU.max))
                link(dve.tensor_tensor(part(c2, 1), part(c1, 0), part(c1, 2), ALU.min))
                link(dve.tensor_tensor(part(c2, 2), part(c1, 1), part(c1, 3), ALU.max))
                link(dve.tensor_tensor(part(c2, 1), part(c2, 1), part(c2, 2), ALU.max))
                link(dve.tensor_tensor(part(c2, 0), part(c2, 0), part(c2, 1), ALU.add))
                gs = part(c2, 0)
                rank = tab[:, T_RANK:T_RANK + N_EXPERTS].unsqueeze(1).broadcast_to([P, TILES, N_EXPERTS])
                grank = tab[:, T_RANK:T_RANK + N_GROUPS].unsqueeze(1).broadcast_to([P, TILES, N_GROUPS])

                def best(value, order, mask, n, tmp):
                    def over(v):
                        return v.unsqueeze(2).broadcast_to([P, TILES, n])
                    link(dve.tensor_reduce(nt[:, 0:2], value, AX_X, ALU.max))
                    link(dve.tensor_tensor(mask, value, over(nt[:, 0:2]), ALU.is_equal))
                    link(dve.tensor_tensor(mask, mask, order, ALU.mult))
                    link(dve.tensor_reduce(nt[:, 2:4], mask, AX_X, ALU.max))
                    link(dve.tensor_tensor(mask, mask, over(nt[:, 2:4]), ALU.is_equal))

                best(gs, grank, part(c3, 0), N_GROUPS, c1)
                link(dve.tensor_copy(gr.rearrange("p t (g e) -> p t g e", g=N_GROUPS),
                                     part(c3, 0).unsqueeze(3).broadcast_to([P, TILES, N_GROUPS, PER_GROUP])))
                link(dve.tensor_tensor(c1, pe_, gr, ALU.mult))
                link(dve.tensor_scalar(c2, gr, 1.0, None, ALU.subtract))
                link(dve.tensor_tensor(c1, c1, c2, ALU.add))
                best(c1, rank, m1, N_EXPERTS, c3)
                link(dve.tensor_copy(nt[:, 4:6], nt[:, 0:2]))
                link(dve.tensor_scalar(c2, m1, -4.0, None, ALU.mult))
                link(dve.tensor_tensor(c1, c1, c2, ALU.add))
                best(c1, rank, m2, N_EXPERTS, c3)
                link(dve.tensor_tensor(nt[:, 2:4], nt[:, 0:2], nt[:, 4:6], ALU.add))
                link(dve.reciprocal(nt[:, 2:4], nt[:, 2:4]))
                link(dve.tensor_tensor(wts[:, 0, :], nt[:, 4:6], nt[:, 2:4], ALU.mult))
                link(dve.tensor_tensor(wts[:, 1, :], nt[:, 0:2], nt[:, 2:4], ALU.mult))
                dve.tensor_tensor(c1, m1, m2, ALU.add).then_inc(chosen, 1)

                dve.wait_ge(counted, l + 1)
                cn = rt[:, 3:5].rearrange("p i t e -> p (i t e)")

                def part16(i):
                    return cn[:, i * N_EXPERTS:(i + 1) * N_EXPERTS]

                link(dve.tensor_copy(cn, pb[2][:, 0:4 * N_EXPERTS]))
                link(dve.tensor_tensor(part16(1), part16(1), part16(2), ALU.subtract))
                link(dve.tensor_scalar(part16(3), part16(3), -1.0, None, ALU.mult))
                link(dve.memset(part16(2), 1.0))
                link(dve.tensor_tensor_scan(gr[:, 0, :], part16(2), part16(3), 0.0, ALU.mult, ALU.add))
                link(dve.tensor_tensor(gr[:, 0, :], gr[:, 0, :], part16(3), ALU.subtract))
                for t in range(TILES):
                    link(dve.tensor_tensor(part16(t), part16(t), gr[:, 0, :], ALU.add))
                places = cn[:, 0:TILES * N_EXPERTS].rearrange("p (t e) -> p t e", t=TILES)
                for c, m in enumerate((m1, m2)):
                    link(dve.tensor_tensor(m, m, places, ALU.mult))
                    link(dve.tensor_reduce(nt[:, c * TILES:(c + 1) * TILES], m, AX_X, ALU.add))
                link(dve.tensor_copy(place[:, :], nt[:, 0:2 * TILES]))
                link(dve.tensor_copy(counts[:, 0:N_EXPERTS], gr[:, 0, :]))
                link(dve.tensor_copy(counts[:, N_EXPERTS:2 * N_EXPERTS], part16(3)))
                link(dve.tensor_tensor(gr[:, 1, :], gr[:, 0, :], part16(3), ALU.add))
                link(dve.tensor_scalar(gr[:, 1, :], gr[:, 1, :], -float(SLOTS), 0.0, ALU.add, ALU.max))
                link(dve.tensor_copy(counts[:, 2 * N_EXPERTS:3 * N_EXPERTS], gr[:, 1, :]))
                link(dve.tensor_reduce(nt[:, 4:5], part16(3), AX_X, ALU.max))
                link(dve.tensor_copy(counts[:, COUNTS - 2:COUNTS - 1], nt[:, 4:5]))
                link(dve.tensor_scalar(part16(0), part16(3), float(SLOTS), None, ALU.is_gt))
                link(dve.tensor_tensor_scan(part16(1), part16(2), part16(0), overs[:, :], ALU.mult, ALU.add))
                link(dve.tensor_copy(overs[:, :], part16(1)[:, N_EXPERTS - 1:N_EXPERTS]))
                link(dve.tensor_tensor(part16(0), part16(1), part16(0), ALU.subtract))
                link(dve.tensor_copy(counts[:, 3 * N_EXPERTS:4 * N_EXPERTS], part16(0)))
                dve.tensor_copy(counts[:, COUNTS - 1:COUNTS], overs[:, :]).then_inc(routed, 1)

                dve.wait_ge(xt_filled, (l + 1) * (2 * XT_FILLS))
                dve.wait_ge(sorted_out, (l + 1) * 64)
                link(dve.tensor_scalar(xs[:, :, :], xs[:, :, :], ALPHA, None, ALU.mult))

                def front(e, par, u, pair):
                    n = l * N_EXPERTS + e
                    dve.wait_ge(gate_exp, n + 1)
                    dve.tensor_scalar(sg[par], sg[par], 1.0, None, ALU.add).then_inc(moe_link, 1)
                    dve.wait_ge(moe_link, n * 3 + 1)
                    dve.reciprocal(sg[par], sg[par]).then_inc(moe_link, 1)
                    dve.wait_ge(moe_link, n * 3 + 2)
                    dve.tensor_tensor(sg[par], sg[par], pp[2 * par][:, :], ALU.mult).then_inc(moe_link, 1)
                    dve.wait_ge(moe_link, n * 3 + 3)
                    dve.wait_ge(slots_free, l * LAYER_UNITS + pair * PAIR_UNITS + (RING + u + 2 * CHUNK_UNITS))
                    dve.tensor_tensor(sg[par], sg[par], pp[2 * par + 1][:, :], ALU.mult).then_inc(h_ready, 1)

                def back(e, par, u, pair):
                    n = l * N_EXPERTS + e
                    dve.wait_ge(y_out, n * 16 + 16)
                    for c in range(4):
                        dve.wait_ge(slots_free, l * LAYER_UNITS + pair * PAIR_UNITS + (RING + u + c + 1))
                        dve.tensor_copy(yb[par][:, c * NW:(c + 1) * NW], pb[1 + c % 2][:, :]).then_inc(y_copied, 1)

                front(0, 0, FRONT_0, 0)
                with dve.Fori(0, PAIRS) as pair:
                    front(pair * 2 + 1, 1, FRONT_ODD, pair)
                    back(pair * 2, 0, BACK_EVEN, pair)
                    front(pair * 2 + 2, 0, FRONT_EVEN, pair)
                    back(pair * 2 + 1, 1, BACK_ODD, pair)
                front(N_EXPERTS - 1, 1, FRONT_ODD + LAST, 0)
                back(N_EXPERTS - 2, 0, BACK_EVEN + LAST, 0)
                back(N_EXPERTS - 1, 1, BACK_LAST, 0)

                most = most_tokens(dve)
                with dve.If(most > SLOTS):
                    with dve.Fori(0, N_EXPERTS) as e:
                        many = tokens(dve, e)
                        with dve.If(many > SLOTS):
                            m = overs_before(dve, e)
                            dve.wait_ge(over_act, m * OVER_ACT + 5)
                            dve.tensor_scalar(sg[0], sg[0], 1.0, None, ALU.add).then_inc(over_link, 1)
                            dve.wait_ge(over_link, m * OVER_LINK + 1)
                            dve.reciprocal(sg[0], sg[0]).then_inc(over_link, 1)
                            dve.wait_ge(over_link, m * OVER_LINK + 2)
                            dve.tensor_tensor(sg[0], sg[0], pp[0][:, :], ALU.mult).then_inc(over_link, 1)
                            dve.wait_ge(over_link, m * OVER_LINK + 3)
                            dve.tensor_tensor(sg[0], sg[0], pp[1][:, :], ALU.mult).then_inc(over_dve, 1)
                            for c in range(4):
                                dve.wait_ge(over_pe, m * OVER_PE + (c + 7))
                                dve.tensor_copy(yb[0][:, c * NW:(c + 1) * NW], pb[1 + c % 2][:, :]).then_inc(over_dve, 1)

                for t in range(TILES):
                    for c in range(2):
                        dve.wait_ge(back_in[2 * t + c], (l + 1) * 16)
                        link(dve.scalar_tensor_tensor(xs[:, t, :], (xg, yb)[t][c], wts[:, c, t:t + 1], xs[:, t, :],
                                                      ALU.mult, ALU.add))
                for t in range(TILES):
                    for n in range(WO_CHUNKS):
                        link(dve.bn_stats(st[:, t, n, :], xs[:, t, n * NW:(n + 1) * NW]), alone=True)
                layer_norm(N_LN2, 1)
            assert links[0] == DVE_LINKS, links


def constants():
    import numpy as np
    f = np.float32
    tab = np.zeros((P, T_COLS), f)
    p, i = np.arange(P)[:, None], np.arange(P)[None, :]
    tab[:, T_ID:T_ID + P] = p == i
    tab[:, T_SUM:T_SUM + P] = np.where(p >= i, f(-1), f(0))
    tab[:, T_NONE:T_NONE + P] = -1
    tab[:, T_STRICT:T_STRICT + P] = p < i
    tab[:, T_NSTRICT:T_NSTRICT + P] = np.where(p >= i, f(NEG), f(0))
    tab[:, T_CAUSAL:T_CAUSAL + P] = np.where(i > p, f(NEG), f(0))
    for h in range(RET_HEADS):
        log_gamma = np.log1p(-(2.0 ** (-5.0 - h)))
        for at, key, query in ((0, p, np.arange(SEQ)[None, :]), (SEQ, p + P, i + P)):
            d = query - key
            v = np.where(d >= 0, np.exp(np.maximum(d, 0) * log_gamma) * SCALE, 0.0)
            first = T_DECAY + h * TRI + at
            tab[:, first:first + v.shape[1]] = v
    theta = f(10000.0) ** (-np.linspace(0.0, 1.0, HEAD_DIM // 2, dtype=f))
    for t in range(TILES):
        ang = (np.arange(P, dtype=f) + f(t * P))[:, None] * theta[None, :]
        tab[:, T_COS + t * P:T_COS + (t + 1) * P] = np.concatenate([np.cos(ang)] * 2, 1)
        tab[:, T_SIN + t * P:T_SIN + (t + 1) * P] = np.concatenate([-np.sin(ang), np.sin(ang)], 1)
    tab[:, T_RANK:T_RANK + N_EXPERTS] = np.arange(N_EXPERTS, 0, -1)
    return tab


INPUTS = ["x", "w_in", "w_kv_up", "kv_norm_g", "ret_gn_g", "w_o", "ln1_g", "ln1_b", "w_router",
          "w_gate", "w_up", "w_down", "ln2_g", "ln2_b"]


def kernel(**inputs):
    import numpy as np
    import concourse.bacc as bacc
    from concourse.bass_utils import run_bass_kernel_spmd

    nc = bacc.Bacc("TRN2", target_bir_lowering=False, num_devices=1)
    arrays, args = {}, {}
    for name in INPUTS + ["tables"]:
        a = constants() if name == "tables" else np.ascontiguousarray(inputs[name])
        if name in ("w_gate", "w_up", "w_down"):
            a = a.reshape((DEPTH * N_EXPERTS,) + a.shape[2:])
        if name in ("kv_norm_g", "ret_gn_g"):
            a = np.ascontiguousarray(a.reshape(DEPTH, -1, P).transpose(0, 2, 1))
        arrays[f"in_{name}"] = a
        args[name] = nc.dram_tensor(f"in_{name}", a.shape, F32, kind="ExternalInput").ap()
    args["out"] = nc.dram_tensor("result", (1, SEQ, D_MODEL), F32, kind="ExternalOutput").ap()
    trunk(nc, **args)
    r = run_bass_kernel_spmd(nc, [arrays], core_ids=[0])
    return r.results[0]["result"]
```

```python
from contextlib import ExitStack

import concourse.bass as bass
from concourse import mybir

F32 = mybir.dt.float32
I32 = mybir.dt.int32
U32 = mybir.dt.uint32
ALU = mybir.AluOpType
ACT = mybir.ActivationFunctionType
AX_X = mybir.AxisListType.X

P = 128
D_MODEL, SEQ, DEPTH = 2048, 256, 2
TILES = SEQ // P
HEAD_DIM = 128
SB_HEADS, RET_HEADS, DSA_HEADS = 6, 4, 6
KV_RANK, IDX_HEADS, IDX_DIM = 256, 8, 64
TOPK = min(256, SEQ // 4)
N_EXPERTS, N_GROUPS, D_FF = 16, 4, 512
PER_GROUP = N_EXPERTS // N_GROUPS
LN_EPS, RMS_EPS, GN_EPS = 1e-5, 1e-6, 1e-6
ALPHA = (2 * DEPTH) ** 0.25
SCALE = HEAD_DIM ** -0.5
IDX_SCALE = IDX_DIM ** -0.5 * IDX_HEADS ** -0.5
NEG = -1.0e30
TAKEN = -3.0e38

C_SBQ = 0
C_SBK = C_SBQ + SB_HEADS * HEAD_DIM
C_SBV = C_SBK + SB_HEADS * HEAD_DIM
C_RQ = C_SBV + SB_HEADS * HEAD_DIM
C_RK = C_RQ + RET_HEADS * HEAD_DIM
C_RV = C_RK + RET_HEADS * HEAD_DIM
C_RG = C_RV + RET_HEADS * HEAD_DIM
C_DQ = C_RG + RET_HEADS * HEAD_DIM
C_CKV = C_DQ + DSA_HEADS * HEAD_DIM
C_QI = C_CKV + KV_RANK
C_KI = C_QI + IDX_HEADS * IDX_DIM
C_W = C_KI + IDX_DIM
D_IN = C_W + IDX_HEADS

KT = D_MODEL // P
NW = 512
KU = 4
CHUNK_UNITS = KT // KU
RING = 8
CHUNKS = [10, 11, 9, 8, 0, 1, 2, 5, 6, 4, 7, 3]
WO_CHUNKS = D_MODEL // NW
IN_UNITS = len(CHUNKS) * CHUNK_UNITS
WO_UNITS = WO_CHUNKS * CHUNK_UNITS
EXPERT_UNITS = 3 * CHUNK_UNITS
MOE = IN_UNITS + WO_UNITS
SLOTS = P
ROWS = 2 * SEQ
COUNTS = 4 * N_EXPERTS + 2

OVER_W, OVER_X, OVER_PE, OVER_ACT, OVER_DVE, OVER_LINK = 16 * EXPERT_UNITS, 32, 10, 6, 5, 3

RT_END = 5 * D_MODEL + 8 * TILES * N_EXPERTS
PAIRS = N_EXPERTS // 2 - 1
PAIR_UNITS = 2 * EXPERT_UNITS
LAYER_UNITS = IN_UNITS + WO_UNITS + N_EXPERTS * EXPERT_UNITS
LAYER_TURNS = LAYER_UNITS // RING
FRONT_0 = MOE
FRONT_ODD = FRONT_0 + 2 * CHUNK_UNITS
BACK_EVEN = FRONT_ODD + 2 * CHUNK_UNITS
FRONT_EVEN = BACK_EVEN + CHUNK_UNITS
BACK_ODD = FRONT_EVEN + 2 * CHUNK_UNITS
LAST = PAIRS * PAIR_UNITS
BACK_LAST = BACK_EVEN + LAST + CHUNK_UNITS

TRI = 3 * P
MOST_OVERS = DEPTH * (ROWS // (SLOTS + 1))

T_ID = 0
T_SUM = T_ID + P
T_NONE = T_SUM + P
T_STRICT = T_NONE + P
T_NSTRICT = T_STRICT + P
T_CAUSAL = T_NSTRICT + P
T_DECAY = T_CAUSAL + P
T_COS = T_DECAY + RET_HEADS * TRI
T_SIN = T_COS + TILES * HEAD_DIM
T_RANK = T_SIN + TILES * HEAD_DIM
T_COLS = T_RANK + N_EXPERTS
T_SLOT = T_COLS
T_ALL = T_SLOT + SLOTS

WO_ORDER = [(n, q) for n in (0, 1) for q in (0, 3)] + [(n, q) for n in (0, 1) for q in (1, 2)]
WO_ORDER += [(n, q) for n in range(2, WO_CHUNKS) for q in (0, 3, 1, 2)]


def width(n):
    return min(NW, D_IN - n * NW)


def plan():
    idx = [[("qiT", 0), ("qiT", 1)], [("ckvT", 0), ("kiT", 0)]]
    idx += [[("idx", h), ("idx", h + 1)] for h in range(0, IDX_HEADS, 2)]
    idx[-1].append(("topk", 0))
    dsa = []
    for i in range(DSA_HEADS + 1):
        a, b = [], []
        if i < DSA_HEADS:
            a += [("kv", i), ("dqT", i)]
            b += [("log", i)]
        if i >= 1:
            a += [("pT", i - 1)]
            b += [("out", i - 1)]
        dsa += [a, b[::-1]]
    sb = []
    for i in range(SB_HEADS + 2):
        a = []
        if i < SB_HEADS:
            a.append(("sbT", i))
        if 1 <= i <= SB_HEADS:
            a.append(("z", i - 1))
        if i >= 2:
            a.append(("arg", i - 2))
        sb.append(a)
    ret = []
    for i in range(RET_HEADS + 1):
        a = []
        if i < RET_HEADS:
            a.append(("rT", i))
        if i >= 1:
            a += [("rs", i - 1)]
        ret.append(a)
    streams = [
        [(2, [("ckvn", 0)])] + [(2, s) for s in idx] + [(4, s) for s in dsa],
        [(7, s) for s in sb] + [(10, [("sbo", 4), ("sbo", 5)])],
        [(10, [("rot", 0)])] + [(10, s) for s in ret] + [(11, [("ro", h), ("ro", h + 1)]) for h in (0, 2)]
        + [(11, [("gn", 0)])],
    ]
    steps = []
    for u in range(IN_UNITS):
        steps.append(("proj", u))
        have = u // CHUNK_UNITS
        for s in streams:
            if s and s[0][0] <= have:
                steps += s.pop(0)[1]
    for s in streams:
        for need, more in s:
            steps += more
    steps += [("sbo", h) for h in range(4)] + [("wo", u) for u in range(4)] + [("ryT", 0), ("ryT", 1)]
    steps += [("wo", u) for u in range(4, WO_UNITS)]
    return steps


STEPS = plan()
assert STEPS[:CHUNK_UNITS] == [("proj", u) for u in range(CHUNK_UNITS)]
DRAIN = {"qiT": "act", "ckvT": "dve", "kiT": "act", "idx": "act", "kv": "act", "dqT": "dve", "log": "dve",
         "pT": "act", "out": "dve", "sbT": "act", "z": "dve", "arg": "act", "sbo": "act", "rT": "dve",
         "rs": "dve", "ro": "dve", "ryT": "dve"}
FILLS = [s for s in STEPS if s[0] in DRAIN]
FILL_AT = {s: n for n, s in enumerate(FILLS)}
BANKS = 4


def reads(kind, h):
    return {"idx": [("qiT", h // 4), ("kiT", 0)], "kv": [("ckvT", 0)], "log": [("kv", h), ("dqT", h)],
            "out": [("pT", h)], "z": [("sbT", h)], "arg": [("sbT", h)], "rs": [("rT", h)],
            "sbo": [("arg", h)], "ro": [("rs", h)]}.get(kind, [])


DRAINS = {e: sum(DRAIN[s[0]] == e for s in FILLS) for e in ("act", "dve")}
DRAIN_AT = {s: sum(DRAIN[r[0]] == DRAIN[s[0]] for r in FILLS[:n + 1]) for n, s in enumerate(FILLS)}

ACT_LINKS = 17
DVE_LINKS = 170
POOL_LINKS = 7
XT_FILLS = TILES * KT // 4
XT_BY = (("act",) * 4 + ("act", "dve") * 2, ("act", "dve") * 4)
NORMS = 5
(N_CKV, N_RET, N_LN1, N_LN2_0, N_LN2_1) = range(NORMS)


def xt_count(e, i, f):
    return sum(by == e for by in (XT_BY[0] + XT_BY[1])[:i * XT_FILLS + f + 1])


XT_COPIES = {e: xt_count(e, 1, XT_FILLS - 1) for e in ("act", "dve")}


def trunk(nc, x, w_in, w_kv_up, kv_norm_g, ret_gn_g, w_o, ln1_g, ln1_b, w_router,
          w_gate, w_up, w_down, in_g, in_b, ln_cols, tables, out):
    with ExitStack() as ctx:
        def sb(name, *shape):
            return ctx.enter_context(nc.sbuf_tensor(name, [P, *shape], F32))

        def sem(name):
            return ctx.enter_context(nc.semaphore(name))

        ring = sb("ring", RING, KU, NW)
        xs = sb("xs", TILES, D_MODEL)
        xT = sb("xT", KT, SEQ)
        proj = sb("proj", TILES * D_IN)
        kvup = sb("kvup", KV_RANK // P, DSA_HEADS * 2 * HEAD_DIM)
        yT = sb("yT", KT, SEQ)
        tab = sb("tab", T_COLS)
        wr = sb("wr", KT, N_EXPERTS)
        gn_col = sb("gn_col", RET_HEADS)
        kvg_col = sb("kvg_col", KV_RANK // P)
        ln_col = sb("ln_col", 4, KT)
        dkv = sb("dkv", 2, 4 * P)
        dp = sb("dp", 2, TRI)
        sba = sb("sba", SB_HEADS, TRI)
        ra = sb("ra", RET_HEADS, TRI)
        sel = sb("sel", TRI)
        st = sb("st", TILES, 4, 6)
        mv = sb("mv", TILES * RET_HEADS, 2)
        var = sb("var", TILES * RET_HEADS)
        rstd = sb("rstd", TILES * RET_HEADS)
        nt = sb("nt", TILES * RET_HEADS)
        top8 = sb("top8", 8)
        nmax = sb("nmax", 2, TILES)
        psums = sb("psums", 2, TILES)
        wts = sb("wts", 2, TILES)
        place = ctx.enter_context(nc.sbuf_tensor("place", [P, 2 * TILES], U32))
        overs = sb("overs", 1)
        counts = ctx.enter_context(nc.sbuf_tensor("counts", [P, COUNTS], I32))

        pr = proj[:, :].rearrange("p (t n) -> p t n", t=TILES)
        ro = pr[:, :, C_RQ:C_RQ + RET_HEADS * P]
        score = yT[:, 0:2, :].rearrange("p k s -> p (k s)")[:, 0:TRI]
        work = yT[:, 2:4, :].rearrange("p k s -> p (k s)")[:, 0:TRI]
        rel = [yT[:, k:k + 2, :].rearrange("p k s -> p (k s)")[:, 0:TRI] for k in (4, 14)]
        rot = [yT[:, k:k + 2, :].rearrange("p k s -> p (k s)") for k in (6, 8)]
        sig_g = yT[:, 6:10, :].rearrange("p (t k) s -> p t (k s)", t=TILES)
        ln_g, ln_b = proj[:, 0:D_MODEL], proj[:, D_MODEL:2 * D_MODEL]
        xg = [proj[:, (2 + i) * D_MODEL:(3 + i) * D_MODEL] for i in range(2)]
        sg = [proj[:, 4 * D_MODEL + i * D_FF:4 * D_MODEL + (i + 1) * D_FF] for i in range(2)]
        hT = [proj[:, 4 * D_MODEL + (2 + i) * D_FF:4 * D_MODEL + (3 + i) * D_FF] for i in range(2)]
        rt = proj[:, 5 * D_MODEL:5 * D_MODEL + 8 * TILES * N_EXPERTS].rearrange(
            "p (i t e) -> p i t e", i=8, t=TILES)
        slot = proj[:, RT_END:RT_END + SLOTS]
        hot = proj[:, RT_END + SLOTS:RT_END + (1 + TILES) * SLOTS].rearrange(
            "p (t s) -> p t s", t=TILES)
        yb = [yT[:, i * KT // 2:(i + 1) * KT // 2, :].rearrange("p k s -> p (k s)") for i in range(2)]

        pp = [ctx.enter_context(nc.psum_tensor(f"pp{i}", [P, NW], F32)) for i in range(4)]
        pb = [ctx.enter_context(nc.psum_tensor(f"pb{i}", [P, NW], F32)) for i in range(BANKS)]

        consts_in = sem("consts_in")
        x_in = [sem(f"x_in{t}") for t in range(TILES)]
        slot_in = sem("slot_in")
        hot_ready = sem("hot_ready")
        layer_in = sem("layer_in")
        lnp_in = sem("lnp_in")
        unit_in = [sem(f"unit_in{i}") for i in range(RING)]
        slots_free = sem("slots_free")
        xt_filled = sem("xt_filled")
        xt_act = sem("xt_act")
        xt_dve = sem("xt_dve")
        chunk_out = sem("chunk_out")
        filled = sem("filled")
        act_drained = sem("act_drained")
        dve_drained = sem("dve_drained")
        ckvn_ready = sem("ckvn_ready")
        rel_used = sem("rel_used")
        ln_ready = sem("ln_ready")
        sp_ready = sem("sp_ready")
        max_ready = sem("max_ready")
        exp_ready = sem("exp_ready")
        p_ready = sem("p_ready")
        rot_ready = sem("rot_ready")
        gexp_ready = sem("gexp_ready")
        gn_ready = sem("gn_ready")
        var_ready = sem("var_ready")
        root_ready = sem("root_ready")
        mix_added = sem("mix_added")
        normed = sem("normed")
        scaled = sem("scaled")
        ident_in = sem("ident_in")
        cols_in = sem("cols_in")
        route_filled = sem("route_filled")
        rexp_ready = sem("rexp_ready")
        rmax_ready = sem("rmax_ready")
        chosen = sem("chosen")
        counted = sem("counted")
        routed = sem("routed")
        sorted_out = sem("sorted_out")
        xg_in = [sem(f"xg_in{i}") for i in range(2)]
        xw_filled = sem("xw_filled")
        xw_copied = sem("xw_copied")
        gate_exp = sem("gate_exp")
        h_ready = sem("h_ready")
        hT_filled = sem("hT_filled")
        hT_ready = sem("hT_ready")
        y_copied = sem("y_copied")
        y_out = sem("y_out")
        back_in = [sem(f"back_in{i}") for i in range(2 * TILES)]
        over_w = sem("over_w")
        over_x = sem("over_x")
        over_pe = sem("over_pe")
        over_act = sem("over_act")
        over_dve = sem("over_dve")
        over_link = sem("over_link")
        out_done = sem("out_done")
        act_link = sem("act_link")
        dve_link = sem("dve_link")
        moe_link = sem("moe_link")
        waited = sem("waited")
        pool_link = sem("pool_link")

        ident = tab[:, T_ID:T_ID + P]

        def freed(l, unit):
            return l * LAYER_UNITS + (RING + unit + 1)

        def wait_drained(eng, l, *steps):
            for which, semaphore in (("act", act_drained), ("dve", dve_drained)):
                at = [DRAIN_AT[s] for s in steps if DRAIN[s[0]] == which]
                if at:
                    eng.wait_ge(semaphore, l * DRAINS[which] + max(at))

        def wait_filled(eng, l, step):
            eng.wait_ge(filled, l * len(FILLS) + FILL_AT[step] + 1)

        def bank(step):
            return pb[FILL_AT[step] % BANKS]

        def wait_apart(eng, semaphore, value):
            eng.wait_ge(semaphore, value)
            eng.sem_inc(waited, 1)

        def col(c, t, n=P):
            return pr[:, t, c:c + n]

        def kvn(r):
            return cols(C_CKV + r * P)

        def cols(c):
            return pr[:, :, c:c + P]

        def wait_xt(eng, l, i, first, last):
            for e, semaphore in (("act", xt_act), ("dve", xt_dve)):
                if e in XT_BY[i][first:last + 1]:
                    eng.wait_ge(semaphore, l * XT_COPIES[e] + xt_count(e, i, last))

        def xT_parts(i, f):
            t, k = f // (KT // 4), f % (KT // 4) * 4
            return [(xT[:, k + j, t * P:(t + 1) * P], pb[f % BANKS][:, j * P:(j + 1) * P],
                     ln_col[:, 2 * i, k + j:k + j + 1], ln_col[:, 2 * i + 1, k + j:k + j + 1]) for j in range(4)]

        x_sorted = nc.dram_tensor("x_sorted", (ROWS + SLOTS, D_MODEL), F32, kind="Internal").ap()
        y_sorted = nc.dram_tensor("y_sorted", (ROWS + SLOTS, D_MODEL), F32, kind="Internal").ap()

        def window(eng, e, table):
            return eng.value_load(counts[0:1, bass.ds(e + table * N_EXPERTS, 1)], min_val=0, max_val=ROWS)

        def tokens(eng, e):
            return eng.value_load(counts[0:1, bass.ds(e + N_EXPERTS, 1)], min_val=0, max_val=SEQ)

        def overs_before(eng, e):
            return eng.value_load(counts[0:1, bass.ds(e + 3 * N_EXPERTS, 1)], min_val=0, max_val=MOST_OVERS)

        def most_tokens(eng):
            return eng.value_load(counts[0:1, COUNTS - 2:COUNTS - 1], min_val=0, max_val=SEQ)

        block = ctx.enter_context(nc.Block())

        @block.sync
        def _(sp):
            for t in range(TILES):
                sp.dma_start(xs[:, t, :], x[0, t * P:(t + 1) * P, :]).then_inc(x_in[t], 16)
            sp.sem_inc(over_x, 16)
            with sp.Fori(0, DEPTH) as l:
                g = 0

                def unit(src, dst, base, g):
                    if g % RING == 0:
                        wait_apart(sp, slots_free, base + g + 1)
                    else:
                        sp.wait_ge(slots_free, base + g + 1)
                    sp.dma_start(dst, src).then_inc(unit_in[g % RING], 16)

                for n in CHUNKS:
                    for q in range(CHUNK_UNITS):
                        src = w_in[bass.ds(l, 1), q * KU * P:(q + 1) * KU * P, n * NW:n * NW + width(n)]
                        unit(src.rearrange("a (k p) n -> p (a k) n", p=P), ring[:, g % RING, :, 0:width(n)],
                             l * LAYER_UNITS, g)
                        g += 1
                for n, q in WO_ORDER:
                    src = w_o[bass.ds(l, 1), q * KU * P:(q + 1) * KU * P, n * NW:(n + 1) * NW]
                    unit(src.rearrange("a (k p) n -> p (a k) n", p=P), ring[:, g % RING, :, :],
                         l * LAYER_UNITS, g)
                    g += 1

                def front(e, u, pair):
                    for i, w in enumerate((w_gate, w_up)):
                        for q in range(CHUNK_UNITS):
                            src = w[bass.ds(l * N_EXPERTS + e, 1), q * KU * P:(q + 1) * KU * P, :]
                            unit(src.rearrange("a (k p) n -> p (a k) n", p=P), ring[:, u % RING, :, :],
                                 l * LAYER_UNITS + pair * PAIR_UNITS, u)
                            u += 1

                def back(e, u, pair):
                    for c in range(WO_CHUNKS):
                        src = w_down[bass.ds(l * N_EXPERTS + e, 1), :, c * NW:(c + 1) * NW]
                        unit(src.rearrange("a (k p) n -> p (a k) n", p=P), ring[:, u % RING, :, :],
                             l * LAYER_UNITS + pair * PAIR_UNITS, u)
                        u += 1

                front(0, FRONT_0, 0)
                with sp.Fori(0, PAIRS) as pair:
                    front(pair * 2 + 1, FRONT_ODD, pair)
                    back(pair * 2, BACK_EVEN, pair)
                    front(pair * 2 + 2, FRONT_EVEN, pair)
                    back(pair * 2 + 1, BACK_ODD, pair)
                front(N_EXPERTS - 1, FRONT_ODD + LAST, 0)
                back(N_EXPERTS - 2, BACK_EVEN + LAST, 0)
                back(N_EXPERTS - 1, BACK_LAST, 0)

                wait_apart(sp, routed, l + 1)
                most = most_tokens(sp)
                with sp.If(most > SLOTS):
                    wait_apart(sp, slots_free, (l + 1) * LAYER_UNITS + RING)
                    wait_apart(sp, y_out, (l + 1) * (16 * N_EXPERTS) + 32)
                    with sp.Fori(0, N_EXPERTS) as e:
                        n = tokens(sp, e)
                        with sp.If(n > SLOTS):
                            m = overs_before(sp, e)
                            first = window(sp, e, 2)
                            sp.dma_start(xg[0], x_sorted[bass.ds(first, SLOTS), :]).then_inc(over_x, 16)
                            for i, w in enumerate((w_gate, w_up)):
                                for q in range(CHUNK_UNITS):
                                    src = w[bass.ds(l * N_EXPERTS + e, 1), q * KU * P:(q + 1) * KU * P, :]
                                    sp.dma_start(ring[:, i * CHUNK_UNITS + q, :, :],
                                                 src.rearrange("a (k p) n -> p (a k) n", p=P)).then_inc(over_w, 16)
                            wait_apart(sp, over_pe, m * OVER_PE + 5)
                            for q in range(CHUNK_UNITS):
                                src = w_down[bass.ds(l * N_EXPERTS + e, 1), q * P:(q + 1) * P, :]
                                sp.dma_start(ring[:, q, :, :].rearrange("p k n -> p (k n)"),
                                             src.rearrange("a p n -> p (a n)")).then_inc(over_w, 16)
                            wait_apart(sp, over_dve, (m + 1) * OVER_DVE)
                            sp.dma_start(y_sorted[bass.ds(first, SLOTS), :], yb[0]).then_inc(over_x, 16)
                            wait_apart(sp, over_w, (m + 1) * OVER_W)
                            wait_apart(sp, over_x, (m + 1) * OVER_X + 16)
            for t in range(TILES):
                sp.wait_ge(scaled, DEPTH * 2 * TILES + t + 1)
                sp.dma_start(out[0, t * P:(t + 1) * P, :], xs[:, t, :]).then_inc(out_done, 16)
            sp.wait_ge(out_done, 16 * TILES)
            sp.wait_ge(cols_in, 16 * (DEPTH + 1))

        @block.gpsimd
        def _(pool):
            links = [0]
            pool.wait_ge(consts_in, 32)
            for table in (x_sorted, y_sorted):
                pool.dma_start(table[ROWS:ROWS + SLOTS, :], x[0, 0:SLOTS, :]).then_inc(y_out, 16)
            pool.wait_ge(y_out, 32)
            with pool.Fori(0, DEPTH) as l:
                def link(ins):
                    links[0] += 1
                    ins.then_inc(pool_link, 1)
                    pool.wait_ge(pool_link, l * POOL_LINKS + links[0])

                pool.wait_ge(chunk_out, l * len(CHUNKS) + 10)
                n = 0
                for c in (C_RQ, C_RK):
                    for t in range(TILES):
                        v = pr[:, t, c:c + RET_HEADS * P].rearrange("p (h d) -> p h d", h=RET_HEADS)
                        a = rot[0].rearrange("p (h d) -> p h d", h=RET_HEADS)
                        b = rot[1].rearrange("p (h d) -> p h d", h=RET_HEADS)
                        half = HEAD_DIM // 2

                        def table(first, n):
                            return tab[:, first:first + n].unsqueeze(1).broadcast_to([P, RET_HEADS, n])

                        pool.tensor_tensor(a, v, table(T_COS + t * P, P), ALU.mult)
                        pool.tensor_tensor(b[:, :, 0:half], v[:, :, half:P], table(T_SIN + t * P, half), ALU.mult)
                        link(pool.tensor_tensor(b[:, :, half:P], v[:, :, 0:half],
                                                table(T_SIN + t * P + half, half), ALU.mult))
                        last = pool.tensor_tensor(v, a, b, ALU.add)
                        n += 1
                        if n < 2 * TILES:
                            link(last)
                        else:
                            last.then_inc(rot_ready, 1)

                wait_apart(pool, routed, l + 1)
                for t in range(TILES):
                    for c in range(2):
                        pool.indirect_dma_start(
                            x_sorted, bass.IndirectOffsetOnAxis(ap=place[:, c * TILES + t:c * TILES + t + 1], axis=0),
                            xs[:, t, :], None).then_inc(sorted_out, 16)
                wait_apart(pool, sorted_out, (l + 1) * 64)

                def load(e, par):
                    first = window(pool, e, 0)
                    wait_apart(pool, xw_filled, (l * N_EXPERTS + e) * 4)
                    pool.dma_start(xg[par], x_sorted[bass.ds(first, SLOTS), :]).then_inc(xg_in[par], 16)

                def store(e, par):
                    first = window(pool, e, 0)
                    n = l * N_EXPERTS + e
                    wait_apart(pool, y_copied, n * 4 + 6)
                    wait_apart(pool, y_out, n * 16 + 32)
                    pool.dma_start(y_sorted[bass.ds(first, SLOTS), :], yb[par]).then_inc(y_out, 16)

                for e in (1, 2):
                    load(e, e % 2)
                with pool.Fori(0, PAIRS - 1) as pair:
                    for par in range(2):
                        load(pair * 2 + (3 + par), 1 - par)
                        store(pair * 2 + par, par)
                load(N_EXPERTS - 1, 1)
                for e in range(N_EXPERTS - 4, N_EXPERTS):
                    store(e, e % 2)
                wait_apart(pool, y_out, (l + 1) * (16 * N_EXPERTS) + 32)

                overs = pool.value_load(counts[0:1, COUNTS - 1:COUNTS], min_val=0, max_val=MOST_OVERS)
                wait_apart(pool, over_x, overs * OVER_X + 16)

                wait_apart(pool, xw_filled, (l + 1) * (4 * N_EXPERTS) + 4)
                for t in range(TILES):
                    for c in range(2):
                        pool.indirect_dma_start(
                            (xg, yb)[t][c], None, y_sorted,
                            bass.IndirectOffsetOnAxis(ap=place[:, c * TILES + t:c * TILES + t + 1], axis=0)).then_inc(
                                back_in[2 * t + c], 16)
            assert links[0] == POOL_LINKS, links

        @block.scalar
        def _(act):
            act.dma_start(ln_col[:, :, :], ln_cols[0]).then_inc(cols_in, 16)
            act.dma_start(ident, tables[:, T_ID:T_ID + P]).then_inc(ident_in, 16)
            act.dma_start(tab[:, P:T_COLS], tables[:, P:T_COLS]).then_inc(consts_in, 16)
            act.dma_start(wr[:, :, :], w_router.rearrange("(k p) e -> p k e", p=P)).then_inc(consts_in, 16)
            act.dma_start(ln_g, in_g[0:1].broadcast_to([P, D_MODEL])).then_inc(lnp_in, 16)
            act.dma_start(ln_b, in_b[0:1].broadcast_to([P, D_MODEL])).then_inc(lnp_in, 16)
            act.sem_inc(hT_ready, 1)
            act.sem_inc(xw_copied, 1)
            links = [0]
            with act.Fori(0, DEPTH) as l:
                def link(ins):
                    links[0] += 1
                    ins.then_inc(act_link, 1)
                    act.wait_ge(act_link, l * ACT_LINKS + links[0])

                def root(which, n, first=0):
                    act.wait_ge(var_ready, l * NORMS + which + 1)
                    link(act.activation(rstd[:, first:n], var[:, first:n], ACT.Ln))
                    act.activation(rstd[:, first:n], rstd[:, first:n], ACT.Exp, scale=-0.5).then_inc(root_ready, 1)

                def copy_xT(i):
                    act.wait_ge(cols_in, l * 16 + 16)
                    for f in [f for f in range(XT_FILLS) if XT_BY[i][f] == "act"]:
                        act.wait_ge(xt_filled, l * (2 * XT_FILLS) + (i * XT_FILLS + f + 1))
                        for to, out_of, gain, bias in xT_parts(i, f):
                            last = act.activation(to, out_of, ACT.Identity, scale=gain, bias=bias)
                        last.then_inc(xt_act, 1)

                act.wait_ge(xt_filled, l * (2 * XT_FILLS) + 1)
                act.dma_start(kvup[:, :, :],
                              w_kv_up[bass.ds(l, 1)].rearrange("a (r p) n -> p (a r) n", p=P)).then_inc(layer_in, 16)
                act.dma_start(kvg_col[:, :],
                              kv_norm_g[bass.ds(l, 1)].rearrange("a p r -> (a p) r")).then_inc(layer_in, 16)
                act.dma_start(gn_col[:, :],
                              ret_gn_g[bass.ds(l, 1)].rearrange("a p h -> (a p) h")).then_inc(layer_in, 16)
                copy_xT(0)

                for kind, h in STEPS:
                    step = (kind, h)
                    if kind == "proj" and h % CHUNK_UNITS == CHUNK_UNITS - 1:
                        c = h // CHUNK_UNITS
                        n = CHUNKS[c]
                        act.wait_ge(slots_free, freed(l, h))
                        act.activation(pr[:, 0, n * NW:n * NW + width(n)], pp[2 * (c % 2)][:, 0:width(n)], ACT.Copy)
                        act.activation(pr[:, 1, n * NW:n * NW + width(n)], pp[2 * (c % 2) + 1][:, 0:width(n)],
                                       ACT.Copy).then_inc(chunk_out, 1)
                    elif kind == "ckvn":
                        root(N_CKV, TILES)
                    elif kind == "qiT":
                        wait_filled(act, l, step)
                        for j in range(2):
                            last = act.activation(cols(C_QI + (2 * h + j) * P),
                                                  bank(step)[:, j * SEQ:(j + 1) * SEQ].rearrange("p (t s) -> p t s", t=2),
                                                  ACT.Copy)
                        last.then_inc(act_drained, 1)
                    elif kind == "kiT":
                        wait_filled(act, l, step)
                        act.activation(dkv[:, 1, 0:SEQ], bank(step)[:, 0:SEQ], ACT.Copy).then_inc(act_drained, 1)
                    elif kind == "idx":
                        wait_filled(act, l, step)
                        if h >= 2:
                            act.wait_ge(rel_used, l * IDX_HEADS + h - 1)
                        act.activation(rel[h % 2], bank(step)[:, 0:TRI], ACT.Relu).then_inc(act_drained, 1)
                    elif kind == "kv":
                        wait_filled(act, l, step)
                        act.activation(dkv[:, h % 2, :], bank(step)[:, :], ACT.Copy).then_inc(act_drained, 1)
                    elif kind == "log":
                        act.wait_ge(max_ready, l * DSA_HEADS + h + 1)
                        for t, (a, b) in enumerate(((0, P), (P, TRI))):
                            last = act.activation(dp[:, h % 2, a:b], dp[:, h % 2, a:b], ACT.Exp,
                                                  bias=nmax[:, h % 2, t:t + 1], accum_out=psums[:, h % 2, t:t + 1])
                            last.then_inc(exp_ready, 1)
                    elif kind == "pT":
                        wait_filled(act, l, step)
                        act.activation(dp[:, h % 2, :], bank(step)[:, 0:TRI], ACT.Copy).then_inc(act_drained, 1)
                    elif kind == "sbT":
                        wait_filled(act, l, step)
                        b = bank(step)[:, :].rearrange("p (j t s) -> p j t s", j=2, t=2)
                        act.activation(cols(C_SBQ + h * P), b[:, 0], ACT.Copy, scale=SCALE)
                        act.activation(cols(C_SBK + h * P), b[:, 1], ACT.Copy).then_inc(act_drained, 1)
                    elif kind == "z":
                        wait_filled(act, l, step)
                        link(act.activation(sba[:, h, :], bank(step)[:, 0:TRI], ACT.Abs))
                        link(act.activation(sba[:, h, :], sba[:, h, :], ACT.Exp, scale=-1.0))
                        act.activation(sba[:, h, :], sba[:, h, :], ACT.Ln, bias=1.0).then_inc(ln_ready, 1)
                    elif kind == "arg":
                        wait_filled(act, l, step)
                        act.activation(sba[:, h, :], bank(step)[:, 0:TRI], ACT.Exp).then_inc(act_drained, 1)
                    elif kind == "sbo":
                        wait_filled(act, l, step)
                        act.activation(yT[:, h, :], bank(step)[:, 0:SEQ], ACT.Copy).then_inc(act_drained, 1)
                    elif kind == "gn":
                        act.wait_ge(chunk_out, l * len(CHUNKS) + 11)
                        act.wait_ge(rot_ready, l + 1)
                        act.activation(sig_g, pr[:, :, C_RG:C_RG + RET_HEADS * P], ACT.Exp,
                                       scale=-1.0).then_inc(gexp_ready, 1)
                        root(N_RET, TILES * RET_HEADS)

                act.wait_ge(dve_drained, (l + 1) * DRAINS["dve"])
                act.wait_ge(filled, (l + 1) * len(FILLS))
                act.dma_start(ln_g, ln1_g[bass.ds(l, 1)].broadcast_to([P, D_MODEL])).then_inc(lnp_in, 16)
                act.dma_start(ln_b, ln1_b[bass.ds(l, 1)].broadcast_to([P, D_MODEL])).then_inc(lnp_in, 16)
                act.dma_start(slot, tables[:, T_SLOT:T_SLOT + SLOTS]).then_inc(slot_in, 16)
                root(N_LN1, TILES)
                copy_xT(1)
                act.wait_ge(scaled, l * (2 * TILES) + 2 * TILES)
                act.dma_start(ln_g, in_g[bass.ds(l + 1, 1)].broadcast_to([P, D_MODEL])).then_inc(lnp_in, 16)
                act.dma_start(ln_b, in_b[bass.ds(l + 1, 1)].broadcast_to([P, D_MODEL])).then_inc(lnp_in, 16)
                wait_xt(act, l, 1, 0, XT_FILLS - 1)
                act.dma_start(ln_col[:, :, :], ln_cols[bass.ds(l + 1, 1)].rearrange("a p i k -> p (a i) k")).then_inc(
                    cols_in, 16)
                act.wait_ge(rmax_ready, l + 1)
                act.activation(rt[:, 1], rt[:, 0], ACT.Exp).then_inc(rexp_ready, 1)

                def copy_window(e, par):
                    for f in range(4):
                        act.wait_ge(xw_filled, (l * N_EXPERTS + e) * 4 + (f + 5))
                        act.activation(xT[:, 4 * f:4 * f + 4, par * P:(par + 1) * P],
                                       pb[3][:, :].rearrange("p (k s) -> p k s", k=4), ACT.Copy).then_inc(xw_copied, 1)

                def front(e, par, u, pair, more=True):
                    if more:
                        copy_window(e + 1, 1 - par)
                    n = l * N_EXPERTS + e
                    act.wait_ge(slots_free, l * LAYER_UNITS + pair * PAIR_UNITS + (RING + u + CHUNK_UNITS))
                    act.wait_ge(hT_filled, n + 1)
                    act.activation(sg[par], pp[2 * par][:, :], ACT.Exp, scale=-1.0).then_inc(gate_exp, 1)

                def back(e, par):
                    act.wait_ge(hT_filled, l * N_EXPERTS + e + 3)
                    act.activation(hT[par], pb[0][:, :], ACT.Copy).then_inc(hT_ready, 1)

                copy_window(0, 0)
                front(0, 0, FRONT_0, 0, more=False)
                copy_window(1, 1)
                with act.Fori(0, PAIRS) as pair:
                    back(pair * 2, 0)
                    front(pair * 2 + 1, 1, FRONT_ODD, pair)
                    back(pair * 2 + 1, 1)
                    front(pair * 2 + 2, 0, FRONT_EVEN, pair)
                back(N_EXPERTS - 2, 0)
                front(N_EXPERTS - 1, 1, FRONT_ODD + LAST, 0, more=False)
                back(N_EXPERTS - 1, 1)

                wait_apart(act, routed, l + 1)
                most = most_tokens(act)
                with act.If(most > SLOTS):
                    with act.Fori(0, N_EXPERTS) as e:
                        n = tokens(act, e)
                        with act.If(n > SLOTS):
                            m = overs_before(act, e)
                            for f in range(4):
                                act.wait_ge(over_pe, m * OVER_PE + (f + 1))
                                act.activation(xT[:, 4 * f:4 * f + 4, 0:P],
                                               pb[3][:, :].rearrange("p (k s) -> p k s", k=4),
                                               ACT.Copy).then_inc(over_act, 1)
                            act.wait_ge(over_pe, m * OVER_PE + 5)
                            act.activation(sg[0], pp[0][:, :], ACT.Exp, scale=-1.0).then_inc(over_act, 1)
                            act.wait_ge(over_pe, m * OVER_PE + 6)
                            act.activation(hT[0], pb[0][:, :], ACT.Copy).then_inc(over_act, 1)
                root(N_LN2_0, 1)
                root(N_LN2_1, 2, first=1)
            assert links[0] == ACT_LINKS, links

        @block.tensor
        def _(pe):
            pe.sem_inc(slots_free, RING)
            pe.sem_inc(hT_filled, 2)
            pe.sem_inc(xw_filled, 4)
            pe.wait_ge(ident_in, 16)
            mm = pe.matmul
            with pe.Fori(0, DEPTH) as l:
                def transpose_x(i, t):
                    for f in range(t * KT // 4, (t + 1) * KT // 4):
                        k = f % (KT // 4) * 4
                        if k == 0:
                            pe.wait_ge(normed, l * (2 * TILES) + (i * TILES + t + 1))
                            if i == 0:
                                pe.wait_ge(x_in[t], 16)
                        if f >= BANKS:
                            wait_xt(pe, l, i, f - BANKS, f - BANKS)
                        for j in range(4):
                            last = pe.transpose(pb[f % BANKS][:, j * P:(j + 1) * P],
                                                xs[:, t, (k + j) * P:(k + j + 1) * P], ident)
                        last.then_inc(xt_filled, 1)

                def project_in(u, t):
                    c, q, slot = u // CHUNK_UNITS, u % CHUNK_UNITS, u % RING
                    w = width(CHUNKS[c])
                    if t == 0:
                        pe.wait_ge(unit_in[slot], l * (16 * LAYER_TURNS) + 16 * (u // RING + 1))
                    for kk in range(KU):
                        k = q * KU + kk
                        last = mm(pp[2 * (c % 2) + t][:, 0:w], xT[:, k, t * P:(t + 1) * P],
                                  ring[:, slot, kk, 0:w], start=(k == 0), stop=(k == KT - 1))
                    return last

                def project_out(u):
                    n, q = WO_ORDER[u]
                    if n >= 2 and q == 0:
                        pe.wait_ge(mix_added, l * WO_CHUNKS + n - 1)
                    i = (IN_UNITS + u) % RING
                    pe.wait_ge(unit_in[i], l * (16 * LAYER_TURNS) + 16 * ((IN_UNITS + u) // RING + 1))
                    for t in range(TILES):
                        for kk in range(KU):
                            last = mm(pp[2 * (n % 2) + t][:, :], yT[:, q * KU + kk, t * P:(t + 1) * P],
                                      ring[:, i, kk, :], start=(q == 0 and kk == 0), stop=(q == 2 and kk == KU - 1))
                    last.then_inc(slots_free, 1)

                for t in range(TILES):
                    transpose_x(0, t)
                    for h in range(CHUNK_UNITS):
                        f = t * KT // 4 + h
                        wait_xt(pe, l, 0, f, f)
                        last = project_in(h, t)
                        if t == TILES - 1:
                            last.then_inc(slots_free, 1)

                for kind, h in STEPS[CHUNK_UNITS:]:
                    step = (kind, h)
                    if kind in DRAIN:
                        f = FILL_AT[step]
                        wait_drained(pe, l, *FILLS[max(f - BANKS, 0):max(f - BANKS + 1, 0)], *reads(kind, h))
                        b = bank(step)
                    if kind == "proj":
                        c, q = h // CHUNK_UNITS, h % CHUNK_UNITS
                        if q == 0 and c >= 2:
                            pe.wait_ge(chunk_out, l * len(CHUNKS) + c - 1)
                        for t in range(TILES):
                            last = project_in(h, t)
                        last.then_inc(slots_free, 1)
                    elif kind == "wo":
                        if h == 0:
                            wait_drained(pe, l, *[s for s in FILLS if s[0] != "ryT"])
                            pe.wait_ge(chunk_out, l * len(CHUNKS) + len(CHUNKS))
                        elif h == 4:
                            wait_drained(pe, l, ("ryT", 1))
                        project_out(h)
                    elif kind == "qiT":
                        pe.wait_ge(chunk_out, l * len(CHUNKS) + 2)
                        for j in range(4):
                            last = pe.transpose(b[:, j * P:(j + 1) * P], col(C_QI + (2 * h + j // 2) * P, j % 2), ident)
                        last.then_inc(filled, 1)
                    elif kind == "ckvT":
                        pe.wait_ge(ckvn_ready, l + 1)
                        for j in range(4):
                            last = pe.transpose(b[:, j * P:(j + 1) * P], col(C_CKV + (j // 2) * P, j % 2), ident)
                        last.then_inc(filled, 1)
                    elif kind == "kiT":
                        for t in range(TILES):
                            last = pe.transpose(b[:, t * P:(t + 1) * P], dkv[:, 0, t * P:(t + 1) * P], ident)
                        last.then_inc(filled, 1)
                    elif kind == "idx":
                        r = slice(IDX_DIM * (h % 2), IDX_DIM * (h % 2) + IDX_DIM)
                        c = C_QI + (h // 2) * P
                        mm(b[:, 0:P], pr[r, 0, c:c + P], dkv[r, 1, 0:P], start=True, stop=True)
                        mm(b[:, P:TRI], pr[r, 1, c:c + P], dkv[r, 1, 0:SEQ], start=True, stop=True).then_inc(filled, 1)
                    elif kind == "kv":
                        pe.wait_ge(layer_in, l * 48 + 48)
                        c = h * 2 * P
                        for r in range(2):
                            mm(b[:, 0:SEQ], kvup[:, r, c:c + P], kvn(r), start=(r == 0), stop=(r == 1))
                        for t in range(TILES):
                            for r in range(2):
                                last = mm(b[:, (2 + t) * P:(3 + t) * P], kvn(r)[:, t, :], kvup[:, r, c + P:c + 2 * P],
                                          start=(r == 0), stop=(r == 1))
                        last.then_inc(filled, 1)
                    elif kind == "dqT":
                        pe.wait_ge(chunk_out, l * len(CHUNKS) + 4)
                        for t in range(TILES):
                            last = pe.transpose(b[:, t * P:(t + 1) * P], col(C_DQ + h * P, t), ident)
                        last.then_inc(filled, 1)
                    elif kind == "log":
                        q = cols(C_DQ + h * P)
                        mm(b[:, 0:P], q[:, 0, :], dkv[:, h % 2, 0:P], start=True, stop=True)
                        mm(b[:, P:TRI], q[:, 1, :], dkv[:, h % 2, 0:SEQ], start=True, stop=True).then_inc(filled, 1)
                    elif kind == "pT":
                        pe.wait_ge(p_ready, l * DSA_HEADS + h + 1)
                        for j in range(3):
                            last = pe.transpose(b[:, j * P:(j + 1) * P], dp[:, h % 2, j * P:(j + 1) * P], ident)
                        last.then_inc(filled, 1)
                    elif kind == "out":
                        mm(b[:, 0:P], dkv[:, h % 2, 2 * P:3 * P], dp[:, h % 2, 0:P], start=True, stop=True)
                        mm(b[:, P:SEQ], dkv[:, h % 2, 2 * P:3 * P], dp[:, h % 2, P:SEQ], start=True, stop=False)
                        mm(b[:, P:SEQ], dkv[:, h % 2, 3 * P:4 * P], dp[:, h % 2, SEQ:TRI],
                           start=False, stop=True).then_inc(filled, 1)
                    elif kind in ("sbT", "rT"):
                        if kind == "sbT":
                            pe.wait_ge(chunk_out, l * len(CHUNKS) + 7)
                            cq, ck = C_SBQ + h * P, C_SBK + h * P
                        else:
                            pe.wait_ge(rot_ready, l + 1)
                            cq, ck = C_RQ + h * P, C_RK + h * P
                        for j in range(4):
                            last = pe.transpose(b[:, j * P:(j + 1) * P], col((cq, ck)[j // 2], j % 2), ident)
                        last.then_inc(filled, 1)
                    elif kind in ("z", "arg", "rs"):
                        cq, ck = (C_RQ + h * P, C_RK + h * P) if kind == "rs" else (C_SBQ + h * P, C_SBK + h * P)
                        if kind == "arg":
                            pe.wait_ge(consts_in, 32)
                            pe.wait_ge(sp_ready, l * SB_HEADS + h + 1)
                        for at, j, i in ((0, 0, 0), (P, 0, 1), (SEQ, 1, 1)):
                            o = b[:, at:at + P]
                            last = mm(o, cols(ck)[:, j, :], cols(cq)[:, i, :], start=True, stop=(kind != "arg"))
                            if kind == "arg":
                                mm(o, tab[:, T_SUM:T_SUM + P], sba[:, h, at:at + P], start=False, stop=False)
                                if i == j:
                                    last = mm(o, ident, tab[:, T_NSTRICT:T_NSTRICT + P], start=False, stop=True)
                                else:
                                    last = mm(o, tab[:, T_NONE:T_NONE + P], sba[:, h, SEQ:TRI], start=False, stop=True)
                        last.then_inc(filled, 1)
                    elif kind == "sbo":
                        pe.wait_ge(chunk_out, l * len(CHUNKS) + (12 if h < 4 else 10))
                        mm(b[:, 0:P], col(C_SBV + h * P, 0), sba[:, h, 0:P], start=True, stop=True)
                        mm(b[:, P:SEQ], col(C_SBV + h * P, 0), sba[:, h, P:SEQ], start=True, stop=False)
                        mm(b[:, P:SEQ], col(C_SBV + h * P, 1), sba[:, h, SEQ:TRI], start=False,
                           stop=True).then_inc(filled, 1)
                    elif kind == "ro":
                        pe.wait_ge(chunk_out, l * len(CHUNKS) + 11)
                        a = ra[:, h, :]
                        mm(b[:, 0:P], a[:, 0:P], col(C_RV + h * P, 0), start=True, stop=True)
                        mm(b[:, P:SEQ], a[:, P:SEQ], col(C_RV + h * P, 0), start=True, stop=False)
                        mm(b[:, P:SEQ], a[:, SEQ:TRI], col(C_RV + h * P, 1), start=False,
                           stop=True).then_inc(filled, 1)
                    elif kind == "ryT":
                        pe.wait_ge(gn_ready, l + 1)
                        for j in range(4):
                            last = pe.transpose(b[:, j * P:(j + 1) * P],
                                                ro[:, j % 2, (2 * h + j // 2) * P:(2 * h + j // 2 + 1) * P], ident)
                        last.then_inc(filled, 1)

                for t in range(TILES):
                    transpose_x(1, t)
                for t in range(TILES):
                    wait_xt(pe, l, 1, t * KT // 4, (t + 1) * KT // 4 - 1)
                    for k in range(KT):
                        last = mm(pp[0][:, t * N_EXPERTS:(t + 1) * N_EXPERTS], xT[:, k, t * P:(t + 1) * P], wr[:, k, :],
                                  start=(k == 0), stop=(k == KT - 1))
                last.then_inc(route_filled, 1)

                pe.wait_ge(chosen, l + 1)
                b = pb[2]
                mm(b[:, 0:N_EXPERTS], tab[:, T_STRICT:T_STRICT + P], rt[:, 2, 0, :], start=True, stop=True)
                mm(b[:, N_EXPERTS:2 * N_EXPERTS], tab[:, T_STRICT:T_STRICT + P], rt[:, 2, 1, :], start=True, stop=True)
                mm(b[:, 2 * N_EXPERTS:3 * N_EXPERTS], tab[:, T_NONE:T_NONE + P], rt[:, 2, 0, :], start=True, stop=True)
                for t in range(TILES):
                    last = mm(b[:, 3 * N_EXPERTS:4 * N_EXPERTS], tab[:, T_NONE:T_NONE + P], rt[:, 2, t, :],
                              start=(t == 0), stop=(t == TILES - 1))
                last.then_inc(counted, 1)

                def window_part(e, par, f):
                    n = l * N_EXPERTS + e
                    if f == 0:
                        pe.wait_ge(xg_in[par], landed(e, par))
                    pe.wait_ge(xw_copied, n * 4 + (f + 1))
                    for j in range(4):
                        k = 4 * f + j
                        last = pe.transpose(pb[3][:, j * P:(j + 1) * P], xg[par][:, k * P:(k + 1) * P], ident)
                    last.then_inc(xw_filled, 1)

                def landed(e, par):
                    if par:
                        return l * (16 * N_EXPERTS // 2) + (e - 1) * 8 + 16
                    return l * (16 * (N_EXPERTS // 2 - 1)) + e * 8

                def wait_unit(u, pair):
                    pe.wait_ge(unit_in[u % RING], l * (16 * LAYER_TURNS) + pair * (16 * PAIR_UNITS // RING)
                               + 16 * (u // RING + 1))

                def front(e, par, u, pair, more=True):
                    n = l * N_EXPERTS + e
                    pe.wait_ge(xw_copied, n * 4 + 5)
                    pe.wait_ge(h_ready, n + 1)
                    for w in range(2):
                        for q in range(CHUNK_UNITS):
                            wait_unit(u, pair)
                            for kk in range(KU):
                                k = q * KU + kk
                                last = mm(pp[2 * par + w][:, :], xT[:, k, par * P:(par + 1) * P],
                                          ring[:, u % RING, kk, :], start=(k == 0), stop=(k == KT - 1))
                            last.then_inc(slots_free, 1)
                            u += 1
                            if w == 0 and more:
                                window_part(e + 1, 1 - par, q)

                def turn(e, par):
                    n = l * N_EXPERTS + e
                    pe.wait_ge(h_ready, n + 3)
                    pe.wait_ge(hT_ready, n + 1)
                    for k in range(4):
                        last = pe.transpose(pb[0][:, k * P:(k + 1) * P], sg[par][:, k * P:(k + 1) * P], ident)
                    last.then_inc(hT_filled, 1)

                def back(e, par, u, pair):
                    n = l * N_EXPERTS + e
                    pe.wait_ge(hT_ready, n + 2)
                    for c in range(WO_CHUNKS):
                        pe.wait_ge(y_copied, n * 4 + (c + 1))
                        wait_unit(u + c, pair)
                        for k in range(KU):
                            last = mm(pb[1 + c % 2][:, :], hT[par][:, k * P:(k + 1) * P],
                                      ring[:, (u + c) % RING, k, :], start=(k == 0), stop=(k == KU - 1))
                        last.then_inc(slots_free, 1)

                pe.wait_ge(hot_ready, l + 1)
                for f in range(4):
                    pe.wait_ge(xw_copied, l * (4 * N_EXPERTS) + (f + 1))
                    for k in range(4 * f, 4 * f + 4):
                        for t in range(TILES):
                            last = mm(pb[3][:, k % 4 * P:(k % 4 + 1) * P], xs[:, t, k * P:(k + 1) * P], hot[:, t, :],
                                      start=(t == 0), stop=(t == TILES - 1))
                    last.then_inc(xw_filled, 1)
                front(0, 0, FRONT_0, 0, more=False)
                for f in range(4):
                    window_part(1, 1, f)
                with pe.Fori(0, PAIRS) as pair:
                    turn(pair * 2, 0)
                    front(pair * 2 + 1, 1, FRONT_ODD, pair)
                    back(pair * 2, 0, BACK_EVEN, pair)
                    turn(pair * 2 + 1, 1)
                    front(pair * 2 + 2, 0, FRONT_EVEN, pair)
                    back(pair * 2 + 1, 1, BACK_ODD, pair)
                turn(N_EXPERTS - 2, 0)
                front(N_EXPERTS - 1, 1, FRONT_ODD + LAST, 0, more=False)
                back(N_EXPERTS - 2, 0, BACK_EVEN + LAST, 0)
                turn(N_EXPERTS - 1, 1)
                back(N_EXPERTS - 1, 1, BACK_LAST, 0)

                wait_apart(pe, routed, l + 1)
                most = most_tokens(pe)
                with pe.If(most > SLOTS):
                    with pe.Fori(0, N_EXPERTS) as e:
                        many = tokens(pe, e)
                        with pe.If(many > SLOTS):
                            m = overs_before(pe, e)
                            pe.wait_ge(over_x, m * OVER_X + 32)
                            for f in range(4):
                                if f:
                                    pe.wait_ge(over_act, m * OVER_ACT + f)
                                for j in range(4):
                                    k = 4 * f + j
                                    last = pe.transpose(pb[3][:, j * P:(j + 1) * P], xg[0][:, k * P:(k + 1) * P], ident)
                                last.then_inc(over_pe, 1)
                            pe.wait_ge(over_act, m * OVER_ACT + 4)
                            pe.wait_ge(over_w, m * OVER_W + 16 * 2 * CHUNK_UNITS)
                            for w in range(2):
                                for k in range(KT):
                                    last = mm(pp[w][:, :], xT[:, k, 0:P], ring[:, w * CHUNK_UNITS + k // KU, k % KU, :],
                                              start=(k == 0), stop=(k == KT - 1))
                            last.then_inc(over_pe, 1)
                            pe.wait_ge(over_dve, m * OVER_DVE + 1)
                            for k in range(4):
                                last = pe.transpose(pb[0][:, k * P:(k + 1) * P], sg[0][:, k * P:(k + 1) * P], ident)
                            last.then_inc(over_pe, 1)
                            pe.wait_ge(over_act, (m + 1) * OVER_ACT)
                            pe.wait_ge(over_w, (m + 1) * OVER_W)
                            for c in range(4):
                                if c >= 2:
                                    pe.wait_ge(over_dve, m * OVER_DVE + c)
                                for k in range(4):
                                    wd = ring[:, k, :, :].rearrange("p k n -> p (k n)")
                                    last = mm(pb[1 + c % 2][:, :], hT[0][:, k * P:(k + 1) * P],
                                              wd[:, c * NW:(c + 1) * NW], start=(k == 0), stop=(k == 3))
                                last.then_inc(over_pe, 1)

        @block.vector
        def _(dve):
            links = [0]
            dve.sem_inc(normed, TILES)
            dve.sem_inc(h_ready, 2)
            dve.memset(overs[:, :], 0.0)
            dve.sem_inc(y_copied, 2)
            with dve.Fori(0, DEPTH) as l:
                def link(ins, alone=False):
                    links[0] += 1
                    ins.then_inc(dve_link, 1)
                    if alone:
                        wait_apart(dve, dve_link, l * DVE_LINKS + links[0])
                    else:
                        dve.wait_ge(dve_link, l * DVE_LINKS + links[0])

                def ask_root(n, variance, eps):
                    dve.tensor_scalar(var[:, 0:n], variance, eps, None, ALU.add).then_inc(var_ready, 1)

                def take_root(which, n, first=0):
                    dve.wait_ge(root_ready, l * NORMS + which + 1)
                    link(dve.tensor_tensor(nt[:, first:n], rstd[:, first:n], rstd[:, first:n], ALU.mult))
                    link(dve.tensor_tensor(nt[:, first:n], nt[:, first:n], var[:, first:n], ALU.mult))
                    link(dve.tensor_scalar(nt[:, first:n], nt[:, first:n], -0.5, 1.5, ALU.mult, ALU.add))
                    link(dve.tensor_tensor(rstd[:, first:n], rstd[:, first:n], nt[:, first:n], ALU.mult))

                def layer_norm(which):
                    for t in range(TILES):
                        last = dve.bn_aggr(mv[:, t, :], st[:, t, :, :].rearrange("p a b -> p (a b)"))
                    link(last)
                    ask_root(TILES, mv[:, 0:TILES, 1], LN_EPS)
                    take_root(which, TILES)
                    for t in range(TILES):
                        dve.tensor_scalar(xs[:, t, :], xs[:, t, :], mv[:, t, 0:1], rstd[:, t:t + 1],
                                          ALU.subtract, ALU.mult).then_inc(normed, 1)

                def scale(i):
                    dve.wait_ge(cols_in, l * 16 + 16)
                    for f in [f for f in range(XT_FILLS) if XT_BY[i // TILES][f] == "dve"]:
                        dve.wait_ge(xt_filled, l * (2 * XT_FILLS) + (i // TILES * XT_FILLS + f + 1))
                        for to, out_of, gain, bias in xT_parts(i // TILES, f):
                            last = dve.tensor_scalar(to, out_of, gain, bias, ALU.mult, ALU.add)
                        last.then_inc(xt_dve, 1)
                    dve.wait_ge(lnp_in, l * 64 + 16 * i + 32)
                    dve.wait_ge(normed, l * (2 * TILES) + (i + TILES))
                    for t in range(TILES):
                        link(dve.tensor_tensor(xs[:, t, :], xs[:, t, :], ln_g, ALU.mult))
                        last = dve.tensor_tensor(xs[:, t, :], xs[:, t, :], ln_b, ALU.add)
                        last.then_inc(scaled, 1)
                    dve.wait_ge(scaled, l * (2 * TILES) + (i + TILES))

                scale(0)
                dve.wait_ge(consts_in, 32)
                for kind, h in STEPS:
                    step = (kind, h)
                    if kind == "ckvn":
                        dve.wait_ge(chunk_out, l * len(CHUNKS) + 2)
                        for t in range(TILES):
                            for j in range(2):
                                link(dve.tensor_copy(dkv[:, 0, t * P + j * IDX_DIM:t * P + (j + 1) * IDX_DIM],
                                                     col(C_KI, t, IDX_DIM)))
                        for t in range(TILES):
                            link(dve.bn_stats(st[:, t, 0, :], col(C_CKV, t, KV_RANK)), alone=True)
                            link(dve.bn_aggr(mv[:, t, :], st[:, t, 0, :]))
                        link(dve.tensor_tensor(nt[:, 0:TILES], mv[:, 0:TILES, 0], mv[:, 0:TILES, 0], ALU.mult))
                        link(dve.tensor_tensor(nt[:, 0:TILES], nt[:, 0:TILES], mv[:, 0:TILES, 1], ALU.add))
                        ask_root(TILES, nt[:, 0:TILES], RMS_EPS)
                        take_root(N_CKV, TILES)
                        dve.tensor_scalar(col(C_CKV, 0, KV_RANK), col(C_CKV, 0, KV_RANK), rstd[:, 0:1], None, ALU.mult)
                        dve.tensor_scalar(col(C_CKV, 1, KV_RANK), col(C_CKV, 1, KV_RANK), rstd[:, 1:2], None,
                                          ALU.mult).then_inc(ckvn_ready, 1)
                    elif kind == "ckvT":
                        wait_filled(dve, l, step)
                        dve.wait_ge(layer_in, l * 48 + 48)
                        for r in range(2):
                            last = dve.tensor_scalar(kvn(r), bank(step)[:, r * SEQ:(r + 1) * SEQ].rearrange(
                                "p (t s) -> p t s", t=2), kvg_col[:, r:r + 1], None, ALU.mult)
                        last.then_inc(dve_drained, 1)
                    elif kind == "idx":
                        wait_drained(dve, l, step)
                        for t, (a, b) in enumerate(((0, P), (P, TRI))):
                            w = col(C_W + h, t, 1)
                            if h == 0:
                                last = dve.tensor_scalar(score[:, a:b], rel[h % 2][:, a:b], w, None, ALU.mult)
                            else:
                                last = dve.scalar_tensor_tensor(score[:, a:b], rel[h % 2][:, a:b], w, score[:, a:b],
                                                                ALU.mult, ALU.add)
                        last.then_inc(rel_used, 1)
                        dve.wait_ge(rel_used, l * IDX_HEADS + h + 1)
                    elif kind == "topk":
                        link(dve.tensor_scalar(work, score, IDX_SCALE, None, ALU.mult))
                        diag = work.rearrange("p (b j) -> p b j", b=3)[:, 0:3:2, :]
                        link(dve.tensor_tensor(diag, diag,
                                               tab[:, T_CAUSAL:T_CAUSAL + P].unsqueeze(1).broadcast_to([P, 2, P]),
                                               ALU.add), alone=True)
                        for a, b in ((0, P), (P, TRI)):
                            for _ in range(TOPK // 8):
                                link(dve.max(top8[:, :], work[:, a:b]), alone=True)
                                link(dve.match_replace(work[:, a:b], top8[:, :], work[:, a:b], TAKEN), alone=True)
                        link(dve.tensor_scalar(sel[:, :], work, 0.5 * TAKEN, NEG, ALU.is_gt, ALU.mult))
                        diag = sel[:, :].rearrange("p (b j) -> p b j", b=3)[:, 0:3:2, :]
                        link(dve.tensor_tensor(diag, diag,
                                               tab[:, T_CAUSAL:T_CAUSAL + P].unsqueeze(1).broadcast_to([P, 2, P]),
                                               ALU.min))
                    elif kind == "dqT":
                        wait_filled(dve, l, step)
                        dve.tensor_copy(cols(C_DQ + h * P), bank(step)[:, 0:SEQ].rearrange(
                            "p (t s) -> p t s", t=2)).then_inc(dve_drained, 1)
                    elif kind == "log":
                        wait_filled(dve, l, step)
                        dve.scalar_tensor_tensor(dp[:, h % 2, :], bank(step)[:, 0:TRI], SCALE, sel[:, :],
                                                 ALU.mult, ALU.add).then_inc(dve_drained, 1)
                        wait_drained(dve, l, step)
                        for t, (a, b) in enumerate(((0, P), (P, TRI))):
                            link(dve.tensor_reduce(nmax[:, h % 2, t:t + 1], dp[:, h % 2, a:b], AX_X, ALU.max))
                        dve.tensor_scalar(nmax[:, h % 2, :], nmax[:, h % 2, :], -1.0, None,
                                          ALU.mult).then_inc(max_ready, 1)
                        dve.wait_ge(exp_ready, l * (2 * DSA_HEADS) + 2 * (h + 1))
                        link(dve.reciprocal(psums[:, h % 2, :], psums[:, h % 2, :]))
                        dve.tensor_scalar(dp[:, h % 2, 0:P], dp[:, h % 2, 0:P], psums[:, h % 2, 0:1], None, ALU.mult)
                        dve.tensor_scalar(dp[:, h % 2, P:TRI], dp[:, h % 2, P:TRI], psums[:, h % 2, 1:2], None,
                                          ALU.mult).then_inc(p_ready, 1)
                    elif kind == "out":
                        wait_filled(dve, l, step)
                        dve.tensor_copy(yT[:, SB_HEADS + RET_HEADS + h, :],
                                        bank(step)[:, 0:SEQ]).then_inc(dve_drained, 1)
                    elif kind == "z":
                        dve.wait_ge(ln_ready, l * SB_HEADS + h + 1)
                        dve.scalar_tensor_tensor(sba[:, h, :], bank(step)[:, 0:TRI], 0.0, sba[:, h, :],
                                                 ALU.max, ALU.add).then_inc(dve_drained, 1)
                        wait_drained(dve, l, step)
                        diag = sba[:, h, :].rearrange("p (b j) -> p b j", b=3)[:, 0:3:2, :]
                        dve.tensor_tensor(diag, diag,
                                          tab[:, T_STRICT:T_STRICT + P].unsqueeze(1).broadcast_to([P, 2, P]),
                                          ALU.mult).then_inc(sp_ready, 1)
                    elif kind == "rT":
                        wait_filled(dve, l, step)
                        b = bank(step)[:, :].rearrange("p (j t s) -> p j t s", j=2, t=2)
                        dve.tensor_copy(cols(C_RQ + h * P), b[:, 0])
                        dve.tensor_copy(cols(C_RK + h * P), b[:, 1]).then_inc(dve_drained, 1)
                    elif kind == "rs":
                        wait_filled(dve, l, step)
                        dve.tensor_tensor(ra[:, h, :], bank(step)[:, 0:TRI],
                                          tab[:, T_DECAY + h * TRI:T_DECAY + (h + 1) * TRI],
                                          ALU.mult).then_inc(dve_drained, 1)
                    elif kind == "ro":
                        wait_filled(dve, l, step)
                        dve.tensor_copy(ro[:, :, h * P:(h + 1) * P],
                                        bank(step)[:, 0:SEQ].rearrange("p (t d) -> p t d", t=2)).then_inc(dve_drained, 1)
                    elif kind == "gn":
                        wait_drained(dve, l, ("ro", RET_HEADS - 1))
                        for t in range(TILES):
                            for i in range(RET_HEADS):
                                last = dve.bn_stats(st[:, t, i, :], ro[:, t, i * P:(i + 1) * P])
                        link(last, alone=True)
                        for i in range(TILES * RET_HEADS):
                            last = dve.bn_aggr(mv[:, i, :], st[:, i // RET_HEADS, i % RET_HEADS, :])
                        link(last)
                        ask_root(TILES * RET_HEADS, mv[:, :, 1], GN_EPS)
                        dve.wait_ge(gexp_ready, l + 1)
                        g = sig_g
                        link(dve.tensor_scalar(g, g, 1.0, None, ALU.add))
                        link(dve.reciprocal(g, g))
                        link(dve.tensor_tensor(g, g, pr[:, :, C_RG:C_RG + RET_HEADS * P], ALU.mult))
                        take_root(N_RET, TILES * RET_HEADS)
                        for i in range(TILES * RET_HEADS):
                            t, k = i // RET_HEADS, i % RET_HEADS
                            v = ro[:, t, k * P:(k + 1) * P]
                            last = dve.tensor_scalar(v, v, mv[:, i, 0:1], rstd[:, i:i + 1], ALU.subtract, ALU.mult)
                        link(last)
                        dve.tensor_tensor(ro, ro, g, ALU.mult).then_inc(gn_ready, 1)
                    elif kind == "ryT":
                        wait_filled(dve, l, step)
                        for j in range(2):
                            last = dve.tensor_scalar(yT[:, SB_HEADS + 2 * h + j, :], bank(step)[:, j * SEQ:(j + 1) * SEQ],
                                                     gn_col[:, 2 * h + j:2 * h + j + 1], None, ALU.mult)
                        last.then_inc(dve_drained, 1)

                for n in range(WO_CHUNKS):
                    dve.wait_ge(slots_free, freed(l, IN_UNITS + WO_ORDER.index((n, 2))))
                    for t in range(TILES):
                        v = xs[:, t, n * NW:(n + 1) * NW]
                        last = dve.scalar_tensor_tensor(v, v, ALPHA, pp[2 * (n % 2) + t][:, :], ALU.mult, ALU.add)
                    last.then_inc(mix_added, 1)
                    dve.wait_ge(mix_added, l * WO_CHUNKS + n + 1)
                    for t in range(TILES):
                        last = dve.bn_stats(st[:, t, n, :], xs[:, t, n * NW:(n + 1) * NW])
                link(last, alone=True)
                layer_norm(N_LN1)
                scale(TILES)

                dve.wait_ge(route_filled, l + 1)
                lg, pe_, c1, c2, c3, gr, m1, m2 = (rt[:, i] for i in range(8))
                link(dve.tensor_copy(lg, pp[0][:, 0:TILES * N_EXPERTS].rearrange("p (t e) -> p t e", t=TILES)))
                link(dve.tensor_reduce(nt[:, 0:TILES], lg, AX_X, ALU.max))
                dve.tensor_tensor(lg, lg, nt[:, 0:TILES].unsqueeze(2).broadcast_to([P, TILES, N_EXPERTS]),
                                  ALU.subtract).then_inc(rmax_ready, 1)
                dve.wait_ge(rexp_ready, l + 1)
                link(dve.tensor_reduce(nt[:, 0:TILES], pe_, AX_X, ALU.add))
                link(dve.reciprocal(nt[:, 0:TILES], nt[:, 0:TILES]))
                link(dve.tensor_tensor(pe_, pe_, nt[:, 0:TILES].unsqueeze(2).broadcast_to([P, TILES, N_EXPERTS]),
                                       ALU.mult))
                pg = pe_.rearrange("p t (g e) -> p t g e", g=N_GROUPS)

                def part(v, i):
                    return v[:, :, i * N_GROUPS:(i + 1) * N_GROUPS]

                link(dve.tensor_tensor(part(c1, 0), pg[:, :, :, 0], pg[:, :, :, 1], ALU.max))
                link(dve.tensor_tensor(part(c1, 1), pg[:, :, :, 0], pg[:, :, :, 1], ALU.min))
                link(dve.tensor_tensor(part(c1, 2), pg[:, :, :, 2], pg[:, :, :, 3], ALU.max))
                link(dve.tensor_tensor(part(c1, 3), pg[:, :, :, 2], pg[:, :, :, 3], ALU.min))
                link(dve.tensor_tensor(part(c2, 0), part(c1, 0), part(c1, 2), ALU.max))
                link(dve.tensor_tensor(part(c2, 1), part(c1, 0), part(c1, 2), ALU.min))
                link(dve.tensor_tensor(part(c2, 2), part(c1, 1), part(c1, 3), ALU.max))
                link(dve.tensor_tensor(part(c2, 1), part(c2, 1), part(c2, 2), ALU.max))
                link(dve.tensor_tensor(part(c2, 0), part(c2, 0), part(c2, 1), ALU.add))
                gs = part(c2, 0)
                rank = tab[:, T_RANK:T_RANK + N_EXPERTS].unsqueeze(1).broadcast_to([P, TILES, N_EXPERTS])
                grank = tab[:, T_RANK:T_RANK + N_GROUPS].unsqueeze(1).broadcast_to([P, TILES, N_GROUPS])

                def best(value, order, mask, n, tmp):
                    def over(v):
                        return v.unsqueeze(2).broadcast_to([P, TILES, n])
                    link(dve.tensor_reduce(nt[:, 0:2], value, AX_X, ALU.max))
                    link(dve.tensor_tensor(mask, value, over(nt[:, 0:2]), ALU.is_equal))
                    link(dve.tensor_tensor(mask, mask, order, ALU.mult))
                    link(dve.tensor_reduce(nt[:, 2:4], mask, AX_X, ALU.max))
                    link(dve.tensor_tensor(mask, mask, over(nt[:, 2:4]), ALU.is_equal))

                best(gs, grank, part(c3, 0), N_GROUPS, c1)
                link(dve.tensor_copy(gr.rearrange("p t (g e) -> p t g e", g=N_GROUPS),
                                     part(c3, 0).unsqueeze(3).broadcast_to([P, TILES, N_GROUPS, PER_GROUP])))
                link(dve.tensor_tensor(c1, pe_, gr, ALU.mult))
                link(dve.tensor_scalar(c2, gr, 1.0, None, ALU.subtract))
                link(dve.tensor_tensor(c1, c1, c2, ALU.add))
                best(c1, rank, m1, N_EXPERTS, c3)
                link(dve.tensor_copy(nt[:, 4:6], nt[:, 0:2]))
                link(dve.tensor_scalar(c2, m1, -4.0, None, ALU.mult))
                link(dve.tensor_tensor(c1, c1, c2, ALU.add))
                best(c1, rank, m2, N_EXPERTS, c3)
                link(dve.tensor_tensor(nt[:, 2:4], nt[:, 0:2], nt[:, 4:6], ALU.add))
                link(dve.reciprocal(nt[:, 2:4], nt[:, 2:4]))
                link(dve.tensor_tensor(wts[:, 0, :], nt[:, 4:6], nt[:, 2:4], ALU.mult))
                link(dve.tensor_tensor(wts[:, 1, :], nt[:, 0:2], nt[:, 2:4], ALU.mult))
                dve.tensor_tensor(c1, m1, m2, ALU.add).then_inc(chosen, 1)

                dve.wait_ge(counted, l + 1)
                cn = rt[:, 3:5].rearrange("p i t e -> p (i t e)")

                def part16(i):
                    return cn[:, i * N_EXPERTS:(i + 1) * N_EXPERTS]

                link(dve.tensor_copy(cn, pb[2][:, 0:4 * N_EXPERTS]))
                link(dve.tensor_tensor(part16(1), part16(1), part16(2), ALU.subtract))
                dve.wait_ge(slot_in, l * 16 + 16)
                for t in range(TILES):
                    hot_last = dve.tensor_scalar(hot[:, t, :], slot, part16(t)[:, 0:1], c1[:, t, 0:1],
                                                 ALU.is_equal, ALU.mult)
                hot_last.then_inc(hot_ready, 1)
                dve.wait_ge(hot_ready, l + 1)
                link(dve.tensor_scalar(part16(3), part16(3), -1.0, None, ALU.mult))
                link(dve.memset(part16(2), 1.0))
                link(dve.tensor_tensor_scan(gr[:, 0, :], part16(2), part16(3), 0.0, ALU.mult, ALU.add))
                link(dve.tensor_tensor(gr[:, 0, :], gr[:, 0, :], part16(3), ALU.subtract))
                for t in range(TILES):
                    link(dve.tensor_tensor(part16(t), part16(t), gr[:, 0, :], ALU.add))
                places = cn[:, 0:TILES * N_EXPERTS].rearrange("p (t e) -> p t e", t=TILES)
                for c, m in enumerate((m1, m2)):
                    link(dve.tensor_tensor(m, m, places, ALU.mult))
                    link(dve.tensor_reduce(nt[:, c * TILES:(c + 1) * TILES], m, AX_X, ALU.add))
                link(dve.tensor_copy(place[:, :], nt[:, 0:2 * TILES]))
                link(dve.tensor_copy(counts[:, 0:N_EXPERTS], gr[:, 0, :]))
                link(dve.tensor_copy(counts[:, N_EXPERTS:2 * N_EXPERTS], part16(3)))
                link(dve.tensor_tensor(gr[:, 1, :], gr[:, 0, :], part16(3), ALU.add))
                link(dve.tensor_scalar(gr[:, 1, :], gr[:, 1, :], -float(SLOTS), 0.0, ALU.add, ALU.max))
                link(dve.tensor_copy(counts[:, 2 * N_EXPERTS:3 * N_EXPERTS], gr[:, 1, :]))
                link(dve.tensor_reduce(nt[:, 4:5], part16(3), AX_X, ALU.max))
                link(dve.tensor_copy(counts[:, COUNTS - 2:COUNTS - 1], nt[:, 4:5]))
                link(dve.tensor_scalar(part16(0), part16(3), float(SLOTS), None, ALU.is_gt))
                link(dve.tensor_tensor_scan(part16(1), part16(2), part16(0), overs[:, :], ALU.mult, ALU.add))
                link(dve.tensor_copy(overs[:, :], part16(1)[:, N_EXPERTS - 1:N_EXPERTS]))
                link(dve.tensor_tensor(part16(0), part16(1), part16(0), ALU.subtract))
                link(dve.tensor_copy(counts[:, 3 * N_EXPERTS:4 * N_EXPERTS], part16(0)))
                dve.tensor_copy(counts[:, COUNTS - 1:COUNTS], overs[:, :]).then_inc(routed, 1)

                def front(e, par, u, pair):
                    n = l * N_EXPERTS + e
                    dve.wait_ge(gate_exp, n + 1)
                    dve.tensor_scalar(sg[par], sg[par], 1.0, None, ALU.add).then_inc(moe_link, 1)
                    dve.wait_ge(moe_link, n * 3 + 1)
                    dve.reciprocal(sg[par], sg[par]).then_inc(moe_link, 1)
                    dve.wait_ge(moe_link, n * 3 + 2)
                    dve.tensor_tensor(sg[par], sg[par], pp[2 * par][:, :], ALU.mult).then_inc(moe_link, 1)
                    dve.wait_ge(moe_link, n * 3 + 3)
                    dve.wait_ge(slots_free, l * LAYER_UNITS + pair * PAIR_UNITS + (RING + u + 2 * CHUNK_UNITS))
                    dve.tensor_tensor(sg[par], sg[par], pp[2 * par + 1][:, :], ALU.mult).then_inc(h_ready, 1)

                def back(e, par, u, pair):
                    n = l * N_EXPERTS + e
                    dve.wait_ge(y_out, n * 16 + 16)
                    for c in range(4):
                        dve.wait_ge(slots_free, l * LAYER_UNITS + pair * PAIR_UNITS + (RING + u + c + 1))
                        dve.tensor_copy(yb[par][:, c * NW:(c + 1) * NW], pb[1 + c % 2][:, :]).then_inc(y_copied, 1)

                front(0, 0, FRONT_0, 0)
                dve.wait_ge(sorted_out, (l + 1) * 64)
                dve.wait_ge(xw_filled, l * (4 * N_EXPERTS) + 8)
                link(dve.tensor_scalar(xs[:, :, :], xs[:, :, :], ALPHA, None, ALU.mult), alone=True)
                with dve.Fori(0, PAIRS) as pair:
                    front(pair * 2 + 1, 1, FRONT_ODD, pair)
                    back(pair * 2, 0, BACK_EVEN, pair)
                    front(pair * 2 + 2, 0, FRONT_EVEN, pair)
                    back(pair * 2 + 1, 1, BACK_ODD, pair)
                front(N_EXPERTS - 1, 1, FRONT_ODD + LAST, 0)
                back(N_EXPERTS - 2, 0, BACK_EVEN + LAST, 0)
                back(N_EXPERTS - 1, 1, BACK_LAST, 0)

                most = most_tokens(dve)
                with dve.If(most > SLOTS):
                    with dve.Fori(0, N_EXPERTS) as e:
                        many = tokens(dve, e)
                        with dve.If(many > SLOTS):
                            m = overs_before(dve, e)
                            dve.wait_ge(over_act, m * OVER_ACT + 5)
                            dve.tensor_scalar(sg[0], sg[0], 1.0, None, ALU.add).then_inc(over_link, 1)
                            dve.wait_ge(over_link, m * OVER_LINK + 1)
                            dve.reciprocal(sg[0], sg[0]).then_inc(over_link, 1)
                            dve.wait_ge(over_link, m * OVER_LINK + 2)
                            dve.tensor_tensor(sg[0], sg[0], pp[0][:, :], ALU.mult).then_inc(over_link, 1)
                            dve.wait_ge(over_link, m * OVER_LINK + 3)
                            dve.tensor_tensor(sg[0], sg[0], pp[1][:, :], ALU.mult).then_inc(over_dve, 1)
                            for c in range(4):
                                dve.wait_ge(over_pe, m * OVER_PE + (c + 7))
                                dve.tensor_copy(yb[0][:, c * NW:(c + 1) * NW], pb[1 + c % 2][:, :]).then_inc(over_dve, 1)

                def combine(t, c):
                    dve.wait_ge(back_in[2 * t + c], (l + 1) * 16)
                    link(dve.scalar_tensor_tensor(xs[:, t, :], (xg, yb)[t][c], wts[:, c, t:t + 1], xs[:, t, :],
                                                  ALU.mult, ALU.add))

                def ask_norm(t):
                    for n in range(WO_CHUNKS):
                        last = dve.bn_stats(st[:, t, n, :], xs[:, t, n * NW:(n + 1) * NW])
                    link(last, alone=True)
                    link(dve.bn_aggr(mv[:, t, :], st[:, t, :, :].rearrange("p a b -> p (a b)")))
                    dve.tensor_scalar(var[:, t:t + 1], mv[:, t, 1:2], LN_EPS, None, ALU.add).then_inc(var_ready, 1)

                def take_norm(which, t):
                    take_root(which, t + 1, first=t)
                    dve.tensor_scalar(xs[:, t, :], xs[:, t, :], mv[:, t, 0:1], rstd[:, t:t + 1],
                                      ALU.subtract, ALU.mult).then_inc(normed, 1)

                combine(0, 0)
                combine(0, 1)
                ask_norm(0)
                combine(1, 0)
                take_norm(N_LN2_0, 0)
                combine(1, 1)
                ask_norm(1)
                take_norm(N_LN2_1, 1)
            assert links[0] == DVE_LINKS, links

            dve.wait_ge(lnp_in, DEPTH * 64 + 32)
            dve.wait_ge(normed, DEPTH * 2 * TILES + TILES)
            for t in range(TILES):
                dve.tensor_tensor(xs[:, t, :], xs[:, t, :], ln_g, ALU.mult).then_inc(dve_link, 1)
                dve.wait_ge(dve_link, DEPTH * DVE_LINKS + t + 1)
                dve.tensor_tensor(xs[:, t, :], xs[:, t, :], ln_b, ALU.add).then_inc(scaled, 1)


def constants():
    import numpy as np
    f = np.float32
    tab = np.zeros((P, T_ALL), f)
    p, i = np.arange(P)[:, None], np.arange(P)[None, :]
    tab[:, T_ID:T_ID + P] = p == i
    tab[:, T_SUM:T_SUM + P] = np.where(p >= i, f(-1), f(0))
    tab[:, T_NONE:T_NONE + P] = -1
    tab[:, T_STRICT:T_STRICT + P] = p < i
    tab[:, T_NSTRICT:T_NSTRICT + P] = np.where(p >= i, f(NEG), f(0))
    tab[:, T_CAUSAL:T_CAUSAL + P] = np.where(i > p, f(NEG), f(0))
    for h in range(RET_HEADS):
        log_gamma = np.log1p(-(2.0 ** (-5.0 - h)))
        for at, key, query in ((0, p, np.arange(SEQ)[None, :]), (SEQ, p + P, i + P)):
            d = query - key
            v = np.where(d >= 0, np.exp(np.maximum(d, 0) * log_gamma) * SCALE, 0.0)
            first = T_DECAY + h * TRI + at
            tab[:, first:first + v.shape[1]] = v
    theta = f(10000.0) ** (-np.linspace(0.0, 1.0, HEAD_DIM // 2, dtype=f))
    for t in range(TILES):
        ang = (np.arange(P, dtype=f) + f(t * P))[:, None] * theta[None, :]
        tab[:, T_COS + t * P:T_COS + (t + 1) * P] = np.concatenate([np.cos(ang)] * 2, 1)
        tab[:, T_SIN + t * P:T_SIN + (t + 1) * P] = np.concatenate([-np.sin(ang), np.sin(ang)], 1)
    tab[:, T_RANK:T_RANK + N_EXPERTS] = np.arange(N_EXPERTS, 0, -1)
    tab[:, T_SLOT:T_SLOT + SLOTS] = np.arange(SLOTS)
    return tab


INPUTS = ["x", "w_in", "w_kv_up", "kv_norm_g", "ret_gn_g", "w_o", "ln1_g", "ln1_b", "w_router",
          "w_gate", "w_up", "w_down"]


def norms(inputs):
    import numpy as np
    n = np.full((1, D_MODEL), 0, inputs["ln2_g"].dtype)
    in_g = np.concatenate([np.ones_like(n), inputs["ln2_g"]])
    in_b = np.concatenate([n, inputs["ln2_b"]])
    first = [np.concatenate([inputs[k], n]) for k in ("ln1_g", "ln1_b")]
    cols = np.stack([a.reshape(DEPTH + 1, KT, P).transpose(0, 2, 1) for a in (in_g, in_b, *first)], 2)
    return {"in_g": in_g, "in_b": in_b, "ln_cols": np.ascontiguousarray(cols)}


def kernel(**inputs):
    import numpy as np
    import concourse.bacc as bacc
    from concourse.bass_utils import run_bass_kernel_spmd

    nc = bacc.Bacc("TRN2", target_bir_lowering=False, num_devices=1)
    arrays, args = {}, {}
    laid = {"tables": constants(), **norms(inputs)}
    for name in INPUTS + list(laid):
        a = laid[name] if name in laid else np.ascontiguousarray(inputs[name])
        if name in ("w_gate", "w_up", "w_down"):
            a = a.reshape((DEPTH * N_EXPERTS,) + a.shape[2:])
        if name in ("kv_norm_g", "ret_gn_g"):
            a = np.ascontiguousarray(a.reshape(DEPTH, -1, P).transpose(0, 2, 1))
        arrays[f"in_{name}"] = a
        args[name] = nc.dram_tensor(f"in_{name}", a.shape, F32, kind="ExternalInput").ap()
    args["out"] = nc.dram_tensor("result", (1, SEQ, D_MODEL), F32, kind="ExternalOutput").ap()
    trunk(nc, **args)
    r = run_bass_kernel_spmd(nc, [arrays], core_ids=[0])
    return r.results[0]["result"]
```
